# Optimizing a Trainium2 kernel written in Bass

```python
import jax, jax.numpy as jnp
from jax import lax
import numpy as np

D_MODEL = 2048
BATCH = 1
SEQ = 256
DEPTH = 1

N_META = 16
CHUNK = 128
Q_BLOCK = 128
RET_HEADS = 8
RET_QK_DIM = 128
RET_V_DIM = 128
MLA_HEADS = 8
MLA_NOPE = 128
MLA_ROPE = 64
MLA_V = 128
MLA_Q_RANK = 512
MLA_KV_RANK = 256
D_MIX = RET_HEADS * RET_V_DIM + MLA_HEADS * MLA_V
IN_SIZES = (RET_HEADS * RET_QK_DIM, RET_HEADS * RET_QK_DIM, RET_HEADS * RET_V_DIM,
            RET_HEADS * RET_V_DIM, MLA_Q_RANK, MLA_KV_RANK, MLA_ROPE)
D_IN = sum(IN_SIZES)
D_FF = 5632
ROPE_THETA = 10000.0
EPS = 1e-6

kernel_name = "hymba_retnet_mla_macaron_sandwich"

def rmsnorm(x, w):
    x32 = x.astype(jnp.float32)
    y = x32 * lax.rsqrt(jnp.mean(x32 * x32, axis=-1, keepdims=True) + EPS)
    return (y * w.astype(jnp.float32)).astype(x.dtype)

def swiglu(h, w_gate, w_up, w_down):
    return (jax.nn.silu(h @ w_gate) * (h @ w_up)) @ w_down

def rope_tables(pos, dim):
    inv = ROPE_THETA ** (-jnp.arange(0, dim, 2, dtype=jnp.float32) / dim)
    ang = pos[:, None] * inv[None, :]
    return jnp.cos(ang), jnp.sin(ang)

def apply_rope(x, cos, sin):
    x32 = x.astype(jnp.float32)
    x1, x2 = jnp.split(x32, 2, axis=-1)
    out = jnp.concatenate([x1 * cos - x2 * sin, x2 * cos + x1 * sin], axis=-1)
    return out.astype(x.dtype)

def retention(q, k, v):
    b, seq_len, n_heads, dv = v.shape
    dk = q.shape[-1]
    log_g = jnp.log(1.0 - 2.0 ** (-5.0 - jnp.arange(n_heads, dtype=jnp.float32)))

    def decay_mask(n):
        idx = jnp.arange(n, dtype=jnp.float32)
        diff = idx[:, None] - idx[None, :]
        return jnp.where(diff[None] >= 0,
                         jnp.exp(jnp.maximum(diff, 0.0)[None] * log_g[:, None, None]), 0.0)

    def intra(qc, kc, vc, dmask):
        s = jnp.einsum('bnhd,bmhd->bhnm', qc, kc) * dmask[None]
        return jnp.einsum('bhnm,bmhv->bnhv', s, vc)

    qm, km, vm = q[:, :N_META], k[:, :N_META], v[:, :N_META]
    o_meta = intra(qm, km, vm, decay_mask(N_META))
    pos_m = jnp.arange(N_META, dtype=jnp.float32)
    zeta_m = jnp.exp((N_META - 1 - pos_m)[:, None] * log_g[None, :])
    state0 = jnp.einsum('bmhd,bmhv,mh->bhdv', km, vm, zeta_m)

    n_chunks = (seq_len - N_META) // CHUNK

    def to_chunks(t):
        return t[:, N_META:].reshape(b, n_chunks, CHUNK, n_heads, t.shape[-1]).transpose(1, 0, 2, 3, 4)

    dmask_c = decay_mask(CHUNK)
    pos_c = jnp.arange(CHUNK, dtype=jnp.float32)
    xi = jnp.exp((pos_c + 1.0)[:, None] * log_g[None, :])
    zeta = jnp.exp((CHUNK - 1 - pos_c)[:, None] * log_g[None, :])
    g_chunk = jnp.exp(CHUNK * log_g)

    def step(state, qkv):
        qc, kc, vc = qkv
        o = intra(qc, kc, vc, dmask_c) + \
            jnp.einsum('bnhd,bhdv->bnhv', qc, state) * xi[None, :, :, None]
        state = state * g_chunk[None, :, None, None] + \
            jnp.einsum('bmhd,bmhv,mh->bhdv', kc, vc, zeta)
        return state, o

    _, o_real = lax.scan(step, state0, (to_chunks(q), to_chunks(k), to_chunks(v)))
    o_real = o_real.transpose(1, 0, 2, 3, 4).reshape(b, n_chunks * CHUNK, n_heads, dv)
    return jnp.concatenate([o_meta, o_real], axis=1)

def mla_attention(q_nope, q_rope, k_nope, k_rope, v):
    b, seq_len, n_heads, dv = v.shape
    scale = (MLA_NOPE + MLA_ROPE) ** -0.5
    kpos = jnp.arange(seq_len, dtype=jnp.int32)

    def attend(qn, qr, qpos, kn, kr, vv, kp):
        s = (jnp.einsum('bqhd,bkhd->bhqk', qn, kn) +
             jnp.einsum('bqhr,bkr->bhqk', qr, kr)).astype(jnp.float32) * scale
        s = jnp.where(kp[None, :] <= qpos[:, None], s, -1e30)
        p = jax.nn.softmax(s, axis=-1)
        return jnp.einsum('bhqk,bkhv->bqhv', p.astype(vv.dtype), vv)

    o_meta = attend(q_nope[:, :N_META], q_rope[:, :N_META], kpos[:N_META],
                    k_nope[:, :N_META], k_rope[:, :N_META], v[:, :N_META], kpos[:N_META])

    n_blocks = (seq_len - N_META) // Q_BLOCK

    def blocks(t):
        return t[:, N_META:].reshape(b, n_blocks, Q_BLOCK, *t.shape[2:]).swapaxes(0, 1)

    qpos_blocks = (N_META + jnp.arange(seq_len - N_META, dtype=jnp.int32)).reshape(n_blocks, Q_BLOCK)
    o_real = lax.map(lambda a: attend(a[0], a[1], a[2], k_nope, k_rope, v, kpos),
                     (blocks(q_nope), blocks(q_rope), qpos_blocks))
    o_real = o_real.swapaxes(0, 1).reshape(b, seq_len - N_META, n_heads, dv)
    return jnp.concatenate([o_meta, o_real], axis=1)

def hybrid_mixer(u, w_in, ret_group_norm, mla_q_norm, mla_w_uq, mla_kv_norm,
                 mla_w_uk, mla_w_uv, w_out, cos_r, sin_r, cos_m, sin_m):
    b, seq_len, _ = u.shape
    proj = u @ w_in
    offsets = np.cumsum(IN_SIZES)[:-1].tolist()
    rq, rk, rv, rg, cq, ckv, kr = jnp.split(proj, offsets, axis=-1)

    rq = apply_rope(rq.reshape(b, seq_len, RET_HEADS, RET_QK_DIM), cos_r[:, None], sin_r[:, None])
    rk = apply_rope(rk.reshape(b, seq_len, RET_HEADS, RET_QK_DIM), cos_r[:, None], sin_r[:, None])
    rv = rv.reshape(b, seq_len, RET_HEADS, RET_V_DIM)
    ret = retention(rq.astype(jnp.float32),
                    rk.astype(jnp.float32) * (RET_QK_DIM ** -0.5),
                    rv.astype(jnp.float32))
    ret = ret * lax.rsqrt(jnp.mean(ret * ret, axis=-1, keepdims=True) + EPS)
    ret = ret.reshape(b, seq_len, RET_HEADS * RET_V_DIM) * ret_group_norm.astype(jnp.float32)
    ret = (jax.nn.silu(rg.astype(jnp.float32)) * ret).astype(u.dtype)

    cq = rmsnorm(cq, mla_q_norm)
    q = (cq @ mla_w_uq).reshape(b, seq_len, MLA_HEADS, MLA_NOPE + MLA_ROPE)
    q_nope, q_rope = q[..., :MLA_NOPE], q[..., MLA_NOPE:]
    q_rope = apply_rope(q_rope, cos_m[:, None], sin_m[:, None])
    ckv = rmsnorm(ckv, mla_kv_norm)
    k_nope = (ckv @ mla_w_uk).reshape(b, seq_len, MLA_HEADS, MLA_NOPE)
    v = (ckv @ mla_w_uv).reshape(b, seq_len, MLA_HEADS, MLA_V)
    k_rope = apply_rope(kr, cos_m, sin_m)
    mla = mla_attention(q_nope, q_rope, k_nope, k_rope, v).reshape(b, seq_len, MLA_HEADS * MLA_V)

    return jnp.concatenate([ret, mla.astype(u.dtype)], axis=-1) @ w_out

def _normal(k, shape, fan_in):
    return jax.random.normal(k, shape, jnp.float32) * (fan_in ** -0.5)

def _gain(k, shape):
    return 1.0 + 0.02 * jax.random.normal(k, shape, jnp.float32)

def setup_inputs(seed: int = 0) -> dict:
    key = jax.random.key(seed)
    ks = jax.random.split(key, 24)
    L = DEPTH
    return {
        "x": jax.random.normal(ks[0], (BATCH, SEQ, D_MODEL), jnp.float32),
        "meta_tokens": jax.random.normal(ks[1], (N_META, D_MODEL), jnp.float32),
        "ffn1_pre_norm": _gain(ks[2], (L, D_MODEL)),
        "ffn1_w_gate": _normal(ks[3], (L, D_MODEL, D_FF), D_MODEL),
        "ffn1_w_up": _normal(ks[4], (L, D_MODEL, D_FF), D_MODEL),
        "ffn1_w_down": _normal(ks[5], (L, D_FF, D_MODEL), D_FF),
        "ffn1_post_norm": _gain(ks[6], (L, D_MODEL)),
        "mix_pre_norm": _gain(ks[7], (L, D_MODEL)),
        "w_in": _normal(ks[8], (L, D_MODEL, D_IN), D_MODEL),
        "ret_group_norm": _gain(ks[9], (L, RET_HEADS * RET_V_DIM)),
        "mla_q_norm": _gain(ks[10], (L, MLA_Q_RANK)),
        "mla_w_uq": _normal(ks[11], (L, MLA_Q_RANK, MLA_HEADS * (MLA_NOPE + MLA_ROPE)), MLA_Q_RANK),
        "mla_kv_norm": _gain(ks[12], (L, MLA_KV_RANK)),
        "mla_w_uk": _normal(ks[13], (L, MLA_KV_RANK, MLA_HEADS * MLA_NOPE), MLA_KV_RANK),
        "mla_w_uv": _normal(ks[14], (L, MLA_KV_RANK, MLA_HEADS * MLA_V), MLA_KV_RANK),
        "w_out": _normal(ks[15], (L, D_MIX, D_MODEL), D_MIX),
        "mix_post_norm": _gain(ks[16], (L, D_MODEL)),
        "ffn2_pre_norm": _gain(ks[17], (L, D_MODEL)),
        "ffn2_w_gate": _normal(ks[18], (L, D_MODEL, D_FF), D_MODEL),
        "ffn2_w_up": _normal(ks[19], (L, D_MODEL, D_FF), D_MODEL),
        "ffn2_w_down": _normal(ks[20], (L, D_FF, D_MODEL), D_FF),
        "ffn2_post_norm": _gain(ks[21], (L, D_MODEL)),
    }

def reference(x, meta_tokens, ffn1_pre_norm, ffn1_w_gate, ffn1_w_up, ffn1_w_down,
              ffn1_post_norm, mix_pre_norm, w_in, ret_group_norm, mla_q_norm, mla_w_uq,
              mla_kv_norm, mla_w_uk, mla_w_uv, w_out, mix_post_norm, ffn2_pre_norm,
              ffn2_w_gate, ffn2_w_up, ffn2_w_down, ffn2_post_norm):
    b = x.shape[0]
    meta = jnp.broadcast_to(meta_tokens.astype(x.dtype)[None], (b, N_META, x.shape[-1]))
    h = jnp.concatenate([meta, x], axis=1)
    seq_len = h.shape[1]
    pos = jnp.arange(seq_len, dtype=jnp.float32)
    cos_r, sin_r = rope_tables(pos, RET_QK_DIM)
    cos_m, sin_m = rope_tables(pos, MLA_ROPE)
    for l in range(DEPTH):
        f = swiglu(rmsnorm(h, ffn1_pre_norm[l]), ffn1_w_gate[l], ffn1_w_up[l], ffn1_w_down[l])
        h = h + 0.5 * rmsnorm(f, ffn1_post_norm[l])
        m = hybrid_mixer(rmsnorm(h, mix_pre_norm[l]), w_in[l], ret_group_norm[l], mla_q_norm[l],
                         mla_w_uq[l], mla_kv_norm[l], mla_w_uk[l], mla_w_uv[l], w_out[l],
                         cos_r, sin_r, cos_m, sin_m)
        h = h + rmsnorm(m, mix_post_norm[l])
        f = swiglu(rmsnorm(h, ffn2_pre_norm[l]), ffn2_w_gate[l], ffn2_w_up[l], ffn2_w_down[l])
        h = h + 0.5 * rmsnorm(f, ffn2_post_norm[l])
    return h[:, N_META:]


_drawn_inputs = setup_inputs


def setup_inputs(seed=0):
    import zlib

    import numpy as np

    out = dict(_drawn_inputs(seed))
    spreads = {}
    factors = {'ffn1_pre_norm': 2.695,
     'ffn1_post_norm': 3.858,
     'ret_group_norm': 33.688,
     'mla_q_norm': 8.0,
     'mla_kv_norm': 8.0,
     'mix_post_norm': 11.242,
     'ffn2_pre_norm': 18.984,
     'ffn2_post_norm': 33.92}
    for name, (base, spread) in spreads.items():
        noise = np.random.default_rng([zlib.crc32(name.encode()), seed]).standard_normal(out[name].shape)
        drawn = base * np.exp(spread * noise) if base else spread * noise
        out[name] = __import__('jax').numpy.asarray(drawn.astype(out[name].dtype))
    for name, factor in factors.items():
        out[name] = (out[name] * factor).astype(out[name].dtype)
    return out
```

```python
from contextlib import ExitStack

import numpy as np

import concourse.bass as bass
from concourse import mybir

ACT = mybir.ActivationFunctionType
ALU = mybir.AluOpType
AX = mybir.AxisListType
F32 = mybir.dt.float32
F32R = mybir.dt.float32r

P = 128
DM, FF = 2048, 5632
REAL, META = 256, 16
TOK = REAL + META
KC = DM // P
HEADS, DH, ROPE = 8, 128, 64
Q_RANK, KV_RANK = 512, 256
QC, CC = Q_RANK // P, KV_RANK // P
EPS = 1e-6
MLA_SCALE = float(DH + ROPE) ** -0.5
PAIRS = HEADS // 2

UNIT = 2048
SLOTS = 3
SEG = 512
SEGS = FF // SEG
FFN_UNITS = 12 * SEGS
PRE_UNITS = 7
PAIR_UNITS = 11
OUT_UNITS = 4
U_FFN = (0, FFN_UNITS + PRE_UNITS + PAIRS * (PAIR_UNITS + OUT_UNITS))
U_PRE = FFN_UNITS
U_MIX = U_PRE + PRE_UNITS
U_ALL = U_FFN[1] + FFN_UNITS
C_RQ, C_RK, C_RV, C_RG = 0, 1024, 2048, 3072
C_CQ, C_CKV, C_KR = 4096, 4608, 4864
A_FFN = (0, 4 + 4 * SEGS + 4 + 4 * PAIRS)
A_MIX = 4 + 4 * SEGS
G_PRE, G_POST = (0, 2 * KC, 4 * KC), (KC, 3 * KC, 5 * KC)
G_RET = 6 * KC
G_Q, G_KV = G_RET + HEADS, G_RET + HEADS + QC
GAINS = G_KV + CC


def pair_unit(p, j):
    if isinstance(p, int):
        return U_MIX + (j if p == 0 else PAIR_UNITS + 15 * (p - 1) + j)
    raise TypeError("give loops their own base")


def constants():
    pos = np.concatenate([META + np.arange(REAL), np.arange(META)]).astype(np.float32)

    def rope(dim):
        inv = np.float32(10000.0) ** (-np.arange(0, dim, 2, dtype=np.float32) / np.float32(dim))
        ang = (pos[:, None] * inv[None, :]).astype(np.float32)
        c, s = np.cos(ang).T, np.sin(ang).T
        reps = P // dim
        return np.stack([np.concatenate([c, c] * reps), np.concatenate([-s, s] * reps)])

    tri = np.where(np.arange(P)[None, :] <= np.arange(P)[:, None], 0.0, -1e30)
    mask = np.zeros((2, P, TOK))
    mask[0, :, 0:P], mask[0, :, P:REAL] = tri, -1e30
    mask[1, :, P:REAL] = tri
    log_g = np.log(1.0 - 2.0 ** (-5.0 - np.arange(HEADS)))
    m, n = np.arange(P), np.arange(REAL)
    diff = (n[None, :] - m[:, None])[None]
    d = np.where(diff >= 0, np.exp(np.maximum(diff, 0) * log_g[:, None, None]), 0.0) * DH ** -0.5
    d = np.concatenate([d, d[:, :, 0:P]], axis=2)
    dm = np.exp((META + n[None, :] - np.arange(META)[:, None])[None] * log_g[:, None, None]) * DH ** -0.5
    f = lambda a: np.ascontiguousarray(a, dtype=np.float32)
    return {
        "rope_ret": f(rope(DH)), "rope_mla": f(rope(ROPE)), "mask": f(mask),
        "decay": f(d.reshape(PAIRS, 2, P, 3 * P).transpose(0, 2, 1, 3)),
        "decay_meta": f(dm.reshape(PAIRS, 2, META, REAL).transpose(0, 2, 1, 3)),
        "ident": f(np.eye(P)),
    }


def build(nc, a, out):
    ctx = ExitStack()
    with ctx:
        def sb(name, shape, dt=F32):
            return ctx.enter_context(nc.sbuf_tensor(name, shape, dt))

        def sem(name):
            return ctx.enter_context(nc.semaphore(name))

        raw = sb("raw", [P, SLOTS, UNIT])
        w_hi = sb("w_hi", [P, SLOTS, UNIT], F32R)
        w_lo = sb("w_lo", [P, SLOTS, UNIT], F32R)
        hT = sb("hT", [P, KC * TOK])
        hn_hi = sb("hn_hi", [P, KC, TOK], F32R)
        hn_lo = sb("hn_lo", [P, KC, TOK], F32R)
        acc = sb("acc", [P, KC * TOK])
        dn_hi = sb("dn_hi", [P, 4, TOK], F32R)
        dn_lo = sb("dn_lo", [P, 4, TOK], F32R)
        tmp = sb("tmp", [P, 4, TOK])
        gains = sb("gains", [P, GAINS])
        ident = sb("ident_sb", [P, P])
        ones = sb("ones", [P, P])
        rope_ret = sb("rope_ret_sb", [P, 2, TOK])
        rope_mla = sb("rope_mla_sb", [P, 2, TOK])
        mask = sb("mask_sb", [P, 2, TOK])
        sq = sb("sq", [P, TOK])
        ssq = sb("ssq", [P, TOK])
        rstd = sb("rstd", [P, TOK])
        small = sb("small", [P, 16])
        eps = small[:, 0:1]
        ckv_hi = sb("ckv_hi", [P, CC, 3 * P], F32R)
        ckv_lo = sb("ckv_lo", [P, CC, 3 * P], F32R)
        cq_hi = sb("cq_hi", [P, QC, REAL], F32R)
        cq_lo = sb("cq_lo", [P, QC, REAL], F32R)

        h = hT[:, :].rearrange("p (c n) -> p c n", c=KC)
        acc_t = acc[:, :].rearrange("p (c n) -> p c n", c=KC)
        sil, act = tmp[:, 0:2, :], tmp[:, 2:4, :]
        swap, prod, probs = tmp[:, 0, :], tmp[:, 1, :], tmp[:, 2:4, :]

        at = [0]

        def carve(t, size, n):
            v = t[:, at[0]:at[0] + size]
            at[0] += size
            return v.rearrange("p (a n) -> p a n", n=n)

        ret_k = carve(hT, 2 * TOK, TOK)
        ret_q = carve(hT, 2 * REAL, REAL)
        ret_vT = carve(hT, 2 * TOK, TOK)
        ret_v = carve(hT, 2 * 3 * P, 3 * P)
        ret_gate = carve(hT, 2 * REAL, REAL)
        mla_q = carve(hT, 2 * REAL, REAL)
        mla_qr = carve(hT, REAL, REAL)[:, 0, :]
        mla_k = carve(hT, 2 * TOK, TOK)
        assert at[0] <= KC * TOK
        MIX = TOK + 3 * REAL + 2 * 640 + 2 * 3 * P + 2 * REAL + 2 * TOK + QC * REAL
        mix = sb("mix", [P, MIX])
        at[0] = 0
        mla_kr = carve(mix, TOK, TOK)[:, 0, :]
        mla_v = carve(mix, 3 * REAL, REAL)
        sc = carve(mix, 2 * 640, 640)
        decay = carve(mix, 2 * 3 * P, 3 * P)
        decay_meta = carve(mix, 2 * REAL, REAL)
        keep = carve(mix, 2 * TOK + QC * REAL, 2 * TOK + QC * REAL)[:, 0, :]
        lat_sq = mix[:, TOK + 3 * REAL:TOK + 3 * REAL + 4 * TOK].rearrange("p (a n) -> p a n", n=TOK)
        ckv_f = keep[:, 0:2 * TOK].rearrange("p (a n) -> p a n", n=TOK)
        cq_f = keep[:, 2 * TOK:].rearrange("p (a n) -> p a n", n=REAL)
        ret_o = keep[:, 0:2 * REAL].rearrange("p (a n) -> p a n", n=REAL)
        ret_sq = keep[:, 2 * REAL:4 * REAL].rearrange("p (a n) -> p a n", n=REAL)
        ret_rs = keep[:, 4 * REAL:6 * REAL].rearrange("p (a n) -> p a n", n=REAL)
        x_sb = acc[:, 0:2 * DM].rearrange("p (t d) -> p t d", t=2)
        meta_sb = mix[0:META, 0:DM]
        gain_rows = mix[0:GAINS, DM:DM + P]

        bank = [ctx.enter_context(nc.psum_tensor(f"bank{i}", [P, 512], F32)) for i in range(8)]
        spill = nc.dram_tensor("h_spill", (P, KC * TOK), F32).ap()

        consts_in = sem("consts_in")
        x_in = sem("x_in")
        raw_full = [sem(f"raw_full{i}") for i in range(SLOTS)]
        hi_ready = sem("hi_ready")
        lo_ready = sem("lo_ready")
        unit_used = sem("unit_used")
        ones_set = sem("ones_set")
        gains_tr = sem("gains_tr")
        gains_ready = sem("gains_ready")
        x_tr = sem("x_tr")
        h_ready = sem("h_ready")
        pool_step = sem("pool_step")
        ssq_ready = sem("ssq_ready")
        ms_done = sem("ms_done")
        std_done = sem("std_done")
        rstd_done = sem("rstd_done")
        dve_step = sem("dve_step")
        normed = sem("normed")
        hn_hi_done = sem("hn_hi_done")
        hn_ready = sem("hn_ready")
        silu_done = sem("silu_done")
        act_done = sem("act_done")
        act_hi_done = sem("act_hi_done")
        act_ready = sem("act_ready")
        acc_ready = sem("acc_ready")
        swapped = sem("swapped")
        rotated = sem("rotated")
        vT_ready = sem("vT_ready")
        gate_ready = sem("gate_ready")
        v_tr = sem("v_tr")
        v_ready = sem("v_ready")
        mq_ready = sem("mq_ready")
        mk_ready = sem("mk_ready")
        mv_ready = sem("mv_ready")
        ret_scores = sem("ret_scores")
        ret_masked = sem("ret_masked")
        ret_out = sem("ret_out")
        ret_sq_done = sem("ret_sq_done")
        ret_ms = sem("ret_ms")
        ret_std = sem("ret_std")
        ret_f = sem("ret_f")
        mix_hi_done = sem("mix_hi_done")
        mix_ready = sem("mix_ready")
        mla_scores = sem("mla_scores")
        neg_max = sem("neg_max")
        exp_done = sem("exp_done")
        probs_ready = sem("probs_ready")
        probs_tr = sem("probs_tr")
        probsT_ready = sem("probsT_ready")
        mla_out = sem("mla_out")
        lat_read = sem("lat_read")
        lat_ms = sem("lat_ms")
        lat_std = sem("lat_std")
        lat_normed = sem("lat_normed")
        lat_hi_done = sem("lat_hi_done")
        lat_ready = sem("lat_ready")
        pad_zero = sem("pad_zero")
        decay_in = sem("decay_in")
        spilled = sem("spilled")
        reloaded = sem("reloaded")
        out_tr = sem("out_tr")
        out_ready = sem("out_ready")
        stored = sem("stored")

        def slot(ring, u0, **shape):
            v = ring[:, u0 % SLOTS, :]
            n = UNIT
            if "n" in shape:
                n = shape["n"]
                v = v[:, 0:n]
            k = shape["k"]
            return v.rearrange("p (k n) -> p k n", k=k)

        def split_parts(u0, kind):
            if kind == "kr":
                src = slot(raw, u0, k=KC, n=KC * ROPE)
                hi, lo = (slot(r, u0, k=KC).rearrange("p k (r n) -> p k r n", r=2) for r in (w_hi, w_lo))
                return [(src, hi[:, :, r, :], lo[:, :, r, :]) for r in range(2)]
            if kind == "uq":
                src = slot(raw, u0, k=QC, n=QC * 384).rearrange("p k (h n) -> p k h n", h=2)
                hi, lo = (slot(r, u0, k=QC, n=QC * 384) for r in (w_hi, w_lo))
                cut = [(slice(0, DH), slice(0, 2 * DH)), (slice(DH, DH + ROPE), slice(2 * DH, 384))]
                return [(src[:, :, :, a_], *(x[:, :, b_].rearrange("p k (h n) -> p k h n", h=2) for x in (hi, lo)))
                        for a_, b_ in cut]
            n = CC * 256 if kind == "ukv" else UNIT
            return [tuple(x[:, u0 % SLOTS, 0:n] for x in (raw, w_hi, w_lo))]

        def pair_kind(j):
            return {8: "uq", 9: "ukv", 10: "ukv"}.get(j, "full")

        kt = {name: a[name].rearrange("(k p) n -> p k n", p=P) for name in
              ("ffn1_w_gate", "ffn1_w_up", "ffn1_w_down", "ffn2_w_gate", "ffn2_w_up",
               "ffn2_w_down", "w_in", "mla_w_uq", "mla_w_uk", "mla_w_uv", "w_out")}
        FILL = 32

        block = ctx.enter_context(nc.Block())

        @block.sync
        def _(sp):
            def load(u, u0, halves):
                if not (isinstance(u, int) and u < SLOTS):
                    sp.wait_ge(lo_ready, u - SLOTS + 1)
                for d, s in halves:
                    sp.dma_start(d, s).then_inc(raw_full[u0 % SLOTS], 16)

            def gate_up(u, u0, w, col, kh):
                v = slot(raw, u0, k=8)
                load(u, u0, [(v[:, 4 * i:4 * i + 4, :],
                              kt[w][:, 8 * kh + 4 * i:8 * kh + 4 * i + 4, bass.ds(col, 256)])
                             for i in range(2)])

            def down(u, u0, w, k0, k1, q):
                v = slot(raw, u0, k=4)
                load(u, u0, [(v[:, 2 * i:2 * i + 2, :], kt[w][:, bass.ds(k, 2), q * 512:q * 512 + 512])
                             for i, k in enumerate((k0, k1))])

            def ffn_loads(f):
                g, up, dn = (f"ffn{f + 1}_w_{x}" for x in ("gate", "up", "down"))
                U = U_FFN[f]

                def half(u, u0, col):
                    for j, (w, kh) in enumerate(((g, 0), (g, 1), (up, 0), (up, 1))):
                        gate_up(u + j, u0 + j, w, col, kh)

                half(U, U, 0)
                half(U + 4, U + 4, 256)
                with sp.Fori(0, SEGS - 1) as i:
                    u0 = U + 8
                    u = sp.snap(i * 12 + u0)
                    col0 = sp.snap(i * SEG + SEG)
                    col1 = sp.snap(i * SEG + SEG + 256)
                    k0 = sp.snap(i * 4)
                    k1 = sp.snap(i * 4 + 2)
                    half(u, u0, col0)
                    for q in range(4):
                        down(u + 4 + q, u0 + 4 + q, dn, k0, k1, q)
                    half(u + 8, u0 + 8, col1)
                for q in range(4):
                    u = U + FFN_UNITS - 4 + q
                    down(u, u, dn, 4 * SEGS - 4, 4 * SEGS - 2, q)

            def pair_loads(u, u0, c256, c384, p2):
                for b, c in enumerate((C_RK, C_RQ, C_RV, C_RG)):
                    for kh in range(2):
                        gate_up(u + 2 * b + kh, u0 + 2 * b + kh, "w_in", c256[c], kh)
                v = slot(raw, u0 + 8, k=QC, n=QC * 384)
                load(u + 8, u0 + 8, [(v[:, 2 * i:2 * i + 2, :],
                                      kt["mla_w_uq"][:, 2 * i:2 * i + 2, bass.ds(c384, 384)])
                                     for i in range(2)])
                for j, w in enumerate(("mla_w_uk", "mla_w_uv")):
                    v = slot(raw, u0 + 9 + j, k=CC, n=CC * 256)
                    load(u + 9 + j, u0 + 9 + j, [(v[:, i:i + 1, :],
                                                  kt[w][:, i:i + 1, bass.ds(c256[0], 256)])
                                                 for i in range(2)])
                if not isinstance(p2, int):
                    sp.wait_ge(ret_masked, p2)

            sp.dma_start(x_sb, a["x"].rearrange("(t p) d -> p t d", p=P)).then_inc(x_in, 16)
            sp.dma_start(meta_sb, a["meta_tokens"]).then_inc(x_in, 16)
            for name, at0, n in (("ffn1_pre_norm", G_PRE[0], KC), ("ffn1_post_norm", G_POST[0], KC),
                                 ("mix_pre_norm", G_PRE[1], KC), ("mix_post_norm", G_POST[1], KC),
                                 ("ffn2_pre_norm", G_PRE[2], KC), ("ffn2_post_norm", G_POST[2], KC),
                                 ("ret_group_norm", G_RET, HEADS), ("mla_q_norm", G_Q, QC),
                                 ("mla_kv_norm", G_KV, CC)):
                sp.dma_start(gain_rows[at0:at0 + n, :],
                             a[name].rearrange("o (c p) -> (o c) p", p=P)).then_inc(consts_in, 16)
            sp.dma_start(ident[:, :], a["ident"]).then_inc(consts_in, 16)
            sp.dma_start(rope_ret[:, :, :], a["rope_ret"].rearrange("t p n -> p t n")).then_inc(consts_in, 16)
            sp.dma_start(rope_mla[:, :, :], a["rope_mla"].rearrange("t p n -> p t n")).then_inc(consts_in, 16)
            sp.dma_start(mask[:, :, :], a["mask"].rearrange("t p n -> p t n")).then_inc(consts_in, 16)

            ffn_loads(0)
            for kh in range(2):
                gate_up(U_PRE + kh, U_PRE + kh, "w_in", C_CKV, kh)
            u = U_PRE + 2
            v = slot(raw, u, k=KC, n=KC * ROPE)
            load(u, u, [(v[:, 8 * i:8 * i + 8, :], kt["w_in"][:, 8 * i:8 * i + 8, C_KR:C_KR + ROPE])
                        for i in range(2)])
            for b in range(2):
                for kh in range(2):
                    u = U_PRE + 3 + 2 * b + kh
                    gate_up(u, u, "w_in", C_CQ + 256 * b, kh)
            sp.wait_ge(h_ready, 2 * KC)
            sp.wait_ge(normed, 2 * KC)
            sp.dma_start(spill, hT[:, :]).then_inc(spilled, 16)

            def decay_load(src_p):
                sp.dma_start(decay, a["decay"][src_p]).then_inc(decay_in, 16)
                sp.dma_start(decay_meta[0:META], a["decay_meta"][src_p]).then_inc(decay_in, 16)

            cols = {c: c for c in (0, C_RK, C_RV, C_RG)}
            pair_loads(U_MIX, U_MIX, cols, 0, 0)
            sp.wait_ge(lat_normed, 2)
            decay_load(0)
            with sp.Fori(0, PAIRS - 1) as i:
                u0 = U_MIX + PAIR_UNITS
                u = sp.snap(i * 15 + u0)
                cols = {c: sp.snap(i * 256 + (256 + c)) for c in (0, C_RK, C_RV, C_RG)}
                c384 = sp.snap(i * 384 + 384)
                p2 = sp.snap(i * 2 + 2)
                k0 = sp.snap(i * 2)
                k1 = sp.snap(i * 2 + HEADS)
                d0 = sp.snap(i * (P * 6 * P) + P * 6 * P)
                dm0 = sp.snap(i * (META * 2 * REAL) + META * 2 * REAL)
                pair_loads(u, u0, cols, c384, p2)
                dsrc = a["decay"].rearrange("a p h n -> (a p h n)")[bass.ds(d0, P * 6 * P)]
                sp.dma_start(decay, dsrc.rearrange("(p h n) -> p h n", p=P, h=2)).then_inc(decay_in, 16)
                msrc = a["decay_meta"].rearrange("a p h n -> (a p h n)")[bass.ds(dm0, META * 2 * REAL)]
                sp.dma_start(decay_meta[0:META], msrc.rearrange("(p h n) -> p h n", p=META, h=2)).then_inc(decay_in, 16)
                for q in range(4):
                    down(u + 11 + q, u0 + 11 + q, "w_out", k0, k1, q)
            for q in range(4):
                u = U_FFN[1] - 4 + q
                down(u, u, "w_out", HEADS - 2, 2 * HEADS - 2, q)
            sp.wait_ge(spilled, 16)
            sp.wait_ge(mix_ready, 4 * PAIRS)
            sp.dma_start(hT[:, :], spill).then_inc(reloaded, 16)
            ffn_loads(1)
            for t in range(2):
                sp.wait_ge(out_ready, 4 * t + 4)
                sp.dma_start(out[t * P:(t + 1) * P, :], raw[:, t, :]).then_inc(stored, 16)
            sp.wait_ge(stored, 32)

        @block.gpsimd
        def _(pool):
            steps = [0]
            nc.gpsimd.memset(ones[:, :], 1.0).then_inc(ones_set, 1)
            nc.gpsimd.memset(eps, EPS).then_inc(ones_set, 1)
            nc.gpsimd.memset(ckv_hi[:, :, TOK:].bitcast(F32), 0.0).then_inc(pad_zero, 1)
            nc.gpsimd.memset(ckv_lo[:, :, TOK:].bitcast(F32), 0.0).then_inc(pad_zero, 1)

            def sum_squares(norm, src, n, ready, base, per):
                if norm:
                    pool.wait_ge(ms_done, norm)
                for c in range(KC):
                    pool.wait_ge(ready, base + per(c))
                    if c == 0:
                        nc.gpsimd.tensor_tensor(ssq[:, 0:n], src[:, c, 0:n], src[:, c, 0:n], ALU.mult).then_inc(pool_step, 1)
                        steps[0] += 1
                        continue
                    pool.wait_ge(pool_step, steps[0])
                    nc.gpsimd.tensor_tensor(sq[:, 0:n], src[:, c, 0:n], src[:, c, 0:n], ALU.mult).then_inc(pool_step, 1)
                    steps[0] += 1
                    pool.wait_ge(pool_step, steps[0])
                    add = nc.gpsimd.tensor_tensor(ssq[:, 0:n], ssq[:, 0:n], sq[:, 0:n], ALU.add)
                    if c < KC - 1:
                        add.then_inc(pool_step, 1)
                        steps[0] += 1
                    else:
                        add.then_inc(ssq_ready, 1)

            one = lambda c: c + 1
            group = lambda c: c // 4 + 1
            sum_squares(0, h, TOK, h_ready, 0, one)
            sum_squares(1, acc_t, TOK, acc_ready, A_MIX - 4, group)
            sum_squares(2, h, TOK, h_ready, KC, one)
            sum_squares(3, acc_t, REAL, acc_ready, A_FFN[1] - 4, group)
            sum_squares(4, h, REAL, h_ready, 2 * KC, one)
            sum_squares(5, acc_t, REAL, acc_ready, A_FFN[1] + 4 * SEGS, group)

        @block.scalar
        def _(act_e):
            def copy(o, i):
                return nc.scalar.activation(o, i, ACT.Copy)

            def split(u, u0, kind="full", filled=0):
                act_e.wait_ge(raw_full[u0 % SLOTS], filled + FILL * (u0 // SLOTS + 1))
                if not (isinstance(u, int) and u < SLOTS):
                    act_e.wait_ge(unit_used, u - SLOTS + 1)
                for src, hi, _ in split_parts(u0, kind):
                    last = copy(hi, src)
                last.then_inc(hi_ready, 1)

            def std(norm, n):
                act_e.wait_ge(ms_done, norm + 1)
                nc.scalar.activation(rstd[:, 0:n], bank[7][:, 0:n], ACT.Sqrt, bias=eps, scale=1.0 / DM).then_inc(std_done, 1)

            def split_normed(stage, n):
                for c in range(KC):
                    act_e.wait_ge(normed, stage * KC + c + 1)
                    copy(hn_hi[:, c, 0:n], acc_t[:, c, 0:n]).then_inc(hn_hi_done, 1)

            def ffn(f, n, tail):
                U = U_FFN[f]

                def silu(u, ch, first_bank):
                    act_e.wait_ge(unit_used, u + 1)
                    for c in range(2):
                        if not (isinstance(ch, int) and ch + c < 2):
                            act_e.wait_ge(act_done, ch + c - 1)
                        nc.scalar.activation(sil[:, c, 0:n], bank[first_bank + c][:, 0:n], ACT.Silu).then_inc(silu_done, 1)

                def act_hi(ch, half):
                    for c in range(2):
                        act_e.wait_ge(act_done, ch + c + 1)
                        copy(dn_hi[:, 2 * half + c, 0:n], act[:, c, 0:n]).then_inc(act_hi_done, 1)

                ch = 44 * f
                for j in range(8):
                    split(U + j + 2, U + j + 2)
                    if j in (1, 5):
                        silu(U + j, ch + (j > 4) * 2, 4 * (j > 4))
                    if j in (3, 7):
                        act_hi(ch + (j > 4) * 2, int(j > 4))
                with act_e.Fori(0, SEGS - 1) as i:
                    u0 = U + 8
                    u = act_e.snap(i * 12 + u0)
                    c0 = act_e.snap(i * 4 + (ch + 4))
                    filled = act_e.snap(i * (12 // SLOTS * FILL))
                    for j in range(12):
                        split(u + (j + 2), u0 + j + 2, filled=filled)
                        if j == 1:
                            silu(u + 1, c0, 0)
                        if j == 7:
                            act_e.wait_ge(unit_used, u + 8)
                            act_hi(c0, 0)
                        if j == 9:
                            silu(u + 9, c0 + 2, 4)
                        if j == 11:
                            act_hi(c0 + 2, 1)
                for q in range(4):
                    tail(U + FFN_UNITS - 4 + q)

            def swap_halves(index, src, n, width):
                if index > 0:
                    act_e.wait_ge(rotated, index)
                last = None
                for b in range(P // width):
                    o = b ^ 1
                    last = copy(swap[b * width:(b + 1) * width, 0:n], src[o * width:(o + 1) * width, 0:n])
                last.then_inc(swapped, 1)

            def pair_projections(j, u, r0, h0, first):
                if j in (1, 3, 5, 7, 8, 9):
                    act_e.wait_ge(unit_used, u + j + 1)
                if j == 1:
                    for c in range(2):
                        swap_halves(r0 + c, bank[c], TOK, 64)
                if j == 3:
                    for c in range(2):
                        swap_halves(r0 + 2 + c, bank[2 + c], REAL, 64)
                if j == 5:
                    for c in range(2):
                        copy(ret_vT[:, c, :], bank[c][:, 0:TOK]).then_inc(vT_ready, 1)
                if j == 7:
                    for c in range(2):
                        nc.scalar.activation(ret_gate[:, c, :], bank[2 + c][:, 0:REAL], ACT.Silu).then_inc(gate_ready, 1)
                if j == 8:
                    for c in range(2):
                        copy(mla_q[:, c, :], bank[c][:, 0:REAL]).then_inc(mq_ready, 1)
                    swap_halves(r0 + 4, bank[2], REAL, 32)
                if j == 9:
                    for c in range(2):
                        copy(mla_k[:, c, :], bank[(3, 0)[c]][:, 0:TOK]).then_inc(mk_ready, 1)
                    for c in range(2):
                        act_e.wait_ge(v_tr, h0 + c + 1)
                        b = bank[(5, 7)[c]]
                        copy(ret_v[:, c, 0:REAL], b[:, 0:REAL])
                        copy(ret_v[0:META, c, REAL:], b[0:META, REAL:3 * P]).then_inc(v_ready, 1)

            def attention(j, h0, m0):
                if j == 1:
                    for c in range(2):
                        act_e.wait_ge(ret_out, h0 + c + 1)
                        copy(ret_o[:, c, :], bank[4 + 2 * c][:, 0:REAL])
                        nc.scalar.activation(ret_sq[:, c, :], bank[4 + 2 * c][:, 0:REAL], ACT.Square).then_inc(ret_sq_done, 1)
                if j == 2:
                    exps(h0)
                    for c in range(2):
                        act_e.wait_ge(ret_ms, h0 + c + 1)
                        nc.scalar.activation(ret_rs[:, c, :], bank[4 + 2 * c][:, 0:REAL], ACT.Sqrt, bias=eps, scale=1.0 / DH).then_inc(ret_std, 1)
                if j == 3:
                    mix_hi_ret(h0, m0, 0)
                if j == 4:
                    probs_copy(h0)
                    mix_hi_ret(h0, m0, 1)
                if j == 5:
                    mix_hi_mla(h0, 0)
                    exps(h0 + 1)
                if j == 7:
                    probs_copy(h0 + 1)
                if j == 8:
                    mix_hi_mla(h0 + 1, 1)

            def exps(hd):
                for t in range(2):
                    act_e.wait_ge(neg_max, hd * 2 + (t + 1))
                    nc.scalar.activation(probs[:, t, :], probs[:, t, :], ACT.Exp, bias=small[:, 4 + t:5 + t],
                                         accum_out=small[:, 6 + t:7 + t]).then_inc(exp_done, 1)

            def probs_copy(hd):
                act_e.wait_ge(probs_tr, hd + 1)
                copy(sc[:, 0, 0:3 * P], bank[5][:, 0:3 * P])
                copy(sc[0:META, 0, 3 * P:640], bank[7][0:META, 0:REAL]).then_inc(probsT_ready, 1)

            def mix_hi_ret(h0, m0, c):
                act_e.wait_ge(ret_f, h0 + c + 1)
                copy(dn_hi[:, c, 0:REAL], ret_o[:, c, :]).then_inc(mix_hi_done, 1)

            def mix_hi_mla(hd, c):
                act_e.wait_ge(mla_out, hd + 1)
                copy(dn_hi[:, 2 + c, 0:REAL], bank[4 + 2 * c][:, 0:REAL]).then_inc(mix_hi_done, 1)

            split(0, 0)
            split(1, 1)
            act_e.wait_ge(ones_set, 2)
            std(0, TOK)
            split_normed(0, TOK)

            def tail1(u):
                if u + 2 == U_PRE + 2:
                    split(u + 2, u + 2, kind="kr")
                else:
                    split(u + 2, u + 2)

            ffn(0, TOK, tail1)
            std(1, TOK)
            std(2, TOK)
            split_normed(1, TOK)

            def latent_read(first, tiles, n, banks, dst):
                for c in range(tiles):
                    copy(dst[:, c, 0:n], bank[banks[c]][:, 0:n])
                    nc.scalar.activation(lat_sq[:, c, 0:n], bank[banks[c]][:, 0:n], ACT.Square).then_inc(lat_read, 1)

            def latent_std(index, rank, n):
                act_e.wait_ge(lat_ms, index + 1)
                nc.scalar.activation(rstd[:, 0:n], bank[7][:, 0:n], ACT.Sqrt, bias=eps, scale=1.0 / rank).then_inc(lat_std, 1)

            def latent_hi(before, tiles, n, f, dst):
                for c in range(tiles):
                    act_e.wait_ge(lat_normed, before + c + 1)
                    copy(dst[:, c, 0:n], f[:, c, 0:n]).then_inc(lat_hi_done, 1)

            for j in range(PRE_UNITS):
                u = U_PRE + j
                split(u + 2, u + 2, kind="kr" if j == 0 else "full")
                if j == 1:
                    act_e.wait_ge(unit_used, u + 1)
                    latent_read(0, CC, TOK, (0, 1), ckv_f)
                if j == 2:
                    act_e.wait_ge(unit_used, u + 1)
                    swap_halves(0, bank[2], TOK, 32)
                if j == 3:
                    latent_std(0, KV_RANK, TOK)
                    latent_hi(0, CC, TOK, ckv_f, ckv_hi)
                if j == 4:
                    act_e.wait_ge(unit_used, u + 1)
                    act_e.wait_ge(lat_ms, 1)
                    latent_read(2, 2, REAL, (3, 4), cq_f)
                if j == 6:
                    act_e.wait_ge(unit_used, u + 1)
                    for c in range(2):
                        copy(cq_f[:, 2 + c, :], bank[5 + c][:, 0:REAL])
                        nc.scalar.activation(lat_sq[:, 2 + c, 0:REAL], bank[5 + c][:, 0:REAL], ACT.Square).then_inc(lat_read, 1)
            act_e.wait_ge(spilled, 16)
            for j in range(PAIR_UNITS):
                u = U_MIX + j
                split(u + 2, u + 2, kind=pair_kind(j + 2))
                if j == 1:
                    latent_std(1, Q_RANK, REAL)
                    latent_hi(2, QC, REAL, cq_f, cq_hi)
                pair_projections(j, U_MIX, 1, 0, True)
            with act_e.Fori(0, PAIRS - 1) as i:
                u0 = U_MIX + PAIR_UNITS
                u = act_e.snap(i * 15 + u0)
                h0 = act_e.snap(i * 2)
                h1 = act_e.snap(i * 2 + 2)
                r0 = act_e.snap(i * 5 + 6)
                filled = act_e.snap(i * (15 // SLOTS * FILL))
                for j in range(15):
                    split(u + (j + 2), u0 + j + 2, kind=pair_kind(j + 2), filled=filled)
                    attention(j, h0, 0)
                    if j < PAIR_UNITS:
                        pair_projections(j, u, r0, h1, False)
            for j in range(1, 9):
                attention(j, HEADS - 2, 0)
            for q in range(4):
                u = U_FFN[1] - 4 + q
                split(u + 2, u + 2)
            std(3, REAL)
            std(4, REAL)
            split_normed(2, REAL)
            last = U_ALL - 1

            def tail2(u):
                if u + 2 <= last:
                    split(u + 2, u + 2)

            ffn(1, REAL, tail2)
            std(5, REAL)
            for t in range(2):
                for b in range(4):
                    act_e.wait_ge(out_tr, 4 * t + b + 1)
                    copy(raw[:, t, b * 512:(b + 1) * 512], bank[4 * (t % 2) + b][:, :]).then_inc(out_ready, 1)

        @block.tensor
        def _(pe):
            mm = nc.tensor.matmul

            def mm3(o, w, wl, x, xl, first, last):
                mm(o, w, x, start=first, stop=False)
                mm(o, w, xl, start=False, stop=False)
                return mm(o, wl, x, start=False, stop=last)

            def proj_unit(u, u0, kh, banks, n, fine=None):
                pe.wait_ge(lo_ready, u + 1)
                wh, wl = slot(w_hi, u0, k=8), slot(w_lo, u0, k=8)
                last = None
                for c in range(2):
                    for k in range(8):
                        kk = 8 * kh + k
                        if fine is not None and c == 0:
                            pe.wait_ge(hn_ready, fine + kk + 1)
                        cs = slice(c * P, (c + 1) * P)
                        last = mm3(bank[banks[c]][:, 0:n], wh[:, k, cs], wl[:, k, cs],
                                   hn_hi[:, kk, 0:n], hn_lo[:, kk, 0:n], kk == 0, kk == KC - 1)
                last.then_inc(unit_used, 1)

            def down_unit(u, u0, q, n):
                pe.wait_ge(lo_ready, u + 1)
                wh, wl = slot(w_hi, u0, k=4), slot(w_lo, u0, k=4)
                last = None
                for i in range(4):
                    o = bank[(4 if q % 2 == 0 else 0) + i][:, 0:n]
                    for k in range(4):
                        cs = slice(i * P, (i + 1) * P)
                        last = mm3(o, wh[:, k, cs], wl[:, k, cs], dn_hi[:, k, 0:n], dn_lo[:, k, 0:n],
                                   k == 0, k == 3)
                last.then_inc(unit_used, 1)

            def feature_sum(norm, n):
                pe.wait_ge(ssq_ready, norm + 1)
                mm(bank[7][:, 0:n], ones[:, :], ssq[:, 0:n], start=True, stop=True).then_inc(ms_done, 1)

            def ffn(f, n):
                U = U_FFN[f]
                ch = 44 * f
                A = A_FFN[f] + 4

                for j in range(8):
                    if j == 4 and f == 1:
                        pe.wait_ge(acc_ready, A_FFN[1])
                    proj_unit(U + j, U + j, j % 2, ((0, 1), (2, 3), (4, 5), (6, 7))[j // 2], n,
                              fine=(0, 2 * KC)[f] if j < 2 else None)
                with pe.Fori(0, SEGS - 1) as i:
                    u0 = U + 8
                    u = pe.snap(i * 12 + u0)
                    c0 = pe.snap(i * 4 + (ch + 4))
                    a0 = pe.snap(i * 4 + A)
                    for j in range(4):
                        if j == 0:
                            pe.wait_ge(silu_done, c0 - 2)
                            pe.wait_ge(acc_ready, a0)
                        if j == 2:
                            pe.wait_ge(act_done, c0 - 2)
                        proj_unit(u + j, u0 + j, j % 2, ((0, 1), (2, 3))[j // 2], n)
                    for q in range(4):
                        if q == 0:
                            pe.wait_ge(act_ready, c0)
                        if q == 1:
                            pe.wait_ge(silu_done, c0 + 2)
                            pe.wait_ge(act_done, c0 + 2)
                        if q > 1:
                            pe.wait_ge(acc_ready, a0 + (q - 1))
                        down_unit(u + (4 + q), u0 + 4 + q, q, n)
                    for j in range(4):
                        if j == 0:
                            pe.wait_ge(acc_ready, a0 + 3)
                        proj_unit(u + (8 + j), u0 + 8 + j, j % 2, ((4, 5), (6, 7))[j // 2], n)
                a0 = A + 4 * (SEGS - 1)
                pe.wait_ge(act_ready, ch + 44)
                for q in range(4):
                    pe.wait_ge(acc_ready, a0 + max(q - 1, 0))
                    u = U + FFN_UNITS - 4 + q
                    down_unit(u, u, q, n)

            def pair_projections(j, u, u0, r0, h0, p0):
                if j < 8:
                    b = ((0, 1), (2, 3))[(j // 2) % 2]
                    n = (TOK, REAL, TOK, REAL)[j // 2]
                    if j == 4:
                        pe.wait_ge(rotated, r0 + 2)
                    if j == 6:
                        pe.wait_ge(rotated, r0 + 4)
                    proj_unit(u + j, u0 + j, j % 2, b, n)
                if j == 8:
                    pe.wait_ge(lo_ready, u + 9)
                    pe.wait_ge(vT_ready, h0 + 2)
                    pe.wait_ge(lat_ready, CC + QC)
                    wh, wl = (slot(r, u0 + 8, k=QC, n=QC * 384) for r in (w_hi, w_lo))
                    last = None
                    for c in range(3):
                        if c == 2:
                            pe.wait_ge(gate_ready, h0 + 2)
                        for k in range(QC):
                            cs = slice(c * P, (c + 1) * P)
                            last = mm3(bank[c][:, 0:REAL], wh[:, k, cs], wl[:, k, cs], cq_hi[:, k, :], cq_lo[:, k, :],
                                       k == 0, k == QC - 1)
                    last.then_inc(unit_used, 1)
                    for c in range(2):
                        b = bank[(5, 7)[c]]
                        for r in range(3):
                            m = META if r == 2 else P
                            last = nc.tensor.transpose(b[0:m, r * P:(r + 1) * P], ret_vT[:, c, r * P:r * P + m], ident[:, :])
                        last.then_inc(v_tr, 1)
                if j == 9:
                    pe.wait_ge(lo_ready, u + 10)
                    wh, wl = (slot(r, u0 + 9, k=CC, n=CC * 256) for r in (w_hi, w_lo))
                    last = None
                    for c in range(2):
                        if c == 1:
                            pe.wait_ge(mq_ready, h0 + 1)
                        for k in range(CC):
                            cs = slice(c * P, (c + 1) * P)
                            last = mm3(bank[(3, 0)[c]][:, 0:TOK], wh[:, k, cs], wl[:, k, cs],
                                       ckv_hi[:, k, 0:TOK], ckv_lo[:, k, 0:TOK], k == 0, k == CC - 1)
                    last.then_inc(unit_used, 1)
                if j == 10:
                    pe.wait_ge(lo_ready, u + 11)
                    wh, wl = (slot(r, u0 + 10, k=CC, n=CC * 256) for r in (w_hi, w_lo))
                    last = None
                    for r in range(3):
                        if r == 0:
                            pe.wait_ge(mq_ready, h0 + 2)
                        if r == 1:
                            pe.wait_ge(rotated, r0 + 5)
                        if r == 2:
                            pe.wait_ge(mk_ready, h0 + 1)
                        o = bank[1 + r][:, 0:REAL]
                        ts = slice(r * P, (r + 1) * P)
                        for k in range(CC):
                            last = mm3(o, ckv_hi[:, k, ts], ckv_lo[:, k, ts], wh[:, k, :], wl[:, k, :],
                                       k == 0, k == CC - 1)
                    last.then_inc(unit_used, 1)

            def values(o, v_real, v_meta, s):
                mm(o[:, 0:REAL], v_real[0], s[:, 0:REAL], start=True, stop=False)
                mm(o[:, P:REAL], v_real[1], s[:, REAL:3 * P], start=False, stop=False)
                return mm(o[:, 0:REAL], v_meta, s[0:META, 3 * P:640], start=False, stop=True)

            def attention(g, h0, r0, p1):
                if g == 0:
                    pe.wait_ge(rotated, r0 + 4)
                    pe.wait_ge(v_ready, h0 + 2)
                    for c in range(2):
                        s, m = bank[4 + 2 * c], bank[5 + 2 * c]
                        k, q = ret_k[:, c, :], ret_q[:, c, :]
                        mm(s[:, 0:REAL], k[:, 0:P], q, start=True, stop=True)
                        mm(s[:, REAL:3 * P], k[:, P:REAL], q[:, P:REAL], start=False, stop=True, skip_group_check=True)
                        mm(m[0:META, 0:REAL], k[:, REAL:TOK], q, start=True, stop=True).then_inc(ret_scores, 1)
                if g == 1:
                    for c in range(2):
                        pe.wait_ge(ret_masked, h0 + c + 1)
                        v = ret_v[:, c, :]
                        values(bank[4 + 2 * c], (v[:, 0:P], v[:, P:REAL]), v[0:META, REAL:3 * P],
                               sc[:, c, :]).then_inc(ret_out, 1)
                if g == 2:
                    for c in range(2):
                        pe.wait_ge(ret_sq_done, h0 + c + 1)
                        mm(bank[4 + 2 * c][:, 0:REAL], ones[:, :], ret_sq[:, c, :], start=True, stop=True).then_inc(ret_ms, 1)
                    mla_s(h0, 0, r0, p1)
                if g == 3:
                    mla_t(h0)
                if g == 4:
                    mla_o(h0, 0)
                    mla_s(h0, 1, r0, p1)
                if g == 5:
                    mla_t(h0 + 1)
                if g == 6:
                    mla_o(h0, 1)

            def mla_s(h0, c, r0, p1):
                pe.wait_ge(mk_ready, h0 + 2)
                pe.wait_ge(rotated, r0 + 5)
                rows = slice(64 * c, 64 * c + 64)
                for t in range(2):
                    ts = slice(t * P, (t + 1) * P)
                    b = bank[(5, 7)[t]][:, 0:TOK]
                    mm(b, mla_q[:, c, ts], mla_k[:, c, :], start=True, stop=False)
                    mm(b, mla_qr[rows, ts], mla_kr[rows, :], start=False, stop=True).then_inc(mla_scores, 1)

            def mla_t(hd):
                pe.wait_ge(probs_ready, hd * 2 + 2)
                tr = nc.tensor.transpose
                tr(bank[5][:, 0:P], probs[:, 0, 0:P], ident[:, :])
                tr(bank[5][:, P:REAL], probs[:, 1, 0:P], ident[:, :])
                tr(bank[5][:, REAL:3 * P], probs[:, 1, P:REAL], ident[:, :])
                tr(bank[7][0:META, 0:P], probs[:, 0, REAL:TOK], ident[:, :])
                tr(bank[7][0:META, P:REAL], probs[:, 1, REAL:TOK], ident[:, :]).then_inc(probs_tr, 1)

            def mla_o(h0, c):
                pe.wait_ge(probsT_ready, h0 + c + 1)
                pe.wait_ge(ret_std, h0 + c + 1)
                cs = slice(c * P, (c + 1) * P)
                values(bank[4 + 2 * c], (mla_v[:, 0, cs], mla_v[:, 1, cs]), mla_v[0:META, 2, cs],
                       sc[:, 0, :]).then_inc(mla_out, 1)

            pe.wait_ge(consts_in, 16 * 13)
            nc.tensor.transpose(bank[0][:, 0:GAINS], gain_rows, ident[0:GAINS, 0:GAINS]).then_inc(gains_tr, 1)
            pe.wait_ge(x_in, 32)
            for c in range(KC):
                b = bank[c % 8]
                if c == 0:
                    pe.wait_ge(gains_ready, 1)
                if c >= 8:
                    pe.wait_ge(h_ready, c - 7)
                cs = slice(c * P, (c + 1) * P)
                for t in range(2):
                    nc.tensor.transpose(b[:, t * P:(t + 1) * P], x_sb[:, t, cs], ident[:, :])
                nc.tensor.transpose(b[:, REAL:TOK], meta_sb[:, cs], ident[0:META, 0:META]).then_inc(x_tr, 1)
            pe.wait_ge(ones_set, 2)
            feature_sum(0, TOK)
            ffn(0, TOK)
            feature_sum(1, TOK)
            feature_sum(2, TOK)

            for j in range(2):
                proj_unit(U_PRE + j, U_PRE + j, j, (0, 1), TOK, fine=KC)
            u = U_PRE + 2
            pe.wait_ge(lo_ready, u + 1)
            wh, wl = slot(w_hi, u, k=KC), slot(w_lo, u, k=KC)
            for k in range(KC):
                last = mm3(bank[2][:, 0:TOK], wh[:, k, :], wl[:, k, :], hn_hi[:, k, :], hn_lo[:, k, :],
                           k == 0, k == KC - 1)
            last.then_inc(unit_used, 1)
            pe.wait_ge(lat_read, CC)
            for c in range(CC):
                last = mm(bank[7][:, 0:TOK], ones[:, :], lat_sq[:, c, :], start=(c == 0), stop=(c == CC - 1))
            last.then_inc(lat_ms, 1)
            for j in range(4):
                proj_unit(U_PRE + 3 + j, U_PRE + 3 + j, j % 2, ((3, 4), (5, 6))[j // 2], REAL)
            for j in range(PAIR_UNITS):
                if j == 1:
                    pe.wait_ge(lat_read, CC + QC)
                    pe.wait_ge(lat_std, 1)
                    for c in range(QC):
                        last = mm(bank[7][:, 0:REAL], ones[:, :], lat_sq[:, c, 0:REAL], start=(c == 0), stop=(c == QC - 1))
                    last.then_inc(lat_ms, 1)
                if j == 2:
                    pe.wait_ge(rotated, 1)
                pair_projections(j, U_MIX, U_MIX, 1, 0, 0)
            STAGE = {0: 1, 1: 2, 3: 3, 4: 4, 6: 5, 7: 6}
            with pe.Fori(0, PAIRS - 1) as i:
                u0 = U_MIX + PAIR_UNITS
                u = pe.snap(i * 15 + u0)
                h0 = pe.snap(i * 2)
                h1 = pe.snap(i * 2 + 2)
                r0 = pe.snap(i * 5 + 1)
                r1 = pe.snap(i * 5 + 6)
                p1 = pe.snap(i + 1)
                a0 = pe.snap(i * 4 + (A_MIX + 4))
                pe.wait_ge(acc_ready, a0)
                attention(0, h0, r0, p1)
                for j in range(PAIR_UNITS):
                    if j == 0:
                        pe.wait_ge(mk_ready, h0 + 2)
                        pe.wait_ge(mv_ready, p1)
                    pair_projections(j, u, u0, r1, h1, p1)
                    if j in STAGE:
                        attention(STAGE[j], h0, r0, p1)
                for q in range(4):
                    if q == 0:
                        pe.wait_ge(mix_ready, h0 * 2 + 4)
                        pe.wait_ge(v_ready, h1 + 2)
                    if q == 1:
                        pe.wait_ge(mk_ready, h1 + 2)
                        pe.wait_ge(mv_ready, p1 + 1)
                    if q > 1:
                        pe.wait_ge(acc_ready, a0 + (q - 1))
                    down_unit(u + (11 + q), u0 + 11 + q, q, REAL)
            a0 = A_MIX + 4 + 4 * (PAIRS - 1)
            pe.wait_ge(acc_ready, a0)
            pe.wait_ge(mv_ready, PAIRS)
            for g in range(7):
                attention(g, HEADS - 2, 1 + 5 * (PAIRS - 1), PAIRS)
            pe.wait_ge(mix_ready, 4 * PAIRS)
            for q in range(4):
                if q > 1:
                    pe.wait_ge(acc_ready, a0 + q - 1)
                u = U_FFN[1] - 4 + q
                down_unit(u, u, q, REAL)
            feature_sum(3, REAL)
            feature_sum(4, REAL)
            ffn(1, REAL)
            feature_sum(5, REAL)
            pe.wait_ge(rstd_done, 6)
            for t in range(2):
                for b in range(4):
                    for i in range(4):
                        c = 4 * b + i
                        pe.wait_ge(h_ready, 3 * KC + c + 1)
                        last = nc.tensor.transpose(bank[4 * t + b][:, i * P:(i + 1) * P], h[:, c, t * P:(t + 1) * P], ident[:, :])
                    last.then_inc(out_tr, 1)

        @block.vector
        def _(dve):
            tt, stt, ts = nc.vector.tensor_tensor, nc.vector.scalar_tensor_tensor, nc.vector.tensor_scalar

            class Own:
                n, turn, per = 0, None, 0

                def wait(self):
                    dve.wait_ge(dve_step, self.n if self.turn is None else self.turn * self.per + self.n)

                def step(self, ins):
                    ins.then_inc(dve_step, 1)
                    self.n += 1

            own = Own()

            def split(u, u0, kind="full"):
                dve.wait_ge(hi_ready, u + 1)
                for src, hi, lo in split_parts(u0, kind):
                    last = tt(lo, src, hi.bitcast(F32), ALU.subtract)
                last.then_inc(lo_ready, 1)

            def clear_acc():
                for q in range(4):
                    nc.vector.memset(acc_t[:, 4 * q:4 * q + 4, :], 0.0).then_inc(acc_ready, 1)

            def add_group(u, q, ready, n):
                dve.wait_ge(unit_used, u + 1)
                dve.wait_ge(acc_ready, ready)
                last = None
                for i in range(4):
                    c = 4 * q + i
                    b = bank[(4 if q % 2 == 0 else 0) + i][:, 0:n]
                    last = tt(acc_t[:, c, 0:n], acc_t[:, c, 0:n], b, ALU.add)
                last.then_inc(acc_ready, 1)

            def rstd_of(norm, n):
                dve.wait_ge(std_done, norm + 1)
                nc.vector.reciprocal(rstd[:, 0:n], rstd[:, 0:n]).then_inc(rstd_done, 1)
                dve.wait_ge(rstd_done, norm + 1)

            def post_norm(norm, stage, n, factor, rounds):
                rstd_of(norm, n)
                for c in range(KC):
                    own.step(stt(out=acc_t[:, c, 0:n], in0=acc_t[:, c, 0:n], scalar=gains[:, G_POST[stage] + c:G_POST[stage] + c + 1],
                                 in1=rstd[:, 0:n], op0=ALU.mult, op1=ALU.mult))
                for c in range(KC):
                    if c == 0:
                        own.wait()
                    stt(out=h[:, c, 0:n], in0=acc_t[:, c, 0:n], scalar=factor, in1=h[:, c, 0:n],
                        op0=ALU.mult, op1=ALU.add).then_inc(h_ready, 1)

            def pre_norm(norm, stage, n):
                rstd_of(norm, n)
                for c in range(KC + 1):
                    if c < KC:
                        stt(out=acc_t[:, c, 0:n], in0=h[:, c, 0:n], scalar=gains[:, G_PRE[stage] + c:G_PRE[stage] + c + 1],
                            in1=rstd[:, 0:n], op0=ALU.mult, op1=ALU.mult).then_inc(normed, 1)
                    if c > 0:
                        k = c - 1
                        dve.wait_ge(hn_hi_done, stage * KC + k + 1)
                        tt(hn_lo[:, k, 0:n], acc_t[:, k, 0:n], hn_hi[:, k, 0:n].bitcast(F32), ALU.subtract).then_inc(hn_ready, 1)
                dve.wait_ge(hn_ready, stage * KC + KC)
                clear_acc()

            def ffn(f, n, tail):
                U = U_FFN[f]
                ch = 44 * f
                A = A_FFN[f] + 4

                def up_times(u, c0, first_bank):
                    dve.wait_ge(unit_used, u + 1)
                    for c in range(2):
                        dve.wait_ge(silu_done, c0 + c + 1)
                        if not (isinstance(c0, int) and c0 + c < 2):
                            dve.wait_ge(act_ready, c0 + c - 1)
                        tt(act[:, c, 0:n], sil[:, c, 0:n], bank[first_bank + c][:, 0:n], ALU.mult).then_inc(act_done, 1)

                def act_lo(c0, half):
                    for c in range(2):
                        dve.wait_ge(act_hi_done, c0 + c + 1)
                        k = 2 * half + c
                        tt(dn_lo[:, k, 0:n], act[:, c, 0:n], dn_hi[:, k, 0:n].bitcast(F32), ALU.subtract).then_inc(act_ready, 1)

                for j in range(8):
                    split(U + j + 2, U + j + 2)
                    if j in (3, 7):
                        up_times(U + j, ch + (j > 4) * 2, 2 + 4 * (j > 4))
                        act_lo(ch + (j > 4) * 2, int(j > 4))
                with dve.Fori(0, SEGS - 1) as i:
                    u0 = U + 8
                    u = dve.snap(i * 12 + u0)
                    c0 = dve.snap(i * 4 + (ch + 4))
                    a0 = dve.snap(i * 4 + A)
                    for j in range(12):
                        split(u + (j + 2), u0 + j + 2)
                        if j == 3:
                            up_times(u + 3, c0, 2)
                        if 4 <= j < 8:
                            add_group(u + j, j - 4, a0 + (j - 4 - 3), n)
                        if j == 7:
                            act_lo(c0, 0)
                        if j == 11:
                            up_times(u + 11, c0 + 2, 6)
                            act_lo(c0 + 2, 1)
                a0 = A + 4 * (SEGS - 1)
                for q in range(4):
                    u = U + FFN_UNITS - 4 + q
                    tail(u)
                    add_group(u, q, a0 + q - 3, n)

            def rotate(index, src, n, table, dst):
                dve.wait_ge(swapped, index + 1)
                own.step(tt(prod[:, 0:n], src[:, 0:n], table[:, 0, 0:n], ALU.mult))
                own.step(tt(swap[:, 0:n], swap[:, 0:n], table[:, 1, 0:n], ALU.mult))
                own.wait()
                tt(dst, prod[:, 0:n], swap[:, 0:n], ALU.add).then_inc(rotated, 1)
                dve.wait_ge(rotated, index + 1)

            def pair_projections(j, u, r0, h0, p0):
                if j == 1:
                    for c in range(2):
                        rotate(r0 + c, bank[c], TOK, rope_ret, ret_k[:, c, :])
                if j == 3:
                    for c in range(2):
                        rotate(r0 + 2 + c, bank[2 + c], REAL, rope_ret, ret_q[:, c, :])
                if j == 8:
                    rotate(r0 + 4, bank[2], REAL, rope_mla, mla_qr)
                if j == 10:
                    dve.wait_ge(unit_used, u + 11)
                    nc.vector.tensor_copy(mla_v[:, 0, :], bank[1][:, 0:REAL])
                    nc.vector.tensor_copy(mla_v[:, 1, :], bank[2][:, 0:REAL])
                    nc.vector.tensor_copy(mla_v[0:META, 2, :], bank[3][0:META, 0:REAL]).then_inc(mv_ready, 1)

            def attention(j, h0, p0):
                if j == 0:
                    dve.wait_ge(decay_in, p0 * 32 + 32)
                    for c in range(2):
                        dve.wait_ge(ret_scores, h0 + c + 1)
                        tt(sc[:, c, 0:3 * P], bank[4 + 2 * c][:, 0:3 * P], decay[:, c, :], ALU.mult)
                        tt(sc[0:META, c, 3 * P:640], bank[5 + 2 * c][0:META, 0:REAL], decay_meta[0:META, c, :], ALU.mult).then_inc(ret_masked, 1)
                    own.step(nc.vector.tensor_copy(small[:, 8:10], gains[:, bass.ds(h0 + G_RET, 2)]))
                if j == 2:
                    softmax(h0)
                if j == 3:
                    group_norm(h0, p0, 0)
                if j == 4:
                    group_norm(h0, p0, 1)
                if j == 5:
                    mla_lo(h0, p0, 0)
                    softmax(h0 + 1)
                if j == 8:
                    mla_lo(h0, p0, 1)

            def softmax(hd):
                for t in range(2):
                    b = bank[(5, 7)[t]][:, 0:TOK]
                    dve.wait_ge(mla_scores, hd * 2 + (t + 1))
                    own.step(stt(out=probs[:, t, :], in0=b, scalar=MLA_SCALE, in1=mask[:, t, :], op0=ALU.mult, op1=ALU.add))
                    own.wait()
                    own.step(nc.vector.reduce_max(small[:, 2 + t:3 + t], probs[:, t, :], AX.X))
                    own.wait()
                    ts(small[:, 4 + t:5 + t], small[:, 2 + t:3 + t], -1.0, None, ALU.mult).then_inc(neg_max, 1)
                for t in range(2):
                    dve.wait_ge(exp_done, hd * 2 + (t + 1))
                    own.step(nc.vector.reciprocal(small[:, 10 + t:11 + t], small[:, 6 + t:7 + t]))
                    own.wait()
                    ts(probs[:, t, :], probs[:, t, :], small[:, 10 + t:11 + t], None, ALU.mult).then_inc(probs_ready, 1)

            def group_norm(h0, p0, c):
                dve.wait_ge(ret_std, h0 + c + 1)
                dve.wait_ge(gate_ready, h0 + c + 1)
                own.step(nc.vector.reciprocal(ret_rs[:, c, :], ret_rs[:, c, :]))
                own.wait()
                own.step(tt(ret_o[:, c, :], ret_o[:, c, :], ret_rs[:, c, :], ALU.mult))
                own.wait()
                stt(out=ret_o[:, c, :], in0=ret_o[:, c, :], scalar=small[:, 8 + c:9 + c], in1=ret_gate[:, c, :],
                    op0=ALU.mult, op1=ALU.mult).then_inc(ret_f, 1)
                dve.wait_ge(mix_hi_done, p0 * 4 + (c + 1))
                tt(dn_lo[:, c, 0:REAL], ret_o[:, c, :], dn_hi[:, c, 0:REAL].bitcast(F32), ALU.subtract).then_inc(mix_ready, 1)

            def mla_lo(h0, p0, c):
                dve.wait_ge(mix_hi_done, p0 * 4 + (c + 3))
                tt(dn_lo[:, 2 + c, 0:REAL], bank[4 + 2 * c][:, 0:REAL], dn_hi[:, 2 + c, 0:REAL].bitcast(F32), ALU.subtract).then_inc(mix_ready, 1)

            split(0, 0)
            split(1, 1)
            dve.wait_ge(gains_tr, 1)
            nc.vector.tensor_copy(gains[:, :], bank[0][:, 0:GAINS]).then_inc(gains_ready, 1)
            for c in range(KC):
                dve.wait_ge(x_tr, c + 1)
                nc.vector.tensor_copy(h[:, c, :], bank[c % 8][:, 0:TOK]).then_inc(h_ready, 1)
            dve.wait_ge(gains_ready, 1)
            dve.wait_ge(h_ready, KC)
            pre_norm(0, 0, TOK)
            ffn(0, TOK, lambda u: split(u + 2, u + 2, kind="kr" if u + 2 == U_PRE + 2 else "full"))
            dve.wait_ge(acc_ready, A_MIX)
            post_norm(1, 0, TOK, 0.5, 0)
            dve.wait_ge(h_ready, 2 * KC)
            pre_norm(2, 1, TOK)

            dve.wait_ge(pad_zero, 2)

            def latent_norm(index, before, tiles, n, f, gain, hi, lo):
                dve.wait_ge(lat_std, index + 1)
                own.step(nc.vector.reciprocal(rstd[:, 0:n], rstd[:, 0:n]))
                own.wait()
                for c in range(tiles):
                    stt(out=f[:, c, 0:n], in0=f[:, c, 0:n], scalar=gains[:, gain + c:gain + c + 1],
                        in1=rstd[:, 0:n], op0=ALU.mult, op1=ALU.mult).then_inc(lat_normed, 1)
                for c in range(tiles):
                    dve.wait_ge(lat_hi_done, before + c + 1)
                    tt(lo[:, c, 0:n], f[:, c, 0:n], hi[:, c, 0:n].bitcast(F32), ALU.subtract).then_inc(lat_ready, 1)

            for j in range(PRE_UNITS):
                u = U_PRE + j
                split(u + 2, u + 2, kind="kr" if j == 0 else "full")
                if j == 2:
                    rotate(0, bank[2], TOK, rope_mla, mla_kr)
                if j == 3:
                    latent_norm(0, 0, CC, TOK, ckv_f, G_KV, ckv_hi, ckv_lo)
            dve.wait_ge(spilled, 16)
            for j in range(PAIR_UNITS):
                u = U_MIX + j
                split(u + 2, u + 2, kind=pair_kind(j + 2))
                if j == 1:
                    latent_norm(1, CC, QC, REAL, cq_f, G_Q, cq_hi, cq_lo)
                pair_projections(j, U_MIX, 1, 0, 0)
            with dve.Fori(0, PAIRS - 1) as i:
                u0 = U_MIX + PAIR_UNITS
                u = dve.snap(i * 15 + u0)
                h0 = dve.snap(i * 2)
                h1 = dve.snap(i * 2 + 2)
                r0 = dve.snap(i * 5 + 6)
                a0 = dve.snap(i * 4 + (A_MIX + 4))
                PER = 27
                own.turn, own.per, start = i, PER, own.n
                for j in range(15):
                    split(u + (j + 2), u0 + j + 2, kind=pair_kind(j + 2))
                    attention(j, h0, i)
                    if j < PAIR_UNITS:
                        pair_projections(j, u, r0, h1, i + 1)
                    else:
                        add_group(u + j, j - 11, a0 + (j - 11 - 3), REAL)
                assert own.n - start == PER, own.n - start
                own.n, own.turn = start + PER * (PAIRS - 1), None
            for j in range(9):
                attention(j, HEADS - 2, PAIRS - 1)
            a0 = A_MIX + 4 + 4 * (PAIRS - 1)
            for q in range(4):
                u = U_FFN[1] - 4 + q
                split(u + 2, u + 2)
                add_group(u, q, a0 + q - 3, REAL)
            dve.wait_ge(acc_ready, A_FFN[1])
            dve.wait_ge(reloaded, 16)
            post_norm(3, 1, REAL, 1.0, 0)
            dve.wait_ge(h_ready, 3 * KC)
            pre_norm(4, 2, REAL)

            def tail(u):
                if u + 2 < U_ALL:
                    split(u + 2, u + 2)

            ffn(1, REAL, tail)
            dve.wait_ge(acc_ready, A_FFN[1] + 4 + 4 * SEGS)
            post_norm(5, 2, REAL, 0.5, 0)


_INS = ["x", "meta_tokens", "ffn1_pre_norm", "ffn1_w_gate", "ffn1_w_up", "ffn1_w_down",
        "ffn1_post_norm", "mix_pre_norm", "w_in", "ret_group_norm", "mla_q_norm", "mla_w_uq",
        "mla_kv_norm", "mla_w_uk", "mla_w_uv", "w_out", "mix_post_norm", "ffn2_pre_norm",
        "ffn2_w_gate", "ffn2_w_up", "ffn2_w_down", "ffn2_post_norm"]


def kernel(**inputs):
    import concourse.bacc as bacc
    from concourse.bass_utils import run_bass_kernel_spmd

    nc = bacc.Bacc("TRN2", target_bir_lowering=False, num_devices=1)
    arrays, aps = {}, {}
    for name in _INS:
        x = np.ascontiguousarray(inputs[name])
        if x.ndim == 3:
            x = x.reshape(x.shape[1:])
        arrays[f"in_{name}"] = x
    for name, x in constants().items():
        arrays[f"in_{name}"] = x
    for name, x in arrays.items():
        aps[name[3:]] = nc.dram_tensor(name, x.shape, mybir.dt.from_np(x.dtype), kind="ExternalInput").ap()
    out = nc.dram_tensor("out_dram", (REAL, DM), F32, kind="ExternalOutput").ap()
    build(nc, aps, out)
    r = run_bass_kernel_spmd(nc, [arrays], core_ids=[0])
    return r.results[0]["out_dram"].reshape(1, REAL, DM)
```

```python
from contextlib import ExitStack

import numpy as np

import concourse.bass as bass
from concourse import mybir

ACT = mybir.ActivationFunctionType
ALU = mybir.AluOpType
AX = mybir.AxisListType
F32 = mybir.dt.float32
F32R = mybir.dt.float32r

P = 128
DM, FF = 2048, 5632
REAL, META = 256, 16
TOK = REAL + META
KC = DM // P
HEADS, DH, ROPE = 8, 128, 64
Q_RANK, KV_RANK = 512, 256
QC, CC = Q_RANK // P, KV_RANK // P
EPS = 1e-6
MLA_SCALE = float(DH + ROPE) ** -0.5
PAIRS = HEADS // 2

UNIT = 2048
SLOTS = 3
SEG = 512
SEGS = FF // SEG
FFN_UNITS = 12 * SEGS
PRE_UNITS = 7
PAIR_UNITS = 11
OUT_UNITS = 4
U_FFN = (0, FFN_UNITS + PRE_UNITS + PAIRS * (PAIR_UNITS + OUT_UNITS))
U_PRE = FFN_UNITS
U_MIX = U_PRE + PRE_UNITS
U_ALL = U_FFN[1] + FFN_UNITS
C_RQ, C_RK, C_RV, C_RG = 0, 1024, 2048, 3072
C_CQ, C_CKV, C_KR = 4096, 4608, 4864
A_FFN = (0, 4 + 4 * SEGS + 4 + 4 * PAIRS)
A_MIX = 4 + 4 * SEGS
A_DONE = tuple(a + 4 + 4 * (n - 1) for a, n in ((A_FFN[0], SEGS), (A_MIX, PAIRS), (A_FFN[1], SEGS)))
POOL_OUT = (14, 38, 62)
X_AHEAD = 6
UNIT_AT_CHUNK = (0, 6, 12)
G_PRE, G_POST = (0, 2 * KC, 4 * KC), (KC, 3 * KC, 5 * KC)
G_RET = 6 * KC
G_Q, G_KV = G_RET + HEADS, G_RET + HEADS + QC
GAINS = G_KV + CC


def pair_unit(p, j):
    if isinstance(p, int):
        return U_MIX + (j if p == 0 else PAIR_UNITS + 15 * (p - 1) + j)
    raise TypeError("give loops their own base")


def constants():
    pos = np.concatenate([META + np.arange(REAL), np.arange(META)]).astype(np.float32)

    def rope(dim):
        inv = np.float32(10000.0) ** (-np.arange(0, dim, 2, dtype=np.float32) / np.float32(dim))
        ang = (pos[:, None] * inv[None, :]).astype(np.float32)
        c, s = np.cos(ang).T, np.sin(ang).T
        reps = P // dim
        return np.stack([np.concatenate([c, c] * reps), np.concatenate([-s, s] * reps)])

    tri = np.where(np.arange(P)[None, :] <= np.arange(P)[:, None], 0.0, -1e30)
    mask = np.zeros((2, P, TOK))
    mask[0, :, 0:P], mask[0, :, P:REAL] = tri, -1e30
    mask[1, :, P:REAL] = tri
    log_g = np.log(1.0 - 2.0 ** (-5.0 - np.arange(HEADS)))
    m, n = np.arange(P), np.arange(REAL)
    diff = (n[None, :] - m[:, None])[None]
    d = np.where(diff >= 0, np.exp(np.maximum(diff, 0) * log_g[:, None, None]), 0.0) * DH ** -0.5
    d = np.concatenate([d, d[:, :, 0:P]], axis=2)
    dm = np.exp((META + n[None, :] - np.arange(META)[:, None])[None] * log_g[:, None, None]) * DH ** -0.5
    f = lambda a: np.ascontiguousarray(a, dtype=np.float32)
    return {
        "rope_ret": f(rope(DH)), "rope_mla": f(rope(ROPE)), "mask": f(mask),
        "decay": f(d.reshape(PAIRS, 2, P, 3 * P).transpose(0, 2, 1, 3)),
        "decay_meta": f(dm.reshape(PAIRS, 2, META, REAL).transpose(0, 2, 1, 3)),
        "ident": f(np.eye(P)),
    }


def build(nc, a, out):
    ctx = ExitStack()
    with ctx:
        def sb(name, shape, dt=F32):
            return ctx.enter_context(nc.sbuf_tensor(name, shape, dt))

        def sem(name):
            return ctx.enter_context(nc.semaphore(name))

        raw = sb("raw", [P, SLOTS, UNIT])
        w_hi = sb("w_hi", [P, SLOTS, UNIT], F32R)
        w_lo = sb("w_lo", [P, SLOTS, UNIT], F32R)
        hT = sb("hT", [P, KC * TOK])
        hn_hi = sb("hn_hi", [P, KC, TOK], F32R)
        hn_lo = sb("hn_lo", [P, KC, TOK], F32R)
        acc = sb("acc", [P, KC * TOK])
        dn_hi = sb("dn_hi", [P, 4, TOK], F32R)
        dn_lo = sb("dn_lo", [P, 4, TOK], F32R)
        tmp = sb("tmp", [P, 4, TOK])
        gains = sb("gains", [P, GAINS])
        ident = sb("ident_sb", [P, P])
        ones = sb("ones", [P, P])
        rope_ret = sb("rope_ret_sb", [P, 2, TOK])
        rope_mla = sb("rope_mla_sb", [P, 2, TOK])
        mask = sb("mask_sb", [P, 2, TOK])
        ssq = sb("ssq", [P, TOK])
        rstd = sb("rstd", [P, TOK])
        r_pre = sb("r_pre", [P, TOK])
        small = sb("small", [P, 16])
        eps = small[:, 0:1]
        ckv_hi = sb("ckv_hi", [P, CC, 3 * P], F32R)
        ckv_lo = sb("ckv_lo", [P, CC, 3 * P], F32R)
        cq_hi = sb("cq_hi", [P, QC, REAL], F32R)
        cq_lo = sb("cq_lo", [P, QC, REAL], F32R)

        h = hT[:, :].rearrange("p (c n) -> p c n", c=KC)
        acc_t = acc[:, :].rearrange("p (c n) -> p c n", c=KC)
        sil, act = tmp[:, 0:2, :], tmp[:, 2:4, :]
        swap, prod, probs = tmp[:, 0, :], tmp[:, 1, :], tmp[:, 2:4, :]

        at = [0]

        def carve(t, size, n):
            v = t[:, at[0]:at[0] + size]
            at[0] += size
            return v.rearrange("p (a n) -> p a n", n=n)

        ret_k = carve(hT, 2 * TOK, TOK)
        ret_q = carve(hT, 2 * REAL, REAL)
        ret_vT = carve(hT, 2 * TOK, TOK)
        ret_v = carve(hT, 2 * 3 * P, 3 * P)
        ret_gate = carve(hT, 2 * REAL, REAL)
        mla_q = carve(hT, 2 * REAL, REAL)
        mla_qr = carve(hT, REAL, REAL)[:, 0, :]
        mla_k = carve(hT, 2 * TOK, TOK)
        assert at[0] <= KC * TOK
        MIX = TOK + 3 * REAL + 2 * 640 + 2 * 3 * P + 2 * REAL + 2 * TOK + QC * REAL
        mix = sb("mix", [P, MIX])
        at[0] = 0
        mla_kr = carve(mix, TOK, TOK)[:, 0, :]
        mla_v = carve(mix, 3 * REAL, REAL)
        sc = carve(mix, 2 * 640, 640)
        decay = carve(mix, 2 * 3 * P, 3 * P)
        decay_meta = carve(mix, 2 * REAL, REAL)
        keep = carve(mix, 2 * TOK + QC * REAL, 2 * TOK + QC * REAL)[:, 0, :]
        lat_sq = mix[:, TOK + 3 * REAL:TOK + 3 * REAL + 4 * TOK].rearrange("p (a n) -> p a n", n=TOK)
        ckv_f = keep[:, 0:2 * TOK].rearrange("p (a n) -> p a n", n=TOK)
        cq_f = keep[:, 2 * TOK:].rearrange("p (a n) -> p a n", n=REAL)
        ret_o = keep[:, 0:2 * REAL].rearrange("p (a n) -> p a n", n=REAL)
        ret_sq = keep[:, 2 * REAL:4 * REAL].rearrange("p (a n) -> p a n", n=REAL)
        ret_rs = keep[:, 4 * REAL:6 * REAL].rearrange("p (a n) -> p a n", n=REAL)
        x_sb = acc[:, 0:2 * DM].rearrange("p (t d) -> p t d", t=2)
        meta_sb = mix[0:META, 0:DM]
        gain_rows = mix[0:GAINS, DM:DM + P]

        bank = [ctx.enter_context(nc.psum_tensor(f"bank{i}", [P, 512], F32)) for i in range(8)]
        spill = nc.dram_tensor("h_spill", (P, KC * TOK), F32).ap()

        gains_in = sem("gains_in")
        consts_in = sem("consts_in")
        tables_in = sem("tables_in")
        x_in = [sem(f"x_in{i}") for i in range(4)]
        raw_full = [sem(f"raw_full{i}") for i in range(SLOTS)]
        hi_ready = sem("hi_ready")
        lo_ready = sem("lo_ready")
        unit_used = sem("unit_used")
        ones_set = sem("ones_set")
        gains_tr = sem("gains_tr")
        gains_ready = sem("gains_ready")
        x_tr = sem("x_tr")
        h_ready = sem("h_ready")
        post_scaled = sem("post_scaled")
        tile_done = sem("tile_done")
        tile_added = sem("tile_added")
        squared = sem("squared")
        pool_step = sem("pool_step")
        ssq_ready = sem("ssq_ready")
        ms_done = sem("ms_done")
        std_done = sem("std_done")
        rstd_done = sem("rstd_done")
        dve_step = sem("dve_step")
        hn_hi_done = sem("hn_hi_done")
        hn_ready = sem("hn_ready")
        up_scaled = sem("up_scaled")
        gate_scaled = sem("gate_scaled")
        silu_done = sem("silu_done")
        act_done = sem("act_done")
        act_hi_done = sem("act_hi_done")
        act_ready = sem("act_ready")
        acc_ready = sem("acc_ready")
        swapped = sem("swapped")
        rotated = sem("rotated")
        vT_ready = sem("vT_ready")
        rg_scaled = sem("rg_scaled")
        gate_ready = sem("gate_ready")
        v_tr = sem("v_tr")
        v_ready = sem("v_ready")
        mq_ready = sem("mq_ready")
        mk_ready = sem("mk_ready")
        mv_ready = sem("mv_ready")
        ret_scores = sem("ret_scores")
        ret_masked = sem("ret_masked")
        ret_out = sem("ret_out")
        ret_sq_done = sem("ret_sq_done")
        ret_ms = sem("ret_ms")
        ret_std = sem("ret_std")
        ret_f = sem("ret_f")
        mix_hi_done = sem("mix_hi_done")
        mix_ready = sem("mix_ready")
        mla_scores = sem("mla_scores")
        neg_max = sem("neg_max")
        exp_done = sem("exp_done")
        probs_ready = sem("probs_ready")
        probs_tr = sem("probs_tr")
        probsT_ready = sem("probsT_ready")
        mla_out = sem("mla_out")
        lat_read = sem("lat_read")
        lat_sqd = sem("lat_sqd")
        lat_ms = sem("lat_ms")
        lat_std = sem("lat_std")
        lat_normed = sem("lat_normed")
        lat_hi_done = sem("lat_hi_done")
        lat_ready = sem("lat_ready")
        pad_zero = sem("pad_zero")
        decay_in = sem("decay_in")
        spilled = sem("spilled")
        reloaded = sem("reloaded")
        out_tr = sem("out_tr")
        out_ready = sem("out_ready")
        stored = sem("stored")

        def slot(ring, u0, **shape):
            v = ring[:, u0 % SLOTS, :]
            n = UNIT
            if "n" in shape:
                n = shape["n"]
                v = v[:, 0:n]
            k = shape["k"]
            return v.rearrange("p (k n) -> p k n", k=k)

        def split_parts(u0, kind):
            if kind == "kr":
                src = slot(raw, u0, k=KC, n=KC * ROPE)
                hi, lo = (slot(r, u0, k=KC).rearrange("p k (r n) -> p k r n", r=2) for r in (w_hi, w_lo))
                return [(src, hi[:, :, r, :], lo[:, :, r, :]) for r in range(2)]
            if kind == "uq":
                src = slot(raw, u0, k=QC, n=QC * 384).rearrange("p k (h n) -> p k h n", h=2)
                hi, lo = (slot(r, u0, k=QC, n=QC * 384) for r in (w_hi, w_lo))
                cut = [(slice(0, DH), slice(0, 2 * DH)), (slice(DH, DH + ROPE), slice(2 * DH, 384))]
                return [(src[:, :, :, a_], *(x[:, :, b_].rearrange("p k (h n) -> p k h n", h=2) for x in (hi, lo)))
                        for a_, b_ in cut]
            n = CC * 256 if kind == "ukv" else UNIT
            return [tuple(x[:, u0 % SLOTS, 0:n] for x in (raw, w_hi, w_lo))]

        def pair_kind(j):
            return {8: "uq", 9: "ukv", 10: "ukv"}.get(j, "full")

        kt = {name: a[name].rearrange("(k p) n -> p k n", p=P) for name in
              ("ffn1_w_gate", "ffn1_w_up", "ffn1_w_down", "ffn2_w_gate", "ffn2_w_up",
               "ffn2_w_down", "w_in", "mla_w_uq", "mla_w_uk", "mla_w_uv", "w_out")}
        FILL = 32

        block = ctx.enter_context(nc.Block())

        @block.sync
        def _(sp):
            def load(u, u0, halves):
                if not (isinstance(u, int) and u < SLOTS):
                    sp.wait_ge(lo_ready, u - SLOTS + 1)
                for d, s in halves:
                    sp.dma_start(d, s).then_inc(raw_full[u0 % SLOTS], 16)

            def gate_up(u, u0, w, col, kh):
                v = slot(raw, u0, k=8)
                load(u, u0, [(v[:, 4 * i:4 * i + 4, :],
                              kt[w][:, 8 * kh + 4 * i:8 * kh + 4 * i + 4, bass.ds(col, 256)])
                             for i in range(2)])

            def down(u, u0, w, k0, k1, q):
                v = slot(raw, u0, k=4)
                load(u, u0, [(v[:, 2 * i:2 * i + 2, :], kt[w][:, bass.ds(k, 2), q * 512:q * 512 + 512])
                             for i, k in enumerate((k0, k1))])

            def ffn_loads(f, between=None):
                g, up, dn = (f"ffn{f + 1}_w_{x}" for x in ("gate", "up", "down"))
                U = U_FFN[f]

                def half(u, u0, col, between=None):
                    for j, (w, kh) in enumerate(((g, 0), (g, 1), (up, 0), (up, 1))):
                        gate_up(u + j, u0 + j, w, col, kh)
                        if between is not None and j < 2:
                            between(j)

                half(U, U, 0, between)
                half(U + 4, U + 4, 256)
                with sp.Fori(0, SEGS - 1) as i:
                    u0 = U + 8
                    u = sp.snap(i * 12 + u0)
                    col0 = sp.snap(i * SEG + SEG)
                    col1 = sp.snap(i * SEG + SEG + 256)
                    k0 = sp.snap(i * 4)
                    k1 = sp.snap(i * 4 + 2)
                    half(u, u0, col0)
                    for q in range(4):
                        down(u + 4 + q, u0 + 4 + q, dn, k0, k1, q)
                    half(u + 8, u0 + 8, col1)
                for q in range(4):
                    u = U + FFN_UNITS - 4 + q
                    down(u, u, dn, 4 * SEGS - 4, 4 * SEGS - 2, q)

            def pair_loads(u, u0, c256, c384, p2):
                for b, c in enumerate((C_RK, C_RQ, C_RV, C_RG)):
                    for kh in range(2):
                        gate_up(u + 2 * b + kh, u0 + 2 * b + kh, "w_in", c256[c], kh)
                v = slot(raw, u0 + 8, k=QC, n=QC * 384)
                load(u + 8, u0 + 8, [(v[:, 2 * i:2 * i + 2, :],
                                      kt["mla_w_uq"][:, 2 * i:2 * i + 2, bass.ds(c384, 384)])
                                     for i in range(2)])
                for j, w in enumerate(("mla_w_uk", "mla_w_uv")):
                    v = slot(raw, u0 + 9 + j, k=CC, n=CC * 256)
                    load(u + 9 + j, u0 + 9 + j, [(v[:, i:i + 1, :],
                                                  kt[w][:, i:i + 1, bass.ds(c256[0], 256)])
                                                 for i in range(2)])
                if not isinstance(p2, int):
                    sp.wait_ge(ret_masked, p2)

            sp.dma_start(meta_sb, a["meta_tokens"]).then_inc(x_in[0], 16)
            def x_loads(pieces):
                for i in pieces:
                    cs = slice(i * 512, (i + 1) * 512)
                    sp.dma_start(x_sb[:, :, cs], a["x"].rearrange("(t p) d -> p t d", p=P)[:, :, cs]).then_inc(x_in[i], 16)

            x_loads((0,))
            ffn_loads(0, between=lambda j: x_loads(((1, 2), (3,))[j]))
            for kh in range(2):
                gate_up(U_PRE + kh, U_PRE + kh, "w_in", C_CKV, kh)
            u = U_PRE + 2
            v = slot(raw, u, k=KC, n=KC * ROPE)
            load(u, u, [(v[:, 8 * i:8 * i + 8, :], kt["w_in"][:, 8 * i:8 * i + 8, C_KR:C_KR + ROPE])
                        for i in range(2)])
            for b in range(2):
                for kh in range(2):
                    u = U_PRE + 3 + 2 * b + kh
                    gate_up(u, u, "w_in", C_CQ + 256 * b, kh)
            sp.wait_ge(h_ready, 2 * KC)
            sp.dma_start(spill, hT[:, :]).then_inc(spilled, 16)

            def decay_load(src_p):
                sp.dma_start(decay, a["decay"][src_p]).then_inc(decay_in, 16)
                sp.dma_start(decay_meta[0:META], a["decay_meta"][src_p]).then_inc(decay_in, 16)

            cols = {c: c for c in (0, C_RK, C_RV, C_RG)}
            pair_loads(U_MIX, U_MIX, cols, 0, 0)
            sp.wait_ge(lat_normed, 2)
            decay_load(0)
            with sp.Fori(0, PAIRS - 1) as i:
                u0 = U_MIX + PAIR_UNITS
                u = sp.snap(i * 15 + u0)
                cols = {c: sp.snap(i * 256 + (256 + c)) for c in (0, C_RK, C_RV, C_RG)}
                c384 = sp.snap(i * 384 + 384)
                p2 = sp.snap(i * 2 + 2)
                k0 = sp.snap(i * 2)
                k1 = sp.snap(i * 2 + HEADS)
                d0 = sp.snap(i * (P * 6 * P) + P * 6 * P)
                dm0 = sp.snap(i * (META * 2 * REAL) + META * 2 * REAL)
                pair_loads(u, u0, cols, c384, p2)
                dsrc = a["decay"].rearrange("a p h n -> (a p h n)")[bass.ds(d0, P * 6 * P)]
                sp.dma_start(decay, dsrc.rearrange("(p h n) -> p h n", p=P, h=2)).then_inc(decay_in, 16)
                msrc = a["decay_meta"].rearrange("a p h n -> (a p h n)")[bass.ds(dm0, META * 2 * REAL)]
                sp.dma_start(decay_meta[0:META], msrc.rearrange("(p h n) -> p h n", p=META, h=2)).then_inc(decay_in, 16)
                for q in range(4):
                    down(u + 11 + q, u0 + 11 + q, "w_out", k0, k1, q)
            for q in range(4):
                u = U_FFN[1] - 4 + q
                down(u, u, "w_out", HEADS - 2, 2 * HEADS - 2, q)
            sp.wait_ge(spilled, 16)
            sp.wait_ge(mix_ready, 4 * PAIRS)
            sp.dma_start(hT[:, :], spill).then_inc(reloaded, 16)
            ffn_loads(1)
            for b in range(4):
                for t in range(2):
                    sp.wait_ge(out_ready, 2 * b + t + 1)
                    sp.dma_start(out[t * P:(t + 1) * P, b * 512:(b + 1) * 512],
                                 raw[:, t, b * 512:(b + 1) * 512]).then_inc(stored, 16)
            sp.wait_ge(stored, 16 * 8)

        @block.gpsimd
        def _(pool):
            steps = [0]
            nc.gpsimd.memset(ones[:, :], 1.0).then_inc(ones_set, 1)
            nc.gpsimd.memset(eps, EPS).then_inc(ones_set, 1)
            nc.gpsimd.memset(ckv_hi[:, :, TOK:].bitcast(F32), 0.0).then_inc(pad_zero, 1)
            nc.gpsimd.memset(ckv_lo[:, :, TOK:].bitcast(F32), 0.0).then_inc(pad_zero, 1)

            def accumulate(src, c, last):
                if c == 0:
                    return
                n = src(c).shape[-1]
                so_far = src(0) if c == 1 else ssq[:, 0:n]
                if c > 1:
                    pool.wait_ge(pool_step, steps[0])
                add = nc.gpsimd.tensor_tensor(ssq[:, 0:n], so_far, src(c), ALU.add)
                if c == last:
                    add.then_inc(ssq_ready, 1)
                else:
                    add.then_inc(pool_step, 1)
                    steps[0] += 1

            def sum_output(norm, sq0, n):
                pool.wait_ge(ms_done, norm)
                for c in range(12):
                    pool.wait_ge(squared, sq0 + c + 1)
                    accumulate(lambda k: tmp[:, k % 4, 0:n], c, 11)

            def sum_residual(norm, sq0, n):
                if norm:
                    pool.wait_ge(ms_done, norm)
                for c in range(KC):
                    pool.wait_ge(squared, sq0 + c + 1)
                    accumulate(lambda k: acc_t[:, k, 0:n], c, KC - 1)

            def add_to_residual(stage, n):
                for c in range(KC):
                    pool.wait_ge(post_scaled, KC * stage + c + 1)
                    nc.gpsimd.tensor_tensor(h[:, c, 0:n], h[:, c, 0:n], acc_t[:, c, 0:n], ALU.add).then_inc(h_ready, 1)

            sum_residual(0, 0, TOK)
            sum_output(1, 16, TOK)
            add_to_residual(0, TOK)
            sum_residual(2, 32, TOK)
            sum_output(3, 48, REAL)
            pool.wait_ge(reloaded, 16)
            add_to_residual(1, REAL)
            sum_residual(4, 64, REAL)
            sum_output(5, 80, REAL)
            add_to_residual(2, REAL)

        @block.scalar
        def _(act_e):
            def copy(o, i):
                return nc.scalar.activation(o, i, ACT.Copy)

            def split(u, u0, kind="full", filled=0):
                act_e.wait_ge(raw_full[u0 % SLOTS], filled + FILL * (u0 // SLOTS + 1))
                if not (isinstance(u, int) and u < SLOTS):
                    act_e.wait_ge(unit_used, u - SLOTS + 1)
                for src, hi, _ in split_parts(u0, kind):
                    last = copy(hi, src)
                last.then_inc(hi_ready, 1)

            def std(norm, n):
                act_e.wait_ge(ms_done, norm + 1)
                dst = rstd if norm % 2 else r_pre
                nc.scalar.activation(dst[:, 0:n], bank[7][:, 0:n], ACT.Sqrt, bias=eps, scale=1.0 / DM).then_inc(std_done, 1)

            def operand_hi(stage, c, n):
                act_e.wait_ge(h_ready, stage * KC + c + 1)
                g = G_PRE[stage] + c
                nc.scalar.activation(hn_hi[:, c, 0:n], h[:, c, 0:n], ACT.Copy, scale=gains[:, g:g + 1]).then_inc(hn_hi_done, 1)

            def square_residual(c, n):
                nc.scalar.activation(acc_t[:, c, 0:n], h[:, c, 0:n], ACT.Square).then_inc(squared, 1)

            def residual_operand(stage, n):
                for c in range(KC):
                    operand_hi(stage, c, n)
                    square_residual(c, n)

            def square_output(stage, q, n):
                for i in range(4):
                    c = 4 * q + i
                    if q < 3 or i == 3:
                        act_e.wait_ge(acc_ready, A_DONE[stage] + q + 1)
                    else:
                        act_e.wait_ge(tile_added, 3 * stage + i + 1)
                    if c == KC - 1:
                        act_e.wait_ge(ssq_ready, 2 * stage + 2)
                    elif q > 0:
                        act_e.wait_ge(pool_step, POOL_OUT[stage] + max(c - 4, 1))
                    nc.scalar.activation(tmp[:, i, 0:n], acc_t[:, c, 0:n], ACT.Square).then_inc(squared, 1)

            def ffn(f, n, tail):
                U = U_FFN[f]

                def silu(ch):
                    for c in range(2):
                        act_e.wait_ge(gate_scaled, ch + c + 1)
                        nc.scalar.activation(sil[:, c, 0:n], sil[:, c, 0:n], ACT.Silu).then_inc(silu_done, 1)

                def act_hi(ch, half):
                    for c in range(2):
                        act_e.wait_ge(act_done, ch + c + 1)
                        copy(dn_hi[:, 2 * half + c, 0:n], act[:, c, 0:n]).then_inc(act_hi_done, 1)

                ch = 44 * f
                for j in range(2 - f, 8):
                    split(U + j + 2, U + j + 2)
                    if j == 5:
                        std(4 * f, n)
                        silu(ch)
                    if j == 6:
                        act_hi(ch, 0)
                        silu(ch + 2)
                    if j == 7:
                        act_hi(ch + 2, 1)
                with act_e.Fori(0, SEGS - 1) as i:
                    u0 = U + 8
                    u = act_e.snap(i * 12 + u0)
                    c0 = act_e.snap(i * 4 + (ch + 4))
                    filled = act_e.snap(i * (12 // SLOTS * FILL))
                    for j in range(12):
                        split(u + (j + 2), u0 + j + 2, filled=filled)
                        if j == 1:
                            silu(c0)
                        if j == 7:
                            act_e.wait_ge(unit_used, u + 8)
                            act_hi(c0, 0)
                        if j == 9:
                            silu(c0 + 2)
                        if j == 11:
                            act_hi(c0 + 2, 1)
                last_units(2 * f, U + FFN_UNITS - 4, tail)

            def last_units(stage, u, tail):
                n = (TOK, REAL, REAL)[stage]
                for q in range(4):
                    tail(u + q)
                    if q > 0:
                        square_output(stage, q - 1, n)
                square_output(stage, 3, n)
                if stage < 2:
                    tail(u + 4)

            def swap_halves(index, src, n, width):
                if index > 0:
                    act_e.wait_ge(rotated, index)
                last = None
                for b in range(P // width):
                    o = b ^ 1
                    last = copy(swap[b * width:(b + 1) * width, 0:n], src[o * width:(o + 1) * width, 0:n])
                last.then_inc(swapped, 1)

            def pair_projections(j, u, r0, h0, first):
                if j in (1, 3, 8, 9):
                    act_e.wait_ge(unit_used, u + j + 1)
                if j == 1:
                    for c in range(2):
                        swap_halves(r0 + c, bank[c], TOK, 64)
                if j == 3:
                    for c in range(2):
                        swap_halves(r0 + 2 + c, bank[2 + c], REAL, 64)
                if j == 7:
                    for c in range(2):
                        act_e.wait_ge(rg_scaled, h0 + c + 1)
                        nc.scalar.activation(ret_gate[:, c, :], ret_gate[:, c, :], ACT.Silu).then_inc(gate_ready, 1)
                if j == 8:
                    for c in range(2):
                        copy(mla_q[:, c, :], bank[c][:, 0:REAL]).then_inc(mq_ready, 1)
                    swap_halves(r0 + 4, bank[2], REAL, 32)
                if j == 9:
                    for c in range(2):
                        copy(mla_k[:, c, :], bank[(3, 0)[c]][:, 0:TOK]).then_inc(mk_ready, 1)
                    for c in range(2):
                        act_e.wait_ge(v_tr, h0 + c + 1)
                        b = bank[(5, 7)[c]]
                        copy(ret_v[:, c, 0:REAL], b[:, 0:REAL])
                        copy(ret_v[0:META, c, REAL:], b[0:META, REAL:3 * P]).then_inc(v_ready, 1)

            def attention(j, h0, m0):
                if j == 1:
                    for c in range(2):
                        act_e.wait_ge(ret_out, h0 + c + 1)
                        copy(ret_o[:, c, :], bank[4 + 2 * c][:, 0:REAL])
                        nc.scalar.activation(ret_sq[:, c, :], bank[4 + 2 * c][:, 0:REAL], ACT.Square).then_inc(ret_sq_done, 1)
                if j == 2:
                    exps(h0)
                    for c in range(2):
                        act_e.wait_ge(ret_ms, h0 + c + 1)
                        nc.scalar.activation(ret_rs[:, c, :], bank[4 + 2 * c][:, 0:REAL], ACT.Sqrt, bias=eps, scale=1.0 / DH).then_inc(ret_std, 1)
                if j == 4:
                    probs_copy(h0)
                    mix_hi_ret(h0, m0, 0)
                if j == 5:
                    exps(h0 + 1)
                if j == 6:
                    mix_hi_ret(h0, m0, 1)
                    mix_hi_mla(h0, 0)
                if j == 7:
                    probs_copy(h0 + 1)
                if j == 10:
                    mix_hi_mla(h0 + 1, 1)

            def exps(hd):
                for t in range(2):
                    act_e.wait_ge(neg_max, hd * 2 + (t + 1))
                    nc.scalar.activation(probs[:, t, :], probs[:, t, :], ACT.Exp, bias=small[:, 4 + t:5 + t],
                                         accum_out=small[:, 6 + t:7 + t]).then_inc(exp_done, 1)

            def probs_copy(hd):
                act_e.wait_ge(probs_tr, hd + 1)
                copy(sc[:, 0, 0:3 * P], bank[5][:, 0:3 * P])
                copy(sc[0:META, 0, 3 * P:640], bank[7][0:META, 0:REAL]).then_inc(probsT_ready, 1)

            def mix_hi_ret(h0, m0, c):
                act_e.wait_ge(ret_f, h0 + c + 1)
                copy(dn_hi[:, c, 0:REAL], ret_o[:, c, :]).then_inc(mix_hi_done, 1)

            def mix_hi_mla(hd, c):
                act_e.wait_ge(mla_out, hd + 1)
                copy(dn_hi[:, 2 + c, 0:REAL], bank[4 + 2 * c][:, 0:REAL]).then_inc(mix_hi_done, 1)

            act_e.dma_start(ident[:, :], a["ident"]).then_inc(consts_in, 16)
            for name, at0, rows in (("ffn1_pre_norm", G_PRE[0], KC), ("ffn1_post_norm", G_POST[0], KC),
                                    ("mix_pre_norm", G_PRE[1], KC), ("mix_post_norm", G_POST[1], KC),
                                    ("ffn2_pre_norm", G_PRE[2], KC), ("ffn2_post_norm", G_POST[2], KC),
                                    ("ret_group_norm", G_RET, HEADS), ("mla_q_norm", G_Q, QC),
                                    ("mla_kv_norm", G_KV, CC)):
                act_e.dma_start(gain_rows[at0:at0 + rows, :], a[name].rearrange("o (c p) -> (o c) p", p=P)
                                ).then_inc(consts_in if at0 == 0 else gains_in, 16)
            act_e.dma_start(rope_ret[:, :, :], a["rope_ret"].rearrange("t p n -> p t n")).then_inc(tables_in, 16)
            act_e.dma_start(rope_mla[:, :, :], a["rope_mla"].rearrange("t p n -> p t n")).then_inc(tables_in, 16)
            act_e.dma_start(mask[:, :, :], a["mask"].rearrange("t p n -> p t n")).then_inc(tables_in, 16)
            for c in range(KC):
                if c in UNIT_AT_CHUNK:
                    split(UNIT_AT_CHUNK.index(c), UNIT_AT_CHUNK.index(c))
                if c == 0:
                    act_e.wait_ge(gains_ready, 1)
                operand_hi(0, c, TOK)
            split(3, 3)
            act_e.wait_ge(x_tr, KC)
            act_e.wait_ge(ones_set, 2)
            for c in range(KC):
                square_residual(c, TOK)

            def tail1(u):
                split(u + 2, u + 2, kind="kr" if u + 2 == U_PRE + 2 else "full")

            ffn(0, TOK, tail1)
            std(1, TOK)
            residual_operand(1, TOK)

            def latent_square(before, tiles, n, f):
                for c in range(tiles):
                    act_e.wait_ge(lat_read, before + c + 1)
                    nc.scalar.activation(lat_sq[:, c, 0:n], f[:, c, 0:n], ACT.Square).then_inc(lat_sqd, 1)

            def latent_std(index, rank, n):
                act_e.wait_ge(lat_ms, index + 1)
                nc.scalar.activation(rstd[:, 0:n], bank[7][:, 0:n], ACT.Sqrt, bias=eps, scale=1.0 / rank).then_inc(lat_std, 1)

            def latent_hi(before, tiles, n, f, dst):
                for c in range(tiles):
                    act_e.wait_ge(lat_normed, before + c + 1)
                    copy(dst[:, c, 0:n], f[:, c, 0:n]).then_inc(lat_hi_done, 1)

            for j in range(1, PRE_UNITS):
                u = U_PRE + j
                split(u + 2, u + 2)
                if j == 2:
                    act_e.wait_ge(unit_used, u + 1)
                    swap_halves(0, bank[2], TOK, 32)
                if j == 5:
                    std(2, TOK)
                    latent_square(0, CC, TOK, ckv_f)
            act_e.wait_ge(spilled, 16)
            for j in range(PAIR_UNITS):
                u = U_MIX + j
                split(u + 2, u + 2, kind=pair_kind(j + 2))
                if j == 1:
                    latent_std(0, KV_RANK, TOK)
                    latent_square(CC, QC, REAL, cq_f)
                    latent_hi(0, CC, TOK, ckv_f, ckv_hi)
                if j == 3:
                    latent_std(1, Q_RANK, REAL)
                    latent_hi(CC, QC, REAL, cq_f, cq_hi)
                pair_projections(j, U_MIX, 1, 0, True)
            with act_e.Fori(0, PAIRS - 1) as i:
                u0 = U_MIX + PAIR_UNITS
                u = act_e.snap(i * 15 + u0)
                h0 = act_e.snap(i * 2)
                h1 = act_e.snap(i * 2 + 2)
                r0 = act_e.snap(i * 5 + 6)
                filled = act_e.snap(i * (15 // SLOTS * FILL))
                for j in range(15):
                    if j == 10:
                        attention(j, h0, 0)
                    split(u + (j + 2), u0 + j + 2, kind=pair_kind(j + 2), filled=filled)
                    if j != 10:
                        attention(j, h0, 0)
                    if j < PAIR_UNITS:
                        pair_projections(j, u, r0, h1, False)
            for j in range(1, PAIR_UNITS):
                attention(j, HEADS - 2, 0)
            last_units(1, U_FFN[1] - 4, lambda u: split(u + 2, u + 2))
            std(3, REAL)
            residual_operand(2, REAL)
            last = U_ALL - 1

            def tail2(u):
                if u + 2 <= last:
                    split(u + 2, u + 2)

            ffn(1, REAL, tail2)
            std(5, REAL)
            for b in range(4):
                for t in range(2):
                    act_e.wait_ge(out_tr, 2 * b + t + 1)
                    copy(raw[:, t, b * 512:(b + 1) * 512], bank[4 * t + b][:, :]).then_inc(out_ready, 1)

        @block.tensor
        def _(pe):
            mm = nc.tensor.matmul

            def mm3(o, w, wl, x, xl, first, last):
                mm(o, w, x, start=first, stop=False)
                mm(o, w, xl, start=False, stop=False)
                return mm(o, wl, x, start=False, stop=last)

            def first_unit(u, u0, kh, banks, n, fine, after=None):
                pe.wait_ge(lo_ready, u + 1)
                wh, wl = slot(w_hi, u0, k=8), slot(w_lo, u0, k=8)
                last = None
                for k in range(8):
                    kk = 8 * kh + k
                    pe.wait_ge(hn_ready, fine + kk + 1)
                    for c in range(2):
                        cs = slice(c * P, (c + 1) * P)
                        last = mm3(bank[banks[c]][:, 0:n], wh[:, k, cs], wl[:, k, cs],
                                   hn_hi[:, kk, 0:n], hn_lo[:, kk, 0:n], kk == 0, kk == KC - 1)
                    if k == 7:
                        last.then_inc(unit_used, 1)
                    if after is not None:
                        after(kk)

            def proj_unit(u, u0, kh, banks, n):
                pe.wait_ge(lo_ready, u + 1)
                wh, wl = slot(w_hi, u0, k=8), slot(w_lo, u0, k=8)
                last = None
                for c in range(2):
                    for k in range(8):
                        kk = 8 * kh + k
                        cs = slice(c * P, (c + 1) * P)
                        last = mm3(bank[banks[c]][:, 0:n], wh[:, k, cs], wl[:, k, cs],
                                   hn_hi[:, kk, 0:n], hn_lo[:, kk, 0:n], kk == 0, kk == KC - 1)
                last.then_inc(unit_used, 1)

            def down_unit(u, u0, q, n, tiles=False, second=None):
                pe.wait_ge(lo_ready, u + 1)
                wh, wl = slot(w_hi, u0, k=4), slot(w_lo, u0, k=4)
                last = None
                parts = [(i, range(4)) for i in range(4)]
                if second:
                    parts = [(i, ks) for ks in ((0, 1), (2, 3)) for i in (0, 1, 3, 2)]
                waited = not second
                for i, ks in parts:
                    o = bank[(4 if q % 2 == 0 else 0) + i][:, 0:n]
                    if not waited and (ks[0] == 2 or i == 2):
                        pe.wait_ge(*second)
                        waited = True
                    for k in ks:
                        cs = slice(i * P, (i + 1) * P)
                        last = mm3(o, wh[:, k, cs], wl[:, k, cs], dn_hi[:, k, 0:n], dn_lo[:, k, 0:n],
                                   k == 0, k == 3)
                    if tiles and i < 3:
                        last.then_inc(tile_done, 1)
                last.then_inc(unit_used, 1)

            def feature_sum(norm, n):
                pe.wait_ge(ssq_ready, norm + 1)
                last = mm(bank[7][:, 0:n], ones[:, :], ssq[:, 0:n], start=True, stop=norm % 2 == 0)
                if norm % 2:
                    for i in range(4):
                        pe.wait_ge(squared, KC * norm + 12 + i + 1)
                        last = mm(bank[7][:, 0:n], ones[:, :], tmp[:, i, 0:n], start=False, stop=i == 3)
                last.then_inc(ms_done, 1)

            def ffn(f, n, after=None):
                U = U_FFN[f]
                ch = 44 * f
                A = A_FFN[f] + 4

                for j in range(8):
                    banks = ((0, 1), (2, 3), (4, 5), (6, 7))[j // 2]
                    if j < 2:
                        first_unit(U + j, U + j, j, banks, n, 2 * KC * f, after if f == 0 else None)
                        continue
                    if j == 2 and f == 0:
                        pe.wait_ge(gains_in, 16 * 8)
                        pe.wait_ge(h_ready, KC)
                        nc.tensor.transpose(bank[7][:, 0:GAINS], gain_rows, ident[0:GAINS, 0:GAINS]).then_inc(gains_tr, 1)
                    if j == 5:
                        if f == 0:
                            pe.wait_ge(gains_ready, 2)
                        feature_sum(4 * f, n)
                    if j == 6:
                        pe.wait_ge(std_done, 4 * f + 1)
                    proj_unit(U + j, U + j, j % 2, banks, n)
                with pe.Fori(0, SEGS - 1) as i:
                    u0 = U + 8
                    u = pe.snap(i * 12 + u0)
                    c0 = pe.snap(i * 4 + (ch + 4))
                    a0 = pe.snap(i * 4 + A)
                    for j in range(4):
                        if j == 0:
                            pe.wait_ge(gate_scaled, c0 - 2)
                            pe.wait_ge(acc_ready, a0)
                        if j == 2:
                            pe.wait_ge(act_done, c0 - 2)
                        proj_unit(u + j, u0 + j, j % 2, ((0, 1), (2, 3))[j // 2], n)
                    for q in range(4):
                        if q == 0:
                            pe.wait_ge(act_ready, c0 - 2)
                            pe.wait_ge(gate_scaled, c0)
                            pe.wait_ge(act_done, c0)
                        if q == 1:
                            pe.wait_ge(gate_scaled, c0 + 2)
                            pe.wait_ge(act_done, c0 + 2)
                        if q > 1:
                            pe.wait_ge(acc_ready, a0 + (q - 1))
                        down_unit(u + (4 + q), u0 + 4 + q, q, n,
                                  second=None if q else (act_ready, c0))
                    for j in range(4):
                        if j == 0:
                            pe.wait_ge(acc_ready, a0 + 3)
                        proj_unit(u + (8 + j), u0 + 8 + j, j % 2, ((4, 5), (6, 7))[j // 2], n)
                a0 = A + 4 * (SEGS - 1)
                pe.wait_ge(act_ready, ch + 42)
                pe.wait_ge(gate_scaled, ch + 44)
                pe.wait_ge(act_done, ch + 44)
                for q in range(4):
                    pe.wait_ge(acc_ready, a0 + max(q - 1, 0))
                    u = U + FFN_UNITS - 4 + q
                    down_unit(u, u, q, n, tiles=q == 3, second=None if q else (act_ready, ch + 44))

            def pair_projections(j, u, u0, r0, h0, p0):
                if j < 8:
                    b = ((0, 1), (2, 3))[(j // 2) % 2]
                    n = (TOK, REAL, TOK, REAL)[j // 2]
                    if j == 4:
                        pe.wait_ge(rotated, r0 + 2)
                    if j == 6:
                        pe.wait_ge(rotated, r0 + 4)
                    proj_unit(u + j, u0 + j, j % 2, b, n)
                if j == 8:
                    pe.wait_ge(lo_ready, u + 9)
                    pe.wait_ge(vT_ready, h0 + 2)
                    pe.wait_ge(lat_ready, CC + QC)
                    wh, wl = (slot(r, u0 + 8, k=QC, n=QC * 384) for r in (w_hi, w_lo))
                    last = None
                    for c in range(3):
                        if c == 2:
                            pe.wait_ge(rg_scaled, h0 + 2)
                        for k in range(QC):
                            cs = slice(c * P, (c + 1) * P)
                            last = mm3(bank[c][:, 0:REAL], wh[:, k, cs], wl[:, k, cs], cq_hi[:, k, :], cq_lo[:, k, :],
                                       k == 0, k == QC - 1)
                    last.then_inc(unit_used, 1)
                    if not isinstance(h0, int):
                        pe.wait_ge(probsT_ready, h0)
                    for c in range(2):
                        b = bank[(5, 7)[c]]
                        for r in range(3):
                            m = META if r == 2 else P
                            last = nc.tensor.transpose(b[0:m, r * P:(r + 1) * P], ret_vT[:, c, r * P:r * P + m], ident[:, :])
                        last.then_inc(v_tr, 1)
                if j == 9:
                    pe.wait_ge(lo_ready, u + 10)
                    wh, wl = (slot(r, u0 + 9, k=CC, n=CC * 256) for r in (w_hi, w_lo))
                    last = None
                    for c in range(2):
                        if c == 1:
                            pe.wait_ge(mq_ready, h0 + 1)
                        for k in range(CC):
                            cs = slice(c * P, (c + 1) * P)
                            last = mm3(bank[(3, 0)[c]][:, 0:TOK], wh[:, k, cs], wl[:, k, cs],
                                       ckv_hi[:, k, 0:TOK], ckv_lo[:, k, 0:TOK], k == 0, k == CC - 1)
                    last.then_inc(unit_used, 1)
                if j == 10:
                    pe.wait_ge(lo_ready, u + 11)
                    wh, wl = (slot(r, u0 + 10, k=CC, n=CC * 256) for r in (w_hi, w_lo))
                    last = None
                    for r in range(3):
                        if r == 0:
                            pe.wait_ge(mq_ready, h0 + 2)
                        if r == 1:
                            pe.wait_ge(rotated, r0 + 5)
                        if r == 2:
                            pe.wait_ge(mk_ready, h0 + 1)
                        o = bank[1 + r][:, 0:REAL]
                        ts = slice(r * P, (r + 1) * P)
                        for k in range(CC):
                            last = mm3(o, ckv_hi[:, k, ts], ckv_lo[:, k, ts], wh[:, k, :], wl[:, k, :],
                                       k == 0, k == CC - 1)
                    last.then_inc(unit_used, 1)

            def values(o, v_real, v_meta, s):
                mm(o[:, 0:REAL], v_real[0], s[:, 0:REAL], start=True, stop=False)
                mm(o[:, P:REAL], v_real[1], s[:, REAL:3 * P], start=False, stop=False)
                return mm(o[:, 0:REAL], v_meta, s[0:META, 3 * P:640], start=False, stop=True)

            def attention(g, h0, r0, p1):
                if g == 0:
                    pe.wait_ge(rotated, r0 + 4)
                    pe.wait_ge(v_ready, h0 + 2)
                    for c in range(2):
                        s, m = bank[4 + 2 * c], bank[5 + 2 * c]
                        k, q = ret_k[:, c, :], ret_q[:, c, :]
                        mm(s[:, 0:REAL], k[:, 0:P], q, start=True, stop=True)
                        mm(s[:, REAL:3 * P], k[:, P:REAL], q[:, P:REAL], start=False, stop=True, skip_group_check=True)
                        mm(m[0:META, 0:REAL], k[:, REAL:TOK], q, start=True, stop=True).then_inc(ret_scores, 1)
                if g == 1:
                    for c in range(2):
                        pe.wait_ge(ret_masked, h0 + c + 1)
                        v = ret_v[:, c, :]
                        values(bank[4 + 2 * c], (v[:, 0:P], v[:, P:REAL]), v[0:META, REAL:3 * P],
                               sc[:, c, :]).then_inc(ret_out, 1)
                if g == 2:
                    for c in range(2):
                        pe.wait_ge(ret_sq_done, h0 + c + 1)
                        mm(bank[4 + 2 * c][:, 0:REAL], ones[:, :], ret_sq[:, c, :], start=True, stop=True).then_inc(ret_ms, 1)
                    mla_s(h0, 0, r0, p1)
                if g == 3:
                    mla_t(h0)
                if g == 4:
                    mla_o(h0, 0)
                    mla_s(h0, 1, r0, p1)
                if g == 5:
                    mla_t(h0 + 1)
                if g == 6:
                    mla_o(h0, 1)

            def mla_s(h0, c, r0, p1):
                pe.wait_ge(mk_ready, h0 + 2)
                pe.wait_ge(rotated, r0 + 5)
                rows = slice(64 * c, 64 * c + 64)
                for t in range(2):
                    ts = slice(t * P, (t + 1) * P)
                    b = bank[(5, 7)[t]][:, 0:TOK]
                    mm(b, mla_q[:, c, ts], mla_k[:, c, :], start=True, stop=False)
                    mm(b, mla_qr[rows, ts], mla_kr[rows, :], start=False, stop=True).then_inc(mla_scores, 1)

            def mla_t(hd):
                pe.wait_ge(probs_ready, hd * 2 + 2)
                tr = nc.tensor.transpose
                tr(bank[5][:, 0:P], probs[:, 0, 0:P], ident[:, :])
                tr(bank[5][:, P:REAL], probs[:, 1, 0:P], ident[:, :])
                tr(bank[5][:, REAL:3 * P], probs[:, 1, P:REAL], ident[:, :])
                tr(bank[7][0:META, 0:P], probs[:, 0, REAL:TOK], ident[:, :])
                tr(bank[7][0:META, P:REAL], probs[:, 1, REAL:TOK], ident[:, :]).then_inc(probs_tr, 1)

            def mla_o(h0, c):
                pe.wait_ge(probsT_ready, h0 + c + 1)
                pe.wait_ge(ret_std, h0 + c + 1)
                cs = slice(c * P, (c + 1) * P)
                values(bank[4 + 2 * c], (mla_v[:, 0, cs], mla_v[:, 1, cs]), mla_v[0:META, 2, cs],
                       sc[:, 0, :]).then_inc(mla_out, 1)

            pe.wait_ge(consts_in, 32)
            nc.tensor.transpose(bank[0][:, 0:KC], gain_rows[0:KC, :], ident[0:KC, 0:KC]).then_inc(gains_tr, 1)

            def transpose_x(c):
                b = bank[2 + c % X_AHEAD]
                if c % 4 == 0:
                    pe.wait_ge(x_in[c // 4], 32 if c == 0 else 16)
                if c >= X_AHEAD:
                    pe.wait_ge(h_ready, c - X_AHEAD + 1)
                cs = slice(c * P, (c + 1) * P)
                for t in range(2):
                    nc.tensor.transpose(b[:, t * P:(t + 1) * P], x_sb[:, t, cs], ident[:, :])
                nc.tensor.transpose(b[:, REAL:TOK], meta_sb[:, cs], ident[0:META, 0:META]).then_inc(x_tr, 1)

            for c in range(X_AHEAD):
                transpose_x(c)
            pe.wait_ge(gains_ready, 1)
            pe.wait_ge(ones_set, 2)
            ffn(0, TOK, after=lambda kk: transpose_x(kk + X_AHEAD) if kk + X_AHEAD < KC else None)
            feature_sum(1, TOK)

            for j in range(2):
                first_unit(U_PRE + j, U_PRE + j, j, (0, 1), TOK, KC)
            u = U_PRE + 2
            pe.wait_ge(lo_ready, u + 1)
            wh, wl = slot(w_hi, u, k=KC), slot(w_lo, u, k=KC)
            for k in range(KC):
                last = mm3(bank[2][:, 0:TOK], wh[:, k, :], wl[:, k, :], hn_hi[:, k, :], hn_lo[:, k, :],
                           k == 0, k == KC - 1)
            last.then_inc(unit_used, 1)
            for j in range(4):
                if j == 2:
                    feature_sum(2, TOK)
                proj_unit(U_PRE + 3 + j, U_PRE + 3 + j, j % 2, ((3, 4), (5, 6))[j // 2], REAL)

            def latent_sum(before, tiles, n):
                for c in range(tiles):
                    pe.wait_ge(lat_sqd, before + c + 1)
                    last = mm(bank[7][:, 0:n], ones[:, :], lat_sq[:, c, 0:n], start=(c == 0), stop=(c == tiles - 1))
                last.then_inc(lat_ms, 1)

            for j in range(PAIR_UNITS):
                if j == 0:
                    pe.wait_ge(lat_read, CC)
                if j == 1:
                    pe.wait_ge(std_done, 3)
                    latent_sum(0, CC, TOK)
                if j == 2:
                    pe.wait_ge(rotated, 1)
                    pe.wait_ge(lat_read, CC + 2)
                if j == 3:
                    pe.wait_ge(lat_std, 1)
                    latent_sum(CC, QC, REAL)
                pair_projections(j, U_MIX, U_MIX, 1, 0, 0)
            STAGE = {0: 1, 1: 2, 3: 3, 4: 4, 6: 5, 9: 6}
            with pe.Fori(0, PAIRS - 1) as i:
                u0 = U_MIX + PAIR_UNITS
                u = pe.snap(i * 15 + u0)
                h0 = pe.snap(i * 2)
                h1 = pe.snap(i * 2 + 2)
                r0 = pe.snap(i * 5 + 1)
                r1 = pe.snap(i * 5 + 6)
                p1 = pe.snap(i + 1)
                a0 = pe.snap(i * 4 + (A_MIX + 4))
                pe.wait_ge(acc_ready, a0 - 1)
                attention(0, h0, r0, p1)
                for j in range(PAIR_UNITS):
                    if j == 0:
                        pe.wait_ge(acc_ready, a0)
                        pe.wait_ge(mk_ready, h0 + 2)
                        pe.wait_ge(mv_ready, p1)
                    pair_projections(j, u, u0, r1, h1, p1)
                    if j in STAGE:
                        attention(STAGE[j], h0, r0, p1)
                for q in range(4):
                    if q == 0:
                        pe.wait_ge(mix_ready, h0 * 2 + 2)
                        pe.wait_ge(v_ready, h1 + 2)
                    if q == 1:
                        pe.wait_ge(mk_ready, h1 + 2)
                        pe.wait_ge(mv_ready, p1 + 1)
                    if q > 1:
                        pe.wait_ge(acc_ready, a0 + (q - 1))
                    down_unit(u + (11 + q), u0 + 11 + q, q, REAL,
                              second=None if q else (mix_ready, h0 * 2 + 4))
            a0 = A_MIX + 4 + 4 * (PAIRS - 1)
            pe.wait_ge(acc_ready, a0)
            pe.wait_ge(mv_ready, PAIRS)
            for g in range(7):
                attention(g, HEADS - 2, 1 + 5 * (PAIRS - 1), PAIRS)
            pe.wait_ge(mix_ready, 4 * PAIRS)
            for q in range(4):
                if q > 1:
                    pe.wait_ge(acc_ready, a0 + q - 1)
                u = U_FFN[1] - 4 + q
                down_unit(u, u, q, REAL, tiles=q == 3)
            feature_sum(3, REAL)
            ffn(1, REAL)
            feature_sum(5, REAL)
            pe.wait_ge(rstd_done, 6)
            for b in range(4):
                for i in range(4):
                    c = 4 * b + i
                    pe.wait_ge(h_ready, 3 * KC + c + 1)
                    for t in range(2):
                        tr = nc.tensor.transpose(bank[4 * t + b][:, i * P:(i + 1) * P], h[:, c, t * P:(t + 1) * P], ident[:, :])
                        if i == 3:
                            tr.then_inc(out_tr, 1)

        @block.vector
        def _(dve):
            tt, stt, ts = nc.vector.tensor_tensor, nc.vector.scalar_tensor_tensor, nc.vector.tensor_scalar

            class Own:
                n, turn, per = 0, None, 0

                def wait(self):
                    dve.wait_ge(dve_step, self.n if self.turn is None else self.turn * self.per + self.n)

                def step(self, ins):
                    ins.then_inc(dve_step, 1)
                    self.n += 1

            own = Own()

            def split(u, u0, kind="full"):
                dve.wait_ge(hi_ready, u + 1)
                for src, hi, lo in split_parts(u0, kind):
                    last = tt(lo, src, hi.bitcast(F32), ALU.subtract)
                last.then_inc(lo_ready, 1)

            def add_group(u, q, ready, n):
                dve.wait_ge(unit_used, u + 1)
                dve.wait_ge(acc_ready, ready)
                last = None
                for i in range(4):
                    c = 4 * q + i
                    b = bank[(4 if q % 2 == 0 else 0) + i][:, 0:n]
                    last = tt(acc_t[:, c, 0:n], acc_t[:, c, 0:n], b, ALU.add)
                last.then_inc(acc_ready, 1)

            def last_units(stage, u, tail):
                n = (TOK, REAL, REAL)[stage]
                for q in range(3):
                    tail(u + q)
                    add_group(u + q, q, A_DONE[stage] + q - 3, n)
                tail(u + 3)
                dve.wait_ge(acc_ready, A_DONE[stage])
                for i in range(4):
                    if i < 3:
                        dve.wait_ge(tile_done, 3 * stage + i + 1)
                    else:
                        dve.wait_ge(unit_used, u + 4)
                    t = acc_t[:, 12 + i, 0:n]
                    tt(t, t, bank[i][:, 0:n], ALU.add).then_inc(tile_added if i < 3 else acc_ready, 1)
                if stage < 2:
                    tail(u + 4)

            def invert(norm, t, n):
                dve.wait_ge(std_done, norm + 1)
                nc.vector.reciprocal(t[:, 0:n], t[:, 0:n]).then_inc(rstd_done, 1)
                dve.wait_ge(rstd_done, norm + 1)

            def operand_lo(stage, c, n):
                dve.wait_ge(hn_hi_done, stage * KC + c + 1)
                g = G_PRE[stage] + c
                stt(out=hn_lo[:, c, 0:n], in0=h[:, c, 0:n], scalar=gains[:, g:g + 1], in1=hn_hi[:, c, 0:n].bitcast(F32),
                    op0=ALU.mult, op1=ALU.subtract).then_inc(hn_ready, 1)

            def post_norm(stage, n):
                invert(2 * stage + 1, rstd, n)
                LAG = 3
                for c in range(KC + LAG):
                    if c < KC:
                        g = G_POST[stage] + c
                        stt(out=acc_t[:, c, 0:n], in0=acc_t[:, c, 0:n], scalar=gains[:, g:g + 1],
                            in1=rstd[:, 0:n], op0=ALU.mult, op1=ALU.mult).then_inc(post_scaled, 1)
                    if c >= LAG and stage < 2:
                        operand_lo(stage + 1, c - LAG, n)

            def pre_norm(norm, n):
                invert(norm, r_pre, n)
                for q in range(4):
                    nc.vector.memset(acc_t[:, 4 * q:4 * q + 4, :], 0.0).then_inc(acc_ready, 1)

            def ffn(f, n, tail):
                U = U_FFN[f]
                ch = 44 * f
                A = A_FFN[f] + 4

                def gate_scale(u, c0, first_bank):
                    dve.wait_ge(unit_used, u + 1)
                    for c in range(2):
                        if not (isinstance(c0, int) and c0 + c < 2):
                            dve.wait_ge(act_done, c0 + c - 1)
                        tt(sil[:, c, 0:n], bank[first_bank + c][:, 0:n], r_pre[:, 0:n], ALU.mult).then_inc(gate_scaled, 1)

                def up_times(u, c0, first_bank):
                    dve.wait_ge(unit_used, u + 1)
                    for c in range(2):
                        if not (isinstance(c0, int) and c0 + c < 2):
                            dve.wait_ge(act_ready, c0 + c - 1)
                        tt(act[:, c, 0:n], bank[first_bank + c][:, 0:n], r_pre[:, 0:n], ALU.mult).then_inc(up_scaled, 1)
                    for c in range(2):
                        dve.wait_ge(silu_done, c0 + c + 1)
                        dve.wait_ge(up_scaled, c0 + c + 1)
                        tt(act[:, c, 0:n], sil[:, c, 0:n], act[:, c, 0:n], ALU.mult).then_inc(act_done, 1)

                def act_lo(c0, half):
                    for c in range(2):
                        dve.wait_ge(act_hi_done, c0 + c + 1)
                        k = 2 * half + c
                        tt(dn_lo[:, k, 0:n], act[:, c, 0:n], dn_hi[:, k, 0:n].bitcast(F32), ALU.subtract).then_inc(act_ready, 1)

                for j in range(2 - f, 8):
                    split(U + j + 2, U + j + 2)
                    if j == 5:
                        pre_norm(4 * f, n)
                        gate_scale(U + 1, ch, 0)
                        up_times(U + 3, ch, 2)
                    if j == 6:
                        act_lo(ch, 0)
                        gate_scale(U + 5, ch + 2, 4)
                    if j == 7:
                        up_times(U + 7, ch + 2, 6)
                        act_lo(ch + 2, 1)
                with dve.Fori(0, SEGS - 1) as i:
                    u0 = U + 8
                    u = dve.snap(i * 12 + u0)
                    c0 = dve.snap(i * 4 + (ch + 4))
                    a0 = dve.snap(i * 4 + A)
                    for j in range(12):
                        split(u + (j + 2), u0 + j + 2)
                        if j == 1:
                            gate_scale(u + 1, c0, 0)
                        if j == 3:
                            up_times(u + 3, c0, 2)
                        if 4 <= j < 8:
                            add_group(u + j, j - 4, a0 + (j - 4 - 3), n)
                        if j == 7:
                            act_lo(c0, 0)
                        if j == 9:
                            gate_scale(u + 9, c0 + 2, 4)
                        if j == 11:
                            up_times(u + 11, c0 + 2, 6)
                            act_lo(c0 + 2, 1)
                last_units(2 * f, U + FFN_UNITS - 4, tail)

            def rotate(index, src, n, table, dst, factor=None):
                dve.wait_ge(swapped, index + 1)
                own.step(tt(prod[:, 0:n], src[:, 0:n], table[:, 0, 0:n], ALU.mult))
                own.step(tt(swap[:, 0:n], swap[:, 0:n], table[:, 1, 0:n], ALU.mult))
                own.wait()
                last = tt(dst, prod[:, 0:n], swap[:, 0:n], ALU.add)
                if factor is not None:
                    own.step(last)
                    own.wait()
                    last = tt(dst, dst, factor[:, 0:n], ALU.mult)
                last.then_inc(rotated, 1)
                dve.wait_ge(rotated, index + 1)

            def pair_projections(j, u, r0, h0, p0):
                if j == 1:
                    for c in range(2):
                        rotate(r0 + c, bank[c], TOK, rope_ret, ret_k[:, c, :])
                if j == 3:
                    for c in range(2):
                        rotate(r0 + 2 + c, bank[2 + c], REAL, rope_ret, ret_q[:, c, :])
                if j == 5:
                    dve.wait_ge(unit_used, u + 6)
                    for c in range(2):
                        tt(ret_vT[:, c, :], bank[c][:, 0:TOK], r_pre[:, :], ALU.mult).then_inc(vT_ready, 1)
                if j == 7:
                    dve.wait_ge(unit_used, u + 8)
                    for c in range(2):
                        tt(ret_gate[:, c, :], bank[2 + c][:, 0:REAL], r_pre[:, 0:REAL], ALU.mult).then_inc(rg_scaled, 1)
                if j == 8:
                    rotate(r0 + 4, bank[2], REAL, rope_mla, mla_qr)
                if j == 10:
                    dve.wait_ge(unit_used, u + 11)
                    nc.vector.tensor_copy(mla_v[:, 0, :], bank[1][:, 0:REAL])
                    nc.vector.tensor_copy(mla_v[:, 1, :], bank[2][:, 0:REAL])
                    nc.vector.tensor_copy(mla_v[0:META, 2, :], bank[3][0:META, 0:REAL]).then_inc(mv_ready, 1)

            def attention(j, h0, p0):
                if j == 0:
                    dve.wait_ge(decay_in, p0 * 32 + 32)
                    for c in range(2):
                        dve.wait_ge(ret_scores, h0 + c + 1)
                        tt(sc[:, c, 0:3 * P], bank[4 + 2 * c][:, 0:3 * P], decay[:, c, :], ALU.mult)
                        tt(sc[0:META, c, 3 * P:640], bank[5 + 2 * c][0:META, 0:REAL], decay_meta[0:META, c, :], ALU.mult).then_inc(ret_masked, 1)
                    own.step(nc.vector.tensor_copy(small[:, 8:10], gains[:, bass.ds(h0 + G_RET, 2)]))
                if j == 2:
                    softmax(h0)
                if j == 4:
                    group_norm(h0, p0, 0)
                if j == 5:
                    softmax(h0 + 1)
                if j == 6:
                    group_norm(h0, p0, 1)
                    mla_lo(h0, p0, 0)
                if j == 10:
                    mla_lo(h0, p0, 1)

            def softmax(hd):
                for t in range(2):
                    b = bank[(5, 7)[t]][:, 0:TOK]
                    dve.wait_ge(mla_scores, hd * 2 + (t + 1))
                    own.step(stt(out=probs[:, t, :], in0=b, scalar=MLA_SCALE, in1=mask[:, t, :], op0=ALU.mult, op1=ALU.add))
                    own.wait()
                    own.step(nc.vector.reduce_max(small[:, 2 + t:3 + t], probs[:, t, :], AX.X))
                    own.wait()
                    ts(small[:, 4 + t:5 + t], small[:, 2 + t:3 + t], -1.0, None, ALU.mult).then_inc(neg_max, 1)
                for t in range(2):
                    dve.wait_ge(exp_done, hd * 2 + (t + 1))
                    own.step(nc.vector.reciprocal(small[:, 10 + t:11 + t], small[:, 6 + t:7 + t]))
                    own.wait()
                    ts(probs[:, t, :], probs[:, t, :], small[:, 10 + t:11 + t], None, ALU.mult).then_inc(probs_ready, 1)

            def group_norm(h0, p0, c):
                dve.wait_ge(ret_std, h0 + c + 1)
                dve.wait_ge(gate_ready, h0 + c + 1)
                own.step(nc.vector.reciprocal(ret_rs[:, c, :], ret_rs[:, c, :]))
                own.wait()
                own.step(tt(ret_o[:, c, :], ret_o[:, c, :], ret_rs[:, c, :], ALU.mult))
                own.wait()
                stt(out=ret_o[:, c, :], in0=ret_o[:, c, :], scalar=small[:, 8 + c:9 + c], in1=ret_gate[:, c, :],
                    op0=ALU.mult, op1=ALU.mult).then_inc(ret_f, 1)
                dve.wait_ge(mix_hi_done, p0 * 4 + (c + 1))
                tt(dn_lo[:, c, 0:REAL], ret_o[:, c, :], dn_hi[:, c, 0:REAL].bitcast(F32), ALU.subtract).then_inc(mix_ready, 1)

            def mla_lo(h0, p0, c):
                dve.wait_ge(mix_hi_done, p0 * 4 + (c + 3))
                tt(dn_lo[:, 2 + c, 0:REAL], bank[4 + 2 * c][:, 0:REAL], dn_hi[:, 2 + c, 0:REAL].bitcast(F32), ALU.subtract).then_inc(mix_ready, 1)

            split(0, 0)
            dve.wait_ge(gains_tr, 1)
            nc.vector.tensor_copy(gains[:, 0:KC], bank[0][:, 0:KC]).then_inc(gains_ready, 1)
            dve.wait_ge(gains_ready, 1)
            for c in range(KC + 2):
                if c in UNIT_AT_CHUNK[1:]:
                    split(UNIT_AT_CHUNK.index(c), UNIT_AT_CHUNK.index(c))
                if c < KC:
                    dve.wait_ge(x_tr, c + 1)
                    nc.vector.tensor_copy(h[:, c, :], bank[2 + c % X_AHEAD][:, 0:TOK]).then_inc(h_ready, 1)
                if c >= 2:
                    operand_lo(0, c - 2, TOK)
            split(3, 3)
            dve.wait_ge(gains_tr, 2)
            ts(gains[:, G_POST[0]:G_POST[0] + KC], bank[7][:, G_POST[0]:G_POST[0] + KC], 0.5, None, ALU.mult)
            ts(gains[:, G_POST[2]:G_POST[2] + KC], bank[7][:, G_POST[2]:G_POST[2] + KC], 0.5, None, ALU.mult)
            nc.vector.tensor_copy(gains[:, G_PRE[1]:G_POST[2]], bank[7][:, G_PRE[1]:G_POST[2]])
            nc.vector.tensor_copy(gains[:, G_RET:GAINS], bank[7][:, G_RET:GAINS]).then_inc(gains_ready, 1)

            def tail1(u):
                split(u + 2, u + 2, kind="kr" if u + 2 == U_PRE + 2 else "full")

            ffn(0, TOK, tail1)
            post_norm(0, TOK)

            dve.wait_ge(pad_zero, 2)
            dve.wait_ge(tables_in, 48)

            def latent_read(u, before, tiles, n, banks, f):
                dve.wait_ge(unit_used, u + 1)
                for c in range(tiles):
                    tt(f[:, before + c, 0:n], bank[banks[c]][:, 0:n], r_pre[:, 0:n], ALU.mult).then_inc(lat_read, 1)

            def latent_norm(index, before, tiles, n, f, gain, hi, lo):
                dve.wait_ge(lat_std, index + 1)
                own.step(nc.vector.reciprocal(rstd[:, 0:n], rstd[:, 0:n]))
                own.wait()
                for c in range(tiles):
                    stt(out=f[:, c, 0:n], in0=f[:, c, 0:n], scalar=gains[:, gain + c:gain + c + 1],
                        in1=rstd[:, 0:n], op0=ALU.mult, op1=ALU.mult).then_inc(lat_normed, 1)
                for c in range(tiles):
                    dve.wait_ge(lat_hi_done, before + c + 1)
                    tt(lo[:, c, 0:n], f[:, c, 0:n], hi[:, c, 0:n].bitcast(F32), ALU.subtract).then_inc(lat_ready, 1)

            for j in range(1, PRE_UNITS):
                u = U_PRE + j
                split(u + 2, u + 2)
                if j == 5:
                    pre_norm(2, TOK)
                    latent_read(U_PRE + 1, 0, CC, TOK, (0, 1), ckv_f)
                    rotate(0, bank[2], TOK, rope_mla, mla_kr, r_pre)
                    latent_read(U_PRE + 4, 0, 2, REAL, (3, 4), cq_f)
                    for t in range(2):
                        own.step(tt(rope_ret[:, t, :], rope_ret[:, t, :], r_pre[:, :], ALU.mult))
                if j == 6:
                    latent_read(U_PRE + 6, 2, 2, REAL, (5, 6), cq_f)
            own.wait()
            dve.wait_ge(spilled, 16)
            for j in range(PAIR_UNITS):
                u = U_MIX + j
                split(u + 2, u + 2, kind=pair_kind(j + 2))
                if j == 1:
                    latent_norm(0, 0, CC, TOK, ckv_f, G_KV, ckv_hi, ckv_lo)
                if j == 3:
                    latent_norm(1, CC, QC, REAL, cq_f, G_Q, cq_hi, cq_lo)
                pair_projections(j, U_MIX, 1, 0, 0)
            with dve.Fori(0, PAIRS - 1) as i:
                u0 = U_MIX + PAIR_UNITS
                u = dve.snap(i * 15 + u0)
                h0 = dve.snap(i * 2)
                h1 = dve.snap(i * 2 + 2)
                r0 = dve.snap(i * 5 + 6)
                a0 = dve.snap(i * 4 + (A_MIX + 4))
                PER = 27
                own.turn, own.per, start = i, PER, own.n
                for j in range(15):
                    if j == 10:
                        attention(j, h0, i)
                    split(u + (j + 2), u0 + j + 2, kind=pair_kind(j + 2))
                    if j != 10:
                        attention(j, h0, i)
                    if j < PAIR_UNITS:
                        pair_projections(j, u, r0, h1, i + 1)
                    else:
                        add_group(u + j, j - 11, a0 + (j - 11 - 3), REAL)
                assert own.n - start == PER, own.n - start
                own.n, own.turn = start + PER * (PAIRS - 1), None
            for j in range(PAIR_UNITS):
                attention(j, HEADS - 2, PAIRS - 1)
            last_units(1, U_FFN[1] - 4, lambda u: split(u + 2, u + 2))
            post_norm(1, REAL)

            def tail(u):
                if u + 2 < U_ALL:
                    split(u + 2, u + 2)

            ffn(1, REAL, tail)
            post_norm(2, REAL)


_INS = ["x", "meta_tokens", "ffn1_pre_norm", "ffn1_w_gate", "ffn1_w_up", "ffn1_w_down",
        "ffn1_post_norm", "mix_pre_norm", "w_in", "ret_group_norm", "mla_q_norm", "mla_w_uq",
        "mla_kv_norm", "mla_w_uk", "mla_w_uv", "w_out", "mix_post_norm", "ffn2_pre_norm",
        "ffn2_w_gate", "ffn2_w_up", "ffn2_w_down", "ffn2_post_norm"]


def kernel(**inputs):
    import concourse.bacc as bacc
    from concourse.bass_utils import run_bass_kernel_spmd

    nc = bacc.Bacc("TRN2", target_bir_lowering=False, num_devices=1)
    arrays, aps = {}, {}
    for name in _INS:
        x = np.ascontiguousarray(inputs[name])
        if x.ndim == 3:
            x = x.reshape(x.shape[1:])
        arrays[f"in_{name}"] = x
    for name, x in constants().items():
        arrays[f"in_{name}"] = x
    for name, x in arrays.items():
        aps[name[3:]] = nc.dram_tensor(name, x.shape, mybir.dt.from_np(x.dtype), kind="ExternalInput").ap()
    out = nc.dram_tensor("out_dram", (REAL, DM), F32, kind="ExternalOutput").ap()
    build(nc, aps, out)
    r = run_bass_kernel_spmd(nc, [arrays], core_ids=[0])
    return r.results[0]["out_dram"].reshape(1, REAL, DM)
```

```python
from contextlib import ExitStack

import numpy as np

import concourse.bass as bass
from concourse import mybir

ACT = mybir.ActivationFunctionType
ALU = mybir.AluOpType
AX = mybir.AxisListType
F32 = mybir.dt.float32
F32R = mybir.dt.float32r

P = 128
DM, FF = 2048, 5632
REAL, META = 256, 16
TOK = REAL + META
KC = DM // P
HEADS, DH, ROPE = 8, 128, 64
Q_RANK, KV_RANK = 512, 256
QC, CC = Q_RANK // P, KV_RANK // P
EPS = 1e-6
MLA_SCALE = float(DH + ROPE) ** -0.5
PAIRS = HEADS // 2

UNIT = 2048
SLOTS = 3
SEG = 512
SEGS = FF // SEG
FFN_UNITS = 12 * SEGS
PRE_UNITS = 7
PAIR_UNITS = 11
OUT_UNITS = 4
U_FFN = (0, FFN_UNITS + PRE_UNITS + PAIRS * (PAIR_UNITS + OUT_UNITS))
U_PRE = FFN_UNITS
U_KR = U_PRE + 4
CQ_BANKS = ((4, 5), (6, 3))
U_MIX = U_PRE + PRE_UNITS
U_ALL = U_FFN[1] + FFN_UNITS
C_RQ, C_RK, C_RV, C_RG = 0, 1024, 2048, 3072
C_CQ, C_CKV, C_KR = 4096, 4608, 4864
A_FFN = (0, 4 + 4 * SEGS + 4 + 4 * PAIRS)
A_MIX = 4 + 4 * SEGS
A_DONE = tuple(a + 4 + 4 * (n - 1) for a, n in ((A_FFN[0], SEGS), (A_MIX, PAIRS), (A_FFN[1], SEGS)))
POOL_OUT = (14, 38, 62)
TILES = (0, 18, 21)
X_AHEAD = 4
UNIT_AT_CHUNK = (1, 8, 9, 11)
G_PRE, G_POST = (0, 2 * KC, 4 * KC), (KC, 3 * KC, 5 * KC)
G_RET = 6 * KC
G_Q, G_KV = G_RET + HEADS, G_RET + HEADS + QC
GAINS = G_KV + CC


def constants():
    pos = np.concatenate([META + np.arange(REAL), np.arange(META)]).astype(np.float32)

    def rope(dim):
        inv = np.float32(10000.0) ** (-np.arange(0, dim, 2, dtype=np.float32) / np.float32(dim))
        ang = (pos[:, None] * inv[None, :]).astype(np.float32)
        c, s = np.cos(ang).T, np.sin(ang).T
        reps = P // dim
        return np.stack([np.concatenate([c, c] * reps), np.concatenate([-s, s] * reps)])

    tri = np.where(np.arange(P)[None, :] <= np.arange(P)[:, None], 0.0, -1e30)
    mask = np.zeros((2, P, TOK))
    mask[0, :, 0:P], mask[0, :, P:REAL] = tri, -1e30
    mask[1, :, P:REAL] = tri
    log_g = np.log(1.0 - 2.0 ** (-5.0 - np.arange(HEADS)))
    m, n = np.arange(P), np.arange(REAL)
    diff = (n[None, :] - m[:, None])[None]
    d = np.where(diff >= 0, np.exp(np.maximum(diff, 0) * log_g[:, None, None]), 0.0) * DH ** -0.5
    d = np.concatenate([d, d[:, :, 0:P]], axis=2)
    dm = np.exp((META + n[None, :] - np.arange(META)[:, None])[None] * log_g[:, None, None]) * DH ** -0.5
    f = lambda a: np.ascontiguousarray(a, dtype=np.float32)
    return {
        "rope_ret": f(rope(DH)), "rope_mla": f(rope(ROPE)), "mask": f(mask),
        "decay": f(d.reshape(PAIRS, 2, P, 3 * P).transpose(0, 2, 1, 3)),
        "decay_meta": f(dm.reshape(PAIRS, 2, META, REAL).transpose(0, 2, 1, 3)),
        "ident": f(np.eye(P)),
    }


def build(nc, a, out):
    ctx = ExitStack()
    with ctx:
        def sb(name, shape, dt=F32):
            return ctx.enter_context(nc.sbuf_tensor(name, shape, dt))

        def sem(name):
            return ctx.enter_context(nc.semaphore(name))

        raw = sb("raw", [P, SLOTS, UNIT])
        w_hi = sb("w_hi", [P, SLOTS, UNIT], F32R)
        w_lo = sb("w_lo", [P, SLOTS, UNIT], F32R)
        hT = sb("hT", [P, KC * TOK])
        hn_hi = sb("hn_hi", [P, KC, TOK], F32R)
        hn_lo = sb("hn_lo", [P, KC, TOK], F32R)
        acc = sb("acc", [P, KC * TOK])
        dn_hi = sb("dn_hi", [P, 4, TOK], F32R)
        dn_lo = sb("dn_lo", [P, 4, TOK], F32R)
        tmp = sb("tmp", [P, 4, TOK])
        gains = sb("gains", [P, GAINS])
        ident = sb("ident_sb", [P, P])
        ones = sb("ones", [P, P])
        rope_ret = sb("rope_ret_sb", [P, 2, TOK])
        rope_mla = sb("rope_mla_sb", [P, 2, TOK])
        mask = sb("mask_sb", [P, 2, TOK])
        ssq = sb("ssq", [P, TOK])
        rstd = sb("rstd", [P, TOK])
        r_pre = sb("r_pre", [P, TOK])
        small = sb("small", [P, 16])
        eps, root = small[:, 0:1], small[:, 12:15]
        ckv_hi = sb("ckv_hi", [P, CC, 3 * P], F32R)
        ckv_lo = sb("ckv_lo", [P, CC, 3 * P], F32R)
        cq_hi = sb("cq_hi", [P, QC, REAL], F32R)
        cq_lo = sb("cq_lo", [P, QC, REAL], F32R)

        h = hT[:, :].rearrange("p (c n) -> p c n", c=KC)
        acc_t = acc[:, :].rearrange("p (c n) -> p c n", c=KC)
        sil, act = tmp[:, 0:2, :], tmp[:, 2:4, :]
        swap, prod, probs = tmp[:, 0, :], tmp[:, 1, :], tmp[:, 2:4, :]

        at = [0]

        def carve(t, size, n):
            v = t[:, at[0]:at[0] + size]
            at[0] += size
            return v.rearrange("p (a n) -> p a n", n=n)

        ret_k = carve(hT, 2 * TOK, TOK)
        ret_q = carve(hT, 2 * REAL, REAL)
        ret_vT = carve(hT, 2 * TOK, TOK)
        ret_v = carve(hT, 2 * 3 * P, 3 * P)
        ret_gate = carve(hT, 2 * REAL, REAL)
        mla_q = carve(hT, 2 * REAL, REAL)
        mla_qr = carve(hT, REAL, REAL)[:, 0, :]
        mla_k = carve(hT, 2 * TOK, TOK)
        assert at[0] <= KC * TOK
        MIX = TOK + 3 * REAL + 2 * 640 + 2 * 3 * P + 2 * REAL + 2 * TOK + QC * REAL
        mix = sb("mix", [P, MIX])
        at[0] = 0
        mla_kr = carve(mix, TOK, TOK)[:, 0, :]
        mla_v = carve(mix, 3 * REAL, REAL)
        sc = carve(mix, 2 * 640, 640)
        decay = carve(mix, 2 * 3 * P, 3 * P)
        decay_meta = carve(mix, 2 * REAL, REAL)
        keep = carve(mix, 2 * TOK + QC * REAL, 2 * TOK + QC * REAL)[:, 0, :]
        lat_sq = mix[:, TOK + 3 * REAL:TOK + 3 * REAL + 4 * TOK].rearrange("p (a n) -> p a n", n=TOK)
        ckv_f = keep[:, 0:2 * TOK].rearrange("p (a n) -> p a n", n=TOK)
        cq_f = keep[:, 2 * TOK:].rearrange("p (a n) -> p a n", n=REAL)
        ret_o = keep[:, 0:2 * REAL].rearrange("p (a n) -> p a n", n=REAL)
        ret_sq = keep[:, 2 * REAL:4 * REAL].rearrange("p (a n) -> p a n", n=REAL)
        ret_rs = keep[:, 4 * REAL:6 * REAL].rearrange("p (a n) -> p a n", n=REAL)
        x_sb = acc[:, 0:2 * DM].rearrange("p (t d) -> p t d", t=2)
        meta_sb = mix[0:META, 0:DM]
        gain_rows = mix[0:GAINS, DM:DM + P]

        bank = [ctx.enter_context(nc.psum_tensor(f"bank{i}", [P, 512], F32)) for i in range(8)]
        spill = nc.dram_tensor("h_spill", (P, KC * TOK), F32).ap()

        gains_in = sem("gains_in")
        consts_in = sem("consts_in")
        tables_in = sem("tables_in")
        x_in = [sem(f"x_in{i}") for i in range(4)]
        raw_full = [sem(f"raw_full{i}") for i in range(SLOTS)]
        hi_ready = sem("hi_ready")
        lo_ready = sem("lo_ready")
        unit_used = sem("unit_used")
        ones_set = sem("ones_set")
        gains_tr = sem("gains_tr")
        gains_ready = sem("gains_ready")
        x_tr = sem("x_tr")
        h_ready = sem("h_ready")
        h_last = sem("h_last")
        post_scaled = sem("post_scaled")
        tile_done = sem("tile_done")
        tile_added = sem("tile_added")
        squared = sem("squared")
        pool_step = sem("pool_step")
        ssq_ready = sem("ssq_ready")
        ms_done = sem("ms_done")
        std_done = sem("std_done")
        diag_done = sem("diag_done")
        spread = sem("spread")
        r_kept = sem("r_kept")
        dve_step = sem("dve_step")
        hn_hi_done = sem("hn_hi_done")
        hn_ready = sem("hn_ready")
        up_scaled = sem("up_scaled")
        gate_scaled = sem("gate_scaled")
        silu_done = sem("silu_done")
        act_done = sem("act_done")
        act_hi_done = sem("act_hi_done")
        act_ready = sem("act_ready")
        acc_ready = sem("acc_ready")
        swapped = sem("swapped")
        rotated = sem("rotated")
        vT_ready = sem("vT_ready")
        rg_scaled = sem("rg_scaled")
        gate_ready = sem("gate_ready")
        v_tr = sem("v_tr")
        v_ready = sem("v_ready")
        mq_ready = sem("mq_ready")
        mk_ready = sem("mk_ready")
        mv_ready = sem("mv_ready")
        ret_scores = sem("ret_scores")
        ret_masked = sem("ret_masked")
        ret_out = sem("ret_out")
        ret_sq_done = sem("ret_sq_done")
        ret_ms = sem("ret_ms")
        ret_std = sem("ret_std")
        ret_f = sem("ret_f")
        mix_hi_done = sem("mix_hi_done")
        mix_ready = sem("mix_ready")
        mla_scores = sem("mla_scores")
        neg_max = sem("neg_max")
        exp_done = sem("exp_done")
        probs_ready = sem("probs_ready")
        probs_tr = sem("probs_tr")
        probsT_ready = sem("probsT_ready")
        mla_out = sem("mla_out")
        lat_read = sem("lat_read")
        lat_sqd = sem("lat_sqd")
        lat_ms = sem("lat_ms")
        lat_std = sem("lat_std")
        lat_normed = sem("lat_normed")
        lat_hi_done = sem("lat_hi_done")
        lat_ready = sem("lat_ready")
        pad_zero = sem("pad_zero")
        decay_in = sem("decay_in")
        spilled = sem("spilled")
        reloaded = sem("reloaded")
        out_tr = sem("out_tr")
        out_ready = sem("out_ready")
        stored = sem("stored")

        def slot(ring, u0, **shape):
            v = ring[:, u0 % SLOTS, :]
            n = UNIT
            if "n" in shape:
                n = shape["n"]
                v = v[:, 0:n]
            k = shape["k"]
            return v.rearrange("p (k n) -> p k n", k=k)

        def split_parts(u0, kind):
            if kind == "kr":
                src = slot(raw, u0, k=KC, n=KC * ROPE)
                hi, lo = (slot(r, u0, k=KC).rearrange("p k (r n) -> p k r n", r=2) for r in (w_hi, w_lo))
                return [(src, hi[:, :, r, :], lo[:, :, r, :]) for r in range(2)]
            if kind == "uq":
                src = slot(raw, u0, k=QC, n=QC * 384).rearrange("p k (h n) -> p k h n", h=2)
                hi, lo = (slot(r, u0, k=QC, n=QC * 384) for r in (w_hi, w_lo))
                cut = [(slice(0, DH), slice(0, 2 * DH)), (slice(DH, DH + ROPE), slice(2 * DH, 384))]
                return [(src[:, :, :, a_], *(x[:, :, b_].rearrange("p k (h n) -> p k h n", h=2) for x in (hi, lo)))
                        for a_, b_ in cut]
            n = CC * 256 if kind == "ukv" else UNIT
            return [tuple(x[:, u0 % SLOTS, 0:n] for x in (raw, w_hi, w_lo))]

        def pair_kind(j):
            return {8: "uq", 9: "ukv", 10: "ukv"}.get(j, "full")

        kt = {name: a[name].rearrange("(k p) n -> p k n", p=P) for name in
              ("ffn1_w_gate", "ffn1_w_up", "ffn1_w_down", "ffn2_w_gate", "ffn2_w_up",
               "ffn2_w_down", "w_in", "mla_w_uq", "mla_w_uk", "mla_w_uv", "w_out")}
        FILL = 32

        def last_banks(stage, q):
            return 4 * (q % 2) if stage != 1 else 4 * (1 - q % 2)

        def sum_bank(norm):
            return bank[3 if norm in (1, 5) else 7]

        def by_dve(c):
            return c % 3 == 2

        block = ctx.enter_context(nc.Block())

        @block.sync
        def _(sp):
            def load(u, u0, halves):
                if not (isinstance(u, int) and u < SLOTS):
                    sp.wait_ge(lo_ready, u - SLOTS + 1)
                for d, s in halves:
                    sp.dma_start(d, s).then_inc(raw_full[u0 % SLOTS], 16)

            def gate_up(u, u0, w, col, kh):
                v = slot(raw, u0, k=8)
                load(u, u0, [(v[:, 4 * i:4 * i + 4, :],
                              kt[w][:, 8 * kh + 4 * i:8 * kh + 4 * i + 4, bass.ds(col, 256)])
                             for i in range(2)])

            def down(u, u0, w, k0, k1, q):
                v = slot(raw, u0, k=4)
                load(u, u0, [(v[:, 2 * i:2 * i + 2, :], kt[w][:, bass.ds(k, 2), q * 512:q * 512 + 512])
                             for i, k in enumerate((k0, k1))])

            def ffn_loads(f, between=None):
                g, up, dn = (f"ffn{f + 1}_w_{x}" for x in ("gate", "up", "down"))
                U = U_FFN[f]

                def half(u, u0, col, between=None):
                    parts = ((g, 0), (g, 1), (up, 0), (up, 1))
                    if between is not None:
                        parts = ((g, 0), (up, 0), (g, 1), (up, 1))
                    for j, (w, kh) in enumerate(parts):
                        gate_up(u + j, u0 + j, w, col, kh)
                        if between is not None and j < 3:
                            between(j)

                half(U, U, 0, between)
                half(U + 4, U + 4, 256)
                with sp.Fori(0, SEGS - 1) as i:
                    u0 = U + 8
                    u = sp.snap(i * 12 + u0)
                    col0 = sp.snap(i * SEG + SEG)
                    col1 = sp.snap(i * SEG + SEG + 256)
                    k0 = sp.snap(i * 4)
                    k1 = sp.snap(i * 4 + 2)
                    half(u, u0, col0)
                    for q in range(4):
                        down(u + 4 + q, u0 + 4 + q, dn, k0, k1, q)
                    half(u + 8, u0 + 8, col1)
                for q in range(4):
                    u = U + FFN_UNITS - 4 + q
                    down(u, u, dn, 4 * SEGS - 4, 4 * SEGS - 2, q)

            def pair_loads(u, u0, c256, c384, p2):
                for b, c in enumerate((C_RK, C_RQ, C_RV, C_RG)):
                    for kh in range(2):
                        gate_up(u + 2 * b + kh, u0 + 2 * b + kh, "w_in", c256[c], kh)
                v = slot(raw, u0 + 8, k=QC, n=QC * 384)
                load(u + 8, u0 + 8, [(v[:, 2 * i:2 * i + 2, :],
                                      kt["mla_w_uq"][:, 2 * i:2 * i + 2, bass.ds(c384, 384)])
                                     for i in range(2)])
                for j, w in enumerate(("mla_w_uk", "mla_w_uv")):
                    v = slot(raw, u0 + 9 + j, k=CC, n=CC * 256)
                    load(u + 9 + j, u0 + 9 + j, [(v[:, i:i + 1, :],
                                                  kt[w][:, i:i + 1, bass.ds(c256[0], 256)])
                                                 for i in range(2)])
                if not isinstance(p2, int):
                    sp.wait_ge(ret_masked, p2)

            sp.dma_start(meta_sb, a["meta_tokens"]).then_inc(x_in[0], 16)

            def x_loads(pieces):
                for i in pieces:
                    cs = slice(i * 512, (i + 1) * 512)
                    sp.dma_start(x_sb[:, :, cs], a["x"].rearrange("(t p) d -> p t d", p=P)[:, :, cs]).then_inc(x_in[i], 16)

            def beside_first_units(j):
                x_loads((j + 1,))
                if j < 2:
                    return
                for name, at0, rows in (("ffn1_post_norm", G_POST[0], KC), ("mix_pre_norm", G_PRE[1], KC),
                                        ("mix_post_norm", G_POST[1], KC), ("ffn2_pre_norm", G_PRE[2], KC),
                                        ("ffn2_post_norm", G_POST[2], KC), ("ret_group_norm", G_RET, HEADS),
                                        ("mla_q_norm", G_Q, QC), ("mla_kv_norm", G_KV, CC)):
                    sp.dma_start(gain_rows[at0:at0 + rows, :],
                                 a[name].rearrange("o (c p) -> (o c) p", p=P)).then_inc(gains_in, 16)
                for t, name in ((rope_ret, "rope_ret"), (rope_mla, "rope_mla"), (mask, "mask")):
                    sp.dma_start(t[:, :, :], a[name].rearrange("t p n -> p t n")).then_inc(tables_in, 16)

            x_loads((0,))
            ffn_loads(0, between=beside_first_units)
            for kh in range(2):
                gate_up(U_PRE + 2 * kh, U_PRE + 2 * kh, "w_in", C_CKV, kh)
                gate_up(U_PRE + 2 * kh + 1, U_PRE + 2 * kh + 1, "w_in", C_CQ, kh)
            u = U_KR
            v = slot(raw, u, k=KC, n=KC * ROPE)
            load(u, u, [(v[:, 8 * i:8 * i + 8, :], kt["w_in"][:, 8 * i:8 * i + 8, C_KR:C_KR + ROPE])
                        for i in range(2)])
            for kh in range(2):
                gate_up(U_PRE + 5 + kh, U_PRE + 5 + kh, "w_in", C_CQ + 256, kh)
            sp.wait_ge(h_ready, 2 * KC)
            sp.dma_start(spill, hT[:, :]).then_inc(spilled, 16)

            def decay_load(src_p):
                sp.dma_start(decay, a["decay"][src_p]).then_inc(decay_in, 16)
                sp.dma_start(decay_meta[0:META], a["decay_meta"][src_p]).then_inc(decay_in, 16)

            cols = {c: c for c in (0, C_RK, C_RV, C_RG)}
            pair_loads(U_MIX, U_MIX, cols, 0, 0)
            sp.wait_ge(lat_normed, 2)
            decay_load(0)
            with sp.Fori(0, PAIRS - 1) as i:
                u0 = U_MIX + PAIR_UNITS
                u = sp.snap(i * 15 + u0)
                cols = {c: sp.snap(i * 256 + (256 + c)) for c in (0, C_RK, C_RV, C_RG)}
                c384 = sp.snap(i * 384 + 384)
                p2 = sp.snap(i * 2 + 2)
                k0 = sp.snap(i * 2)
                k1 = sp.snap(i * 2 + HEADS)
                d0 = sp.snap(i * (P * 6 * P) + P * 6 * P)
                dm0 = sp.snap(i * (META * 2 * REAL) + META * 2 * REAL)
                pair_loads(u, u0, cols, c384, p2)
                dsrc = a["decay"].rearrange("a p h n -> (a p h n)")[bass.ds(d0, P * 6 * P)]
                sp.dma_start(decay, dsrc.rearrange("(p h n) -> p h n", p=P, h=2)).then_inc(decay_in, 16)
                msrc = a["decay_meta"].rearrange("a p h n -> (a p h n)")[bass.ds(dm0, META * 2 * REAL)]
                sp.dma_start(decay_meta[0:META], msrc.rearrange("(p h n) -> p h n", p=META, h=2)).then_inc(decay_in, 16)
                for q in range(4):
                    down(u + 11 + q, u0 + 11 + q, "w_out", k0, k1, q)
            for q in range(4):
                u = U_FFN[1] - 4 + q
                down(u, u, "w_out", HEADS - 2, 2 * HEADS - 2, q)
            def reload(j):
                if j == 1:
                    sp.wait_ge(spilled, 16)
                    sp.wait_ge(mix_ready, 4 * PAIRS)
                    sp.dma_start(hT[:, :], spill).then_inc(reloaded, 16)

            ffn_loads(1, between=reload)
            for b in range(4):
                for t in range(2):
                    sp.wait_ge(out_ready, 2 * b + t + 1)
                    sp.dma_start(out[t * P:(t + 1) * P, b * 512:(b + 1) * 512],
                                 raw[:, t, b * 512:(b + 1) * 512]).then_inc(stored, 16)
            sp.wait_ge(stored, 16 * 8)

        @block.gpsimd
        def _(pool):
            steps = [0]
            nc.gpsimd.memset(ones[:, :], 1.0).then_inc(ones_set, 1)
            nc.gpsimd.memset(eps, EPS).then_inc(ones_set, 1)
            nc.gpsimd.memset(ckv_hi[:, :, TOK:].bitcast(F32), 0.0).then_inc(pad_zero, 1)
            nc.gpsimd.memset(ckv_lo[:, :, TOK:].bitcast(F32), 0.0).then_inc(pad_zero, 1)

            def accumulate(src, c, last):
                if c == 0:
                    return
                n = src(c).shape[-1]
                so_far = src(0) if c == 1 else ssq[:, 0:n]
                if c > 1:
                    pool.wait_ge(pool_step, steps[0])
                add = nc.gpsimd.tensor_tensor(ssq[:, 0:n], so_far, src(c), ALU.add)
                if c == last:
                    add.then_inc(ssq_ready, 1)
                else:
                    add.then_inc(pool_step, 1)
                    steps[0] += 1

            def sum_output(norm, sq0, n):
                pool.wait_ge(ms_done, norm)
                for c in range(12):
                    pool.wait_ge(squared, sq0 + c + 1)
                    accumulate(lambda k: tmp[:, k % 4, 0:n], c, 11)

            def sum_residual(norm, sq0, n):
                if norm:
                    pool.wait_ge(ms_done, norm)
                for c in range(KC):
                    pool.wait_ge(squared, sq0 + c + 1)
                    accumulate(lambda k: acc_t[:, k, 0:n] if norm else tmp[:, k % 4, 0:n], c, KC - 1)

            def add_to_residual(stage, n):
                for c in range(KC):
                    if stage == 2 and by_dve(c):
                        continue
                    pool.wait_ge(post_scaled, KC * stage + c + 1)
                    nc.gpsimd.tensor_tensor(h[:, c, 0:n], h[:, c, 0:n], acc_t[:, c, 0:n], ALU.add).then_inc(h_ready, 1)

            sum_residual(0, 0, TOK)
            sum_output(1, 16, TOK)
            add_to_residual(0, TOK)
            sum_residual(2, 32, TOK)
            sum_output(3, 48, REAL)
            pool.wait_ge(reloaded, 16)
            add_to_residual(1, REAL)
            sum_residual(4, 64, REAL)
            sum_output(5, 80, REAL)
            add_to_residual(2, REAL)

        @block.scalar
        def _(act_e):
            def copy(o, i):
                return nc.scalar.activation(o, i, ACT.Copy)

            def split(u, u0, kind="full", filled=0):
                act_e.wait_ge(raw_full[u0 % SLOTS], filled + FILL * (u0 // SLOTS + 1))
                if not (isinstance(u, int) and u < SLOTS):
                    act_e.wait_ge(unit_used, u - SLOTS + 1)
                for src, hi, _ in split_parts(u0, kind):
                    last = copy(hi, src)
                last.then_inc(hi_ready, 1)

            def std(norm, n):
                act_e.wait_ge(ms_done, norm + 1)
                last = nc.scalar.activation(root[:, 0:2], sum_bank(norm)[:, 0:2], ACT.Sqrt, bias=eps, scale=1.0 / DM)
                if n == TOK:
                    last = nc.scalar.activation(root[0:META, 2:3], sum_bank(norm)[0:META, 2:3], ACT.Sqrt, bias=small[0:META, 0:1], scale=1.0 / DM)
                last.then_inc(std_done, 1)

            def operand_hi(stage, c, n):
                act_e.wait_ge(h_ready, stage * KC + c + 1)
                g = G_PRE[stage] + c
                nc.scalar.activation(hn_hi[:, c, 0:n], h[:, c, 0:n], ACT.Copy, scale=gains[:, g:g + 1]).then_inc(hn_hi_done, 1)

            def square_residual(c, n):
                nc.scalar.activation(acc_t[:, c, 0:n], h[:, c, 0:n], ACT.Square).then_inc(squared, 1)

            def residual_operand(stage, n, split_fourth):
                for c in range(KC):
                    if c == 12:
                        split_fourth()
                    operand_hi(stage, c, n)
                    square_residual(c, n)

            def square_output(stage, q, n):
                for i in range(4):
                    c = 4 * q + i
                    if q < 3 or i == 3:
                        act_e.wait_ge(acc_ready, A_DONE[stage] + q + 1)
                    else:
                        act_e.wait_ge(tile_added, TILES[stage] + i + 1)
                    if c == KC - 1:
                        act_e.wait_ge(ssq_ready, 2 * stage + 2)
                    elif q > 0:
                        act_e.wait_ge(pool_step, POOL_OUT[stage] + max(c - 4, 1))
                    nc.scalar.activation(tmp[:, i, 0:n], acc_t[:, c, 0:n], ACT.Square).then_inc(squared, 1)

            def ffn(f, n, tail):
                U = U_FFN[f]

                def silu(ch):
                    for c in range(2):
                        act_e.wait_ge(gate_scaled, ch + c + 1)
                        nc.scalar.activation(sil[:, c, 0:n], sil[:, c, 0:n], ACT.Silu).then_inc(silu_done, 1)

                def act_hi(ch, half):
                    for c in range(2):
                        act_e.wait_ge(act_done, ch + c + 1)
                        copy(dn_hi[:, 2 * half + c, 0:n], act[:, c, 0:n]).then_inc(act_hi_done, 1)

                ch = 44 * f
                for j in range(3 - f, 8):
                    if j == 5:
                        std(4 * f, n)
                    split(U + j + 2, U + j + 2)
                    if j == 5:
                        silu(ch)
                    if j == 6:
                        act_hi(ch, 0)
                        silu(ch + 2)
                    if j == 7:
                        act_hi(ch + 2, 1)
                with act_e.Fori(0, SEGS - 1) as i:
                    u0 = U + 8
                    u = act_e.snap(i * 12 + u0)
                    c0 = act_e.snap(i * 4 + (ch + 4))
                    filled = act_e.snap(i * (12 // SLOTS * FILL))
                    for j in range(12):
                        split(u + (j + 2), u0 + j + 2, filled=filled)
                        if j == 1:
                            silu(c0)
                        if j == 7:
                            act_e.wait_ge(unit_used, u + 8)
                            act_hi(c0, 0)
                        if j == 9:
                            silu(c0 + 2)
                        if j == 11:
                            act_hi(c0 + 2, 1)
                last_units(2 * f, U + FFN_UNITS - 4, tail)

            def last_units(stage, u, tail, after_first=None):
                n = (TOK, REAL, REAL)[stage]
                nc.scalar.activation(small[:, 15:16], eps, ACT.Sqrt)
                for q in range(4):
                    tail(u + q)
                    if q == 0 and after_first is not None:
                        after_first()
                    if q > 0:
                        square_output(stage, q - 1, n)
                square_output(stage, 3, n)
                std(2 * stage + 1, n)
                if stage < 2:
                    tail(u + 4)

            def swap_halves(index, src, n, width):
                if index > 0:
                    act_e.wait_ge(rotated, index)
                last = None
                for b in range(P // width):
                    o = b ^ 1
                    last = copy(swap[b * width:(b + 1) * width, 0:n], src[o * width:(o + 1) * width, 0:n])
                last.then_inc(swapped, 1)

            def pair_projections(j, u, r0, h0, first):
                if j in (1, 3, 8, 9):
                    act_e.wait_ge(unit_used, u + j + 1)
                if j == 1:
                    for c in range(2):
                        swap_halves(r0 + c, bank[c], TOK, 64)
                if j == 3:
                    for c in range(2):
                        swap_halves(r0 + 2 + c, bank[2 + c], REAL, 64)
                if j == 7:
                    for c in range(2):
                        act_e.wait_ge(rg_scaled, h0 + c + 1)
                        nc.scalar.activation(ret_gate[:, c, :], ret_gate[:, c, :], ACT.Silu).then_inc(gate_ready, 1)
                if j == 8:
                    swap_halves(r0 + 4, bank[2], REAL, 32)
                if j == 9:
                    for c in range(2):
                        copy(mla_k[:, c, :], bank[(3, 0)[c]][:, 0:TOK]).then_inc(mk_ready, 1)
                    for c in range(2):
                        act_e.wait_ge(v_tr, h0 + c + 1)
                        b = bank[(5, 7)[c]]
                        copy(ret_v[:, c, 0:REAL], b[:, 0:REAL])
                        copy(ret_v[0:META, c, REAL:], b[0:META, REAL:3 * P]).then_inc(v_ready, 1)

            def attention(j, h0, m0):
                if j == 1:
                    for c in range(2):
                        act_e.wait_ge(ret_out, h0 + c + 1)
                        copy(ret_o[:, c, :], bank[4 + 2 * c][:, 0:REAL])
                        nc.scalar.activation(ret_sq[:, c, :], bank[4 + 2 * c][:, 0:REAL], ACT.Square).then_inc(ret_sq_done, 1)
                if j == 2:
                    exps(h0)
                    ret_root(h0)
                if j == 4:
                    mix_hi_ret(h0, m0, 0)
                if j == 5:
                    exps(h0 + 1)
                if j == 6:
                    mix_hi_ret(h0, m0, 1)
                    mix_hi_mla(h0, 0)
                if j == 7:
                    probs_copy(h0 + 1)
                if j == 10:
                    mix_hi_mla(h0 + 1, 1)

            def ret_root(h0):
                for c in range(2):
                    act_e.wait_ge(ret_ms, h0 + c + 1)
                    nc.scalar.activation(ret_rs[:, c, :], bank[4 + 2 * c][:, 0:REAL], ACT.Sqrt, bias=eps, scale=1.0 / DH).then_inc(ret_std, 1)

            def exps(hd):
                for t in range(2):
                    act_e.wait_ge(neg_max, hd * 2 + (t + 1))
                    nc.scalar.activation(probs[:, t, :], probs[:, t, :], ACT.Exp, bias=small[:, 4 + t:5 + t],
                                         accum_out=small[:, 6 + t:7 + t]).then_inc(exp_done, 1)

            def probs_copy(hd):
                act_e.wait_ge(probs_tr, hd + 1)
                copy(sc[:, 0, 0:3 * P], bank[5][:, 0:3 * P])
                copy(sc[0:META, 0, 3 * P:640], bank[7][0:META, 0:REAL]).then_inc(probsT_ready, 1)

            def mix_hi_ret(h0, m0, c, dst=dn_hi):
                act_e.wait_ge(ret_f, h0 + c + 1)
                copy(dst[:, c, 0:REAL], ret_o[:, c, :]).then_inc(mix_hi_done, 1)

            def mix_hi_mla(hd, c, dst=dn_hi):
                act_e.wait_ge(mla_out, hd + 1)
                copy(dst[:, 2 + c, 0:REAL], bank[4 + 2 * c][:, 0:REAL]).then_inc(mix_hi_done, 1)

            act_e.dma_start(ident[:, :], a["ident"]).then_inc(consts_in, 16)
            def square_input(chunks):
                for c in chunks:
                    if c >= 4:
                        act_e.wait_ge(pool_step, max(c - 4, 1))
                    nc.scalar.activation(tmp[:, c % 4, :], h[:, c, :], ACT.Square).then_inc(squared, 1)

            def residual_in(c):
                act_e.wait_ge(x_tr, c + 1)
                copy(h[:, c, :], bank[4 + c % X_AHEAD][:, 0:TOK]).then_inc(h_ready, 1)

            act_e.dma_start(gain_rows[0:KC, :], a["ffn1_pre_norm"].rearrange("o (c p) -> (o c) p", p=P)).then_inc(consts_in, 16)
            for c in range(KC):
                if c in UNIT_AT_CHUNK:
                    split(UNIT_AT_CHUNK.index(c), UNIT_AT_CHUNK.index(c))
                if c == UNIT_AT_CHUNK[3]:
                    square_input(range(8))
                if c == 0:
                    act_e.wait_ge(gains_ready, 1)
                    residual_in(0)
                if c + 1 < KC:
                    residual_in(c + 1)
                operand_hi(0, c, TOK)
            split(4, 4)
            square_input(range(8, KC))
            act_e.wait_ge(ones_set, 2)

            def tail1(u):
                split(u + 2, u + 2)

            ffn(0, TOK, tail1)
            residual_operand(1, TOK, lambda: split(U_PRE + 3, U_PRE + 3))

            def latent_square(before, tiles, n, f):
                for c in range(tiles):
                    act_e.wait_ge(lat_read, before + c + 1)
                    nc.scalar.activation(lat_sq[:, c, 0:n], f[:, c, 0:n], ACT.Square).then_inc(lat_sqd, 1)

            def latent_std(index, rank, n):
                act_e.wait_ge(lat_ms, index + 1)
                nc.scalar.activation(rstd[:, 0:n], bank[7][:, 0:n], ACT.Sqrt, bias=eps, scale=1.0 / rank).then_inc(lat_std, 1)

            def latent_hi(before, tiles, n, f, dst):
                for c in range(tiles):
                    act_e.wait_ge(lat_normed, before + c + 1)
                    copy(dst[:, c, 0:n], f[:, c, 0:n]).then_inc(lat_hi_done, 1)

            for j in range(2, PRE_UNITS):
                u = U_PRE + j
                if j == 5:
                    std(2, TOK)
                split(u + 2, u + 2, kind="kr" if u + 2 == U_KR else "full")
                if u == U_KR:
                    act_e.wait_ge(unit_used, u + 1)
                    swap_halves(0, bank[2], TOK, 32)
                if j == 5:
                    latent_square(0, CC, TOK, ckv_f)
            act_e.wait_ge(spilled, 16)
            for j in range(PAIR_UNITS):
                u = U_MIX + j
                split(u + 2, u + 2, kind=pair_kind(j + 2))
                if j == 1:
                    latent_std(0, KV_RANK, TOK)
                    latent_square(CC, QC, REAL, cq_f)
                    latent_hi(0, CC, TOK, ckv_f, ckv_hi)
                if j == 3:
                    latent_std(1, Q_RANK, REAL)
                    latent_hi(CC, QC, REAL, cq_f, cq_hi)
                pair_projections(j, U_MIX, 1, 0, True)
            def pair_projection_units(u, u0, h0, h1, r0, filled):
                for j in range(PAIR_UNITS):
                    if j == 4:
                        probs_copy(h0)
                    if j == 10:
                        attention(j, h0, 0)
                    split(u + (j + 2), u0 + j + 2, kind=pair_kind(j + 2), filled=filled)
                    if j != 10:
                        attention(j, h0, 0)
                    pair_projections(j, u, r0, h1, False)

            with act_e.Fori(0, PAIRS - 2) as i:
                u0 = U_MIX + PAIR_UNITS
                u = act_e.snap(i * 15 + u0)
                h0 = act_e.snap(i * 2)
                h1 = act_e.snap(i * 2 + 2)
                r0 = act_e.snap(i * 5 + 6)
                filled = act_e.snap(i * (15 // SLOTS * FILL))
                pair_projection_units(u, u0, h0, h1, r0, filled)
                for j in range(PAIR_UNITS, 15):
                    split(u + (j + 2), u0 + j + 2, kind=pair_kind(j + 2), filled=filled)
            v = U_FFN[1] - 8
            pair_projection_units(v - PAIR_UNITS, v - PAIR_UNITS, HEADS - 4, HEADS - 2, 6 + 5 * (PAIRS - 2), 0)
            h0 = HEADS - 2
            split(v + 2, v + 2)
            attention(1, h0, 0)
            split(v + 3, v + 3)
            exps(h0)
            split(v + 4, v + 4)
            ret_root(h0)
            probs_copy(h0)
            mix_hi_ret(h0, 0, 0, hn_hi)
            exps(h0 + 1)
            split(v + 5, v + 5)
            mix_hi_ret(h0, 0, 1, hn_hi)
            mix_hi_mla(h0, 0, hn_hi)
            probs_copy(h0 + 1)
            last_units(1, v + 4, lambda u: split(u + 2, u + 2), lambda: mix_hi_mla(h0 + 1, 1, hn_hi))
            residual_operand(2, REAL, lambda: split(U_FFN[1] + 3, U_FFN[1] + 3))
            last = U_ALL - 1

            def tail2(u):
                if u + 2 <= last:
                    split(u + 2, u + 2)

            ffn(1, REAL, tail2)
            for b in range(4):
                for t in range(2):
                    act_e.wait_ge(out_tr, 2 * b + t + 1)
                    copy(raw[:, t, b * 512:(b + 1) * 512], bank[4 * t + b][:, :]).then_inc(out_ready, 1)

        @block.tensor
        def _(pe):
            mm = nc.tensor.matmul

            def keep_warm(b, count):
                for _ in range(count):
                    mm(b[:, 0:P], ones[:, :], ones[:, :], start=True, stop=True)

            def mm3(o, w, wl, x, xl, first, last):
                mm(o, w, x, start=first, stop=False)
                mm(o, w, xl, start=False, stop=False)
                return mm(o, wl, x, start=False, stop=last)

            def first_unit(u, u0, kh, banks, n, fine, after=None):
                pe.wait_ge(lo_ready, u + 1)
                wh, wl = slot(w_hi, u0, k=8), slot(w_lo, u0, k=8)
                last = None
                for k in range(8):
                    kk = 8 * kh + k
                    pe.wait_ge(hn_ready, fine + kk + 1)
                    for c in range(2):
                        cs = slice(c * P, (c + 1) * P)
                        last = mm3(bank[banks[c]][:, 0:n], wh[:, k, cs], wl[:, k, cs],
                                   hn_hi[:, kk, 0:n], hn_lo[:, kk, 0:n], kk == 0, kk == KC - 1)
                    if k == 7:
                        last.then_inc(unit_used, 1)
                    if after is not None:
                        after(kk)

            def proj_unit(u, u0, kh, banks, n, between=None):
                pe.wait_ge(lo_ready, u + 1)
                wh, wl = slot(w_hi, u0, k=8), slot(w_lo, u0, k=8)
                last = None
                for c in range(2):
                    if c == 1 and between is not None:
                        between()
                    for k in range(8):
                        kk = 8 * kh + k
                        cs = slice(c * P, (c + 1) * P)
                        last = mm3(bank[banks[c]][:, 0:n], wh[:, k, cs], wl[:, k, cs],
                                   hn_hi[:, kk, 0:n], hn_lo[:, kk, 0:n], kk == 0, kk == KC - 1)
                last.then_inc(unit_used, 1)

            def down_unit(u, u0, first_bank, n, dn=(dn_hi, dn_lo), phases=(((0, 1, 2, 3), None),), tiles=False,
                          order=(0, 1, 2, 3)):
                pe.wait_ge(lo_ready, u + 1)
                wh, wl = slot(w_hi, u0, k=4), slot(w_lo, u0, k=4)
                last = None
                for ks, before in phases:
                    for i in order:
                        if before is not None:
                            before(i)
                        for k in ks:
                            cs = slice(i * P, (i + 1) * P)
                            last = mm3(bank[first_bank + i][:, 0:n], wh[:, k, cs], wl[:, k, cs], dn[0][:, k, 0:n], dn[1][:, k, 0:n],
                                       k == 0, k == 3)
                        if tiles and i < 3 and ks[-1] == 3:
                            last.then_inc(tile_done, 1)
                last.then_inc(unit_used, 1)

            WHOLE = (((0, 1, 2, 3), None),)

            def halves(second):
                return (((0, 1), None), ((2, 3), once(0, second)))

            def once(i0, *waits):
                def before(i):
                    if i == i0:
                        for w in waits:
                            pe.wait_ge(*w)
                return before

            def token_tiles(n):
                return [(0, P), (P, REAL), (REAL, TOK)][:3 if n == TOK else 2]

            def feature_sum(norm, n):
                if norm % 2 == 0:
                    pe.wait_ge(ssq_ready, norm + 1)
                    sum_term(norm, n, ssq, True, True).then_inc(ms_done, 1)
                    return
                for k in (1, 2):
                    pe.wait_ge(squared, KC * norm + 12 + k + 1)
                    sum_term(norm, n, tmp[:, k, :], False, False)
                pe.wait_ge(ssq_ready, norm + 1)
                sum_term(norm, n, ssq, False, False)
                pe.wait_ge(squared, KC * norm + KC)
                sum_term(norm, n, tmp[:, 3, :], False, True).then_inc(ms_done, 1)

            def sum_term(norm, n, src, start, stop):
                for t, (t0, t1) in enumerate(token_tiles(n)):
                    last = mm(sum_bank(norm)[0:t1 - t0, t:t + 1], src[:, t0:t1], ones[:, 0:1],
                              start=start and t == 0, stop=stop, skip_group_check=True)
                return last

            def first_square(norm, n):
                def before(i):
                    if i == 3:
                        pe.wait_ge(squared, KC * norm + 13)
                        sum_term(norm, n, tmp[:, 0, :], True, False)
                return before

            def spread_factor(norm, n):
                pe.wait_ge(diag_done, norm + 1)
                for t0, t1 in token_tiles(n):
                    last = mm(sum_bank(norm)[:, t0:t1], ones[0:t1 - t0, :], rstd[0:t1 - t0, t0:t1], start=t0 == 0,
                              stop=True, skip_group_check=True)
                last.then_inc(spread, 1)

            def ffn(f, n, after=None):
                U = U_FFN[f]
                ch = 44 * f
                A = A_FFN[f] + 4

                for j in range(8):
                    banks = ((0, 1), (2, 3), (0, 1), (2, 3), (4, 5), (4, 5), (6, 7), (6, 7))[j]
                    kh = (0, 0, 1, 1, 0, 1, 0, 1)[j]
                    if j in (0, 2):
                        first_unit(U + j, U + j, kh, banks, n, 2 * KC * f, after)
                        continue
                    if j == 3 and f == 0:
                        pe.wait_ge(gains_in, 16 * 8)
                        pe.wait_ge(h_ready, KC)
                        nc.tensor.transpose(bank[7][:, 0:GAINS], gain_rows, ident[0:GAINS, 0:GAINS]).then_inc(gains_tr, 1)
                    if j == 5:
                        if f == 0:
                            pe.wait_ge(gains_ready, 2)
                        feature_sum(4 * f, n)
                    if j == 6:
                        pe.wait_ge(r_kept, 2 * f + 1)
                    proj_unit(U + j, U + j, kh, banks, n,
                              between=(lambda: spread_factor(4 * f, n)) if j == 5 else None)
                with pe.Fori(0, SEGS - 1) as i:
                    u0 = U + 8
                    u = pe.snap(i * 12 + u0)
                    c0 = pe.snap(i * 4 + (ch + 4))
                    a0 = pe.snap(i * 4 + A)
                    for j in range(4):
                        if j == 0:
                            pe.wait_ge(gate_scaled, c0 - 2)
                            pe.wait_ge(acc_ready, a0)
                        if j == 2:
                            pe.wait_ge(act_done, c0 - 2)
                        proj_unit(u + j, u0 + j, j % 2, ((0, 1), (2, 3))[j // 2], n)
                    for q in range(4):
                        if q == 0:
                            pe.wait_ge(act_ready, c0 - 2)
                            pe.wait_ge(gate_scaled, c0)
                            pe.wait_ge(act_done, c0)
                        if q == 1:
                            pe.wait_ge(gate_scaled, c0 + 2)
                            pe.wait_ge(act_done, c0 + 2)
                        if q > 1:
                            pe.wait_ge(acc_ready, a0 + (q - 1))
                        down_unit(u + (4 + q), u0 + 4 + q, 4 * (1 - q % 2), n,
                                  phases=WHOLE if q else halves((act_ready, c0)))
                    for j in range(4):
                        if j == 0:
                            pe.wait_ge(acc_ready, a0 + 3)
                        proj_unit(u + (8 + j), u0 + 8 + j, j % 2, ((4, 5), (6, 7))[j // 2], n)
                a0 = A + 4 * (SEGS - 1)
                pe.wait_ge(act_ready, ch + 42)
                for q in range(4):
                    if q == 1:
                        pe.wait_ge(gate_scaled, ch + 44)
                        pe.wait_ge(act_done, ch + 44)
                    pe.wait_ge(acc_ready, a0 + max(q - 1, 0))
                    u = U + FFN_UNITS - 4 + q
                    down_unit(u, u, last_banks(2 * f, q), n, tiles=q == 3,
                              phases=halves((act_ready, ch + 44)) if q == 0 else WHOLE if q < 3 else
                              (((0, 1, 2, 3), first_square(4 * f + 1, n)),))

            def pair_projections(j, u, u0, r0, h0, p0):
                if j < 8:
                    b = ((0, 1), (2, 3))[(j // 2) % 2]
                    n = (TOK, REAL, TOK, REAL)[j // 2]
                    if j == 4:
                        pe.wait_ge(rotated, r0 + 2)
                    if j == 6:
                        pe.wait_ge(rotated, r0 + 4)
                    proj_unit(u + j, u0 + j, j % 2, b, n)
                if j == 8:
                    pe.wait_ge(lo_ready, u + 9)
                    pe.wait_ge(vT_ready, h0 + 2)
                    pe.wait_ge(lat_ready, CC + QC)
                    wh, wl = (slot(r, u0 + 8, k=QC, n=QC * 384) for r in (w_hi, w_lo))
                    last = None
                    for c in range(3):
                        if c == 2:
                            pe.wait_ge(rg_scaled, h0 + 2)
                        for k in range(QC):
                            cs = slice(c * P, (c + 1) * P)
                            last = mm3(bank[c][:, 0:REAL], wh[:, k, cs], wl[:, k, cs], cq_hi[:, k, :], cq_lo[:, k, :],
                                       k == 0, k == QC - 1)
                    last.then_inc(unit_used, 1)
                    if not (isinstance(h0, int) and h0 == 0):
                        pe.wait_ge(probsT_ready, h0)
                    for c in range(2):
                        b = bank[(5, 7)[c]]
                        for r in range(3):
                            m = META if r == 2 else P
                            last = nc.tensor.transpose(b[0:m, r * P:(r + 1) * P], ret_vT[:, c, r * P:r * P + m], ident[:, :])
                        last.then_inc(v_tr, 1)
                if j == 9:
                    pe.wait_ge(lo_ready, u + 10)
                    wh, wl = (slot(r, u0 + 9, k=CC, n=CC * 256) for r in (w_hi, w_lo))
                    last = None
                    for c in range(2):
                        if c == 1:
                            pe.wait_ge(mq_ready, h0 + 1)
                        for k in range(CC):
                            cs = slice(c * P, (c + 1) * P)
                            last = mm3(bank[(3, 0)[c]][:, 0:TOK], wh[:, k, cs], wl[:, k, cs],
                                       ckv_hi[:, k, 0:TOK], ckv_lo[:, k, 0:TOK], k == 0, k == CC - 1)
                    last.then_inc(unit_used, 1)
                if j == 10:
                    pe.wait_ge(lo_ready, u + 11)
                    wh, wl = (slot(r, u0 + 10, k=CC, n=CC * 256) for r in (w_hi, w_lo))
                    last = None
                    for r in range(3):
                        if r == 0:
                            pe.wait_ge(mq_ready, h0 + 2)
                        if r == 1:
                            pe.wait_ge(rotated, r0 + 5)
                        if r == 2:
                            pe.wait_ge(mk_ready, h0 + 1)
                        o = bank[1 + r][:, 0:REAL]
                        ts = slice(r * P, (r + 1) * P)
                        for k in range(CC):
                            last = mm3(o, ckv_hi[:, k, ts], ckv_lo[:, k, ts], wh[:, k, :], wl[:, k, :],
                                       k == 0, k == CC - 1)
                    last.then_inc(unit_used, 1)

            def values(o, v_real, v_meta, s):
                mm(o[:, 0:REAL], v_real[0], s[:, 0:REAL], start=True, stop=False)
                mm(o[:, P:REAL], v_real[1], s[:, REAL:3 * P], start=False, stop=False)
                return mm(o[:, 0:REAL], v_meta, s[0:META, 3 * P:640], start=False, stop=True)

            def attention(g, h0, r0, p1):
                if g == 0:
                    pe.wait_ge(rotated, r0 + 4)
                    pe.wait_ge(v_ready, h0 + 2)
                    for c in range(2):
                        s, m = bank[4 + 2 * c], bank[5 + 2 * c]
                        k, q = ret_k[:, c, :], ret_q[:, c, :]
                        mm(s[:, 0:REAL], k[:, 0:P], q, start=True, stop=True)
                        mm(s[:, REAL:3 * P], k[:, P:REAL], q[:, P:REAL], start=False, stop=True, skip_group_check=True)
                        mm(m[0:META, 0:REAL], k[:, REAL:TOK], q, start=True, stop=True).then_inc(ret_scores, 1)
                if g == 1:
                    for c in range(2):
                        pe.wait_ge(ret_masked, h0 + c + 1)
                        v = ret_v[:, c, :]
                        values(bank[4 + 2 * c], (v[:, 0:P], v[:, P:REAL]), v[0:META, REAL:3 * P],
                               sc[:, c, :]).then_inc(ret_out, 1)
                if g == 2:
                    ret_mean(h0)
                    mla_s(h0, 0, r0, p1)
                if g == 3:
                    mla_t(h0)
                if g == 4:
                    mla_o(h0, 0)
                    mla_s(h0, 1, r0, p1)
                if g == 5:
                    mla_t(h0 + 1)
                if g == 6:
                    mla_o(h0, 1)

            def ret_mean(h0):
                for c in range(2):
                    pe.wait_ge(ret_sq_done, h0 + c + 1)
                    mm(bank[4 + 2 * c][:, 0:REAL], ones[:, :], ret_sq[:, c, :], start=True, stop=True).then_inc(ret_ms, 1)

            def mla_s(h0, c, r0, p1):
                pe.wait_ge(mk_ready, h0 + 2)
                pe.wait_ge(rotated, r0 + 5)
                rows = slice(64 * c, 64 * c + 64)
                for t in range(2):
                    ts = slice(t * P, (t + 1) * P)
                    b = bank[(5, 7)[t]][:, 0:TOK]
                    mm(b, mla_q[:, c, ts], mla_k[:, c, :], start=True, stop=False)
                    mm(b, mla_qr[rows, ts], mla_kr[rows, :], start=False, stop=True).then_inc(mla_scores, 1)

            def mla_t(hd):
                pe.wait_ge(probs_ready, hd * 2 + 2)
                tr = nc.tensor.transpose
                tr(bank[5][:, 0:P], probs[:, 0, 0:P], ident[:, :])
                tr(bank[5][:, P:REAL], probs[:, 1, 0:P], ident[:, :])
                tr(bank[5][:, REAL:3 * P], probs[:, 1, P:REAL], ident[:, :])
                tr(bank[7][0:META, 0:P], probs[:, 0, REAL:TOK], ident[:, :])
                tr(bank[7][0:META, P:REAL], probs[:, 1, REAL:TOK], ident[:, :]).then_inc(probs_tr, 1)

            def mla_o(h0, c):
                pe.wait_ge(probsT_ready, h0 + c + 1)
                pe.wait_ge(ret_std, h0 + c + 1)
                cs = slice(c * P, (c + 1) * P)
                values(bank[4 + 2 * c], (mla_v[:, 0, cs], mla_v[:, 1, cs]), mla_v[0:META, 2, cs],
                       sc[:, 0, :]).then_inc(mla_out, 1)

            pe.wait_ge(ones_set, 2)
            keep_warm(bank[1], 9)
            pe.wait_ge(consts_in, 32)
            nc.tensor.transpose(bank[0][:, 0:KC], gain_rows[0:KC, :], ident[0:KC, 0:KC]).then_inc(gains_tr, 1)

            def transpose_x(c):
                b = bank[4 + c % X_AHEAD]
                if c % 4 == 0:
                    pe.wait_ge(x_in[c // 4], 32 if c == 0 else 16)
                if c >= X_AHEAD:
                    pe.wait_ge(h_ready, c - X_AHEAD + 1)
                cs = slice(c * P, (c + 1) * P)
                for t in range(2):
                    nc.tensor.transpose(b[:, t * P:(t + 1) * P], x_sb[:, t, cs], ident[:, :])
                nc.tensor.transpose(b[:, REAL:TOK], meta_sb[:, cs], ident[0:META, 0:META]).then_inc(x_tr, 1)

            for c in range(X_AHEAD):
                transpose_x(c)
            keep_warm(bank[1], 22)
            pe.wait_ge(gains_ready, 1)
            ffn(0, TOK, after=lambda kk: transpose_x(kk + X_AHEAD) if kk + X_AHEAD < KC else None)
            feature_sum(1, TOK)
            keep_warm(bank[2], 6)
            spread_factor(1, TOK)
            keep_warm(bank[2], 10)

            for kh in range(2):
                first_unit(U_PRE + 2 * kh, U_PRE + 2 * kh, kh, (0, 1), TOK, KC)
                proj_unit(U_PRE + 2 * kh + 1, U_PRE + 2 * kh + 1, kh, CQ_BANKS[0], REAL)
            u = U_KR
            pe.wait_ge(lo_ready, u + 1)
            wh, wl = slot(w_hi, u, k=KC), slot(w_lo, u, k=KC)
            for k in range(KC):
                last = mm3(bank[2][:, 0:TOK], wh[:, k, :], wl[:, k, :], hn_hi[:, k, :], hn_lo[:, k, :],
                           k == 0, k == KC - 1)
            last.then_inc(unit_used, 1)
            feature_sum(2, TOK)
            for kh in range(2):
                proj_unit(U_PRE + 5 + kh, U_PRE + 5 + kh, kh, CQ_BANKS[1], REAL,
                          between=(lambda: spread_factor(2, TOK)) if kh == 0 else None)

            def latent_sum(before, tiles, n):
                for c in range(tiles):
                    pe.wait_ge(lat_sqd, before + c + 1)
                    last = mm(bank[7][:, 0:n], ones[:, :], lat_sq[:, c, 0:n], start=(c == 0), stop=(c == tiles - 1))
                last.then_inc(lat_ms, 1)

            for j in range(PAIR_UNITS):
                if j == 0:
                    pe.wait_ge(lat_read, CC)
                if j == 1:
                    pe.wait_ge(r_kept, 2)
                    latent_sum(0, CC, TOK)
                if j == 2:
                    pe.wait_ge(rotated, 1)
                    pe.wait_ge(lat_read, CC + QC)
                if j == 3:
                    pe.wait_ge(lat_std, 1)
                    latent_sum(CC, QC, REAL)
                pair_projections(j, U_MIX, U_MIX, 1, 0, 0)
            STAGE = {0: 1, 1: 2, 3: 3, 4: 4, 6: 5, 9: 6}

            def pair_projection_units(u, u0, h0, h1, r0, r1, p1, a0):
                pe.wait_ge(acc_ready, a0 - 1)
                attention(0, h0, r0, p1)
                for j in range(PAIR_UNITS):
                    if j == 0:
                        pe.wait_ge(acc_ready, a0)
                        pe.wait_ge(mk_ready, h0 + 2)
                        pe.wait_ge(mv_ready, p1)
                    pair_projections(j, u, u0, r1, h1, p1)
                    if j in STAGE:
                        attention(STAGE[j], h0, r0, p1)

            with pe.Fori(0, PAIRS - 2) as i:
                u0 = U_MIX + PAIR_UNITS
                u = pe.snap(i * 15 + u0)
                h0 = pe.snap(i * 2)
                h1 = pe.snap(i * 2 + 2)
                r0 = pe.snap(i * 5 + 1)
                r1 = pe.snap(i * 5 + 6)
                p1 = pe.snap(i + 1)
                a0 = pe.snap(i * 4 + (A_MIX + 4))
                pair_projection_units(u, u0, h0, h1, r0, r1, p1, a0)
                for q in range(4):
                    if q == 0:
                        pe.wait_ge(mix_ready, h0 * 2 + 3)
                        pe.wait_ge(v_ready, h1 + 2)
                    if q == 1:
                        pe.wait_ge(mk_ready, h1 + 2)
                        pe.wait_ge(mv_ready, p1 + 1)
                    if q > 1:
                        pe.wait_ge(acc_ready, a0 + (q - 1))
                    out4 = (mix_ready, h0 * 2 + 4)
                    down_unit(u + (11 + q), u0 + 11 + q, 4 * (1 - q % 2), REAL,
                              phases=WHOLE if q else (((0, 1), once(2, out4)), ((2, 3), once(0, out4))),
                              order=(0, 1, 2, 3) if q else (0, 1, 3, 2))

            v = U_FFN[1] - 8
            a0 = A_MIX + 4 + 4 * (PAIRS - 2)
            pair_projection_units(v - PAIR_UNITS, v - PAIR_UNITS, HEADS - 4, HEADS - 2, 1 + 5 * (PAIRS - 2),
                                  1 + 5 * (PAIRS - 1), PAIRS - 1, a0)
            h0, r0 = HEADS - 2, 1 + 5 * (PAIRS - 1)

            def bank_free(k, i):
                if k > 0:
                    if i < 3:
                        pe.wait_ge(tile_added, 3 + 3 * (k - 1) + i + 1)
                    else:
                        pe.wait_ge(acc_ready, a0 + k)

            pe.wait_ge(mix_ready, 4 * (PAIRS - 1))
            attention(0, h0, r0, PAIRS)
            pe.wait_ge(mk_ready, HEADS)
            pe.wait_ge(mv_ready, PAIRS)
            down_unit(v, v, 0, REAL, tiles=True)
            attention(1, h0, r0, PAIRS)
            mla_s(h0, 0, r0, PAIRS)
            down_unit(v + 1, v + 1, 0, REAL, tiles=True, phases=(((0, 1, 2, 3), lambda i: bank_free(1, i)),))
            ret_mean(h0)
            mla_t(h0)

            def beside_third(i):
                bank_free(2, i)
                if i == 2:
                    mla_o(h0, 0)
                    mla_s(h0, 1, r0, PAIRS)

            down_unit(v + 2, v + 2, 0, REAL, tiles=True, phases=(((0, 1, 2, 3), beside_third),))
            down_unit(v + 3, v + 3, 0, REAL, tiles=True, phases=(((0, 1, 2, 3), lambda i: bank_free(3, i)),))
            mla_t(h0 + 1)

            def last_head(i):
                if i == 0:
                    mla_o(h0, 1)
                    pe.wait_ge(mix_ready, 4 * PAIRS - 1)

            pe.wait_ge(mix_ready, 4 * PAIRS - 2)
            down_unit(v + 4, v + 4, 0, REAL, dn=(hn_hi, hn_lo), tiles=True,
                      phases=(((0, 1), lambda i: bank_free(4, i)), ((2,), last_head),
                              ((3,), once(0, (mix_ready, 4 * PAIRS)))))
            down_unit(v + 5, v + 5, 0, REAL, dn=(hn_hi, hn_lo), phases=(((0, 1, 2, 3), lambda i: bank_free(5, i)),))
            down_unit(v + 6, v + 6, 4, REAL, dn=(hn_hi, hn_lo))
            pe.wait_ge(acc_ready, a0 + 6)
            down_unit(v + 7, v + 7, 0, REAL, dn=(hn_hi, hn_lo), tiles=True,
                      phases=(((0, 1, 2, 3), first_square(3, REAL)),))
            feature_sum(3, REAL)
            keep_warm(bank[6], 5)
            spread_factor(3, REAL)
            keep_warm(bank[6], 10)
            ffn(1, REAL)
            feature_sum(5, REAL)
            keep_warm(bank[2], 5)
            spread_factor(5, REAL)
            for b in range(4):
                for i in range(4):
                    c = 4 * b + i
                    if by_dve(c):
                        pe.wait_ge(h_last, c // 3 + 1)
                    else:
                        pe.wait_ge(h_ready, 3 * KC + c + 1 - c // 3)
                    if c == KC - 4:
                        pe.wait_ge(post_scaled, 3 * KC)
                    for t in range(2):
                        tr = nc.tensor.transpose(bank[4 * t + b][:, i * P:(i + 1) * P], h[:, c, t * P:(t + 1) * P], ident[:, :])
                        if i == 3:
                            tr.then_inc(out_tr, 1)

        @block.vector
        def _(dve):
            tt, stt, ts = nc.vector.tensor_tensor, nc.vector.scalar_tensor_tensor, nc.vector.tensor_scalar

            class Own:
                n, turn, per = 0, None, 0

                def wait(self):
                    dve.wait_ge(dve_step, self.n if self.turn is None else self.turn * self.per + self.n)

                def step(self, ins):
                    ins.then_inc(dve_step, 1)
                    self.n += 1

            own = Own()

            def split(u, u0, kind="full"):
                dve.wait_ge(hi_ready, u + 1)
                for src, hi, lo in split_parts(u0, kind):
                    last = tt(lo, src, hi.bitcast(F32), ALU.subtract)
                last.then_inc(lo_ready, 1)

            def add_group(u, q, ready, n, first_bank=None):
                dve.wait_ge(unit_used, u + 1)
                dve.wait_ge(acc_ready, ready)
                last = None
                for i in range(4):
                    c = 4 * q + i
                    b = bank[(4 * (1 - q % 2) if first_bank is None else first_bank) + i][:, 0:n]
                    last = tt(acc_t[:, c, 0:n], acc_t[:, c, 0:n], b, ALU.add)
                last.then_inc(acc_ready, 1)

            def last_units(stage, u, tail):
                n = (TOK, REAL, REAL)[stage]
                for q in range(3):
                    if stage == 1 and q == 0:
                        continue
                    tail(u + q)
                    add_group(u + q, q, A_DONE[stage] + q - 3, n, last_banks(stage, q))
                dve.wait_ge(acc_ready, A_DONE[stage])
                for i in range(4):
                    if i == 1:
                        tail(u + 3)
                    if i < 3:
                        dve.wait_ge(tile_done, TILES[stage] + i + 1)
                    else:
                        dve.wait_ge(unit_used, u + 4)
                    t = acc_t[:, 12 + i, 0:n]
                    tt(t, t, bank[last_banks(stage, 3) + i][:, 0:n], ALU.add).then_inc(tile_added if i < 3 else acc_ready, 1)
                token_factor(2 * stage + 1, n)

            def token_factor(norm, n):
                dve.wait_ge(std_done, norm + 1)
                own.step(nc.vector.reciprocal(root[:, 0:2], root[:, 0:2]))
                if n == TOK:
                    own.step(nc.vector.reciprocal(root[0:META, 2:3], root[0:META, 2:3]))
                own.wait()
                for t in range(2):
                    last = ts(rstd[:, t * P:(t + 1) * P], ident[:, :], root[:, t:t + 1], None, ALU.mult)
                if n == TOK:
                    last = ts(rstd[0:META, REAL:TOK], ident[0:META, 0:META], root[0:META, 2:3], None, ALU.mult)
                last.then_inc(diag_done, 1)

            def operand_lo(stage, c, n):
                dve.wait_ge(hn_hi_done, stage * KC + c + 1)
                g = G_PRE[stage] + c
                stt(out=hn_lo[:, c, 0:n], in0=h[:, c, 0:n], scalar=gains[:, g:g + 1], in1=hn_hi[:, c, 0:n].bitcast(F32),
                    op0=ALU.mult, op1=ALU.subtract).then_inc(hn_ready, 1)

            def post_norm(stage, n, split_unit=None):
                dve.wait_ge(spread, 2 * stage + 2)
                LAG = 2
                for c in range(KC + LAG):
                    if c < KC:
                        g = G_POST[stage] + c
                        stt(out=acc_t[:, c, 0:n], in0=acc_t[:, c, 0:n], scalar=gains[:, g:g + 1],
                            in1=sum_bank(2 * stage + 1)[:, 0:n], op0=ALU.mult, op1=ALU.mult).then_inc(post_scaled, 1)
                    if stage == 2 and 0 < c < KC and by_dve(c - 1):
                        dve.wait_ge(post_scaled, 2 * KC + c)
                        tt(h[:, c - 1, 0:n], h[:, c - 1, 0:n], acc_t[:, c - 1, 0:n], ALU.add).then_inc(h_last, 1)
                    if c >= LAG and stage < 2:
                        operand_lo(stage + 1, c - LAG, n)
                    if c == 7 + LAG and split_unit is not None:
                        split_unit(2)
                if split_unit is not None:
                    split_unit(3)

            def pre_norm(norm, n):
                dve.wait_ge(spread, norm + 1)
                nc.vector.tensor_copy(r_pre[:, 0:n], bank[7][:, 0:n]).then_inc(r_kept, 1)
                dve.wait_ge(r_kept, norm // 2 + 1)

            def clear_acc(q):
                nc.vector.memset(acc_t[:, 4 * q:4 * q + 4, :], 0.0).then_inc(acc_ready, 1)

            def ffn(f, n, tail):
                U = U_FFN[f]
                ch = 44 * f
                A = A_FFN[f] + 4

                def gate_scale(u, c0, first_bank):
                    dve.wait_ge(unit_used, u + 1)
                    for c in range(2):
                        if not (isinstance(c0, int) and c0 + c < 2):
                            dve.wait_ge(act_done, c0 + c - 1)
                        tt(sil[:, c, 0:n], bank[first_bank + c][:, 0:n], r_pre[:, 0:n], ALU.mult).then_inc(gate_scaled, 1)

                def up_times(u, c0, first_bank):
                    dve.wait_ge(unit_used, u + 1)
                    for c in range(2):
                        if not (isinstance(c0, int) and c0 + c < 2):
                            dve.wait_ge(act_ready, c0 + c - 1)
                        tt(act[:, c, 0:n], bank[first_bank + c][:, 0:n], r_pre[:, 0:n], ALU.mult).then_inc(up_scaled, 1)
                    for c in range(2):
                        dve.wait_ge(silu_done, c0 + c + 1)
                        dve.wait_ge(up_scaled, c0 + c + 1)
                        tt(act[:, c, 0:n], sil[:, c, 0:n], act[:, c, 0:n], ALU.mult).then_inc(act_done, 1)

                def act_lo(c0, half):
                    for c in range(2):
                        dve.wait_ge(act_hi_done, c0 + c + 1)
                        k = 2 * half + c
                        tt(dn_lo[:, k, 0:n], act[:, c, 0:n], dn_hi[:, k, 0:n].bitcast(F32), ALU.subtract).then_inc(act_ready, 1)

                for j in range(3 - f, 8):
                    if j == 5:
                        token_factor(4 * f, n)
                    split(U + j + 2, U + j + 2)
                    if j == 5:
                        pre_norm(4 * f, n)
                        gate_scale(U + 2, ch, 0)
                        up_times(U + 3, ch, 2)
                        for q in range(4):
                            clear_acc(q)
                    if j == 6:
                        act_lo(ch, 0)
                        gate_scale(U + 5, ch + 2, 4)
                    if j == 7:
                        up_times(U + 7, ch + 2, 6)
                        act_lo(ch + 2, 1)
                with dve.Fori(0, SEGS - 1) as i:
                    u0 = U + 8
                    u = dve.snap(i * 12 + u0)
                    c0 = dve.snap(i * 4 + (ch + 4))
                    a0 = dve.snap(i * 4 + A)
                    for j in range(12):
                        split(u + (j + 2), u0 + j + 2)
                        if j == 1:
                            gate_scale(u + 1, c0, 0)
                        if j == 3:
                            up_times(u + 3, c0, 2)
                        if 4 <= j < 8:
                            add_group(u + j, j - 4, a0 + (j - 4 - 3), n)
                        if j == 7:
                            act_lo(c0, 0)
                        if j == 9:
                            gate_scale(u + 9, c0 + 2, 4)
                        if j == 11:
                            up_times(u + 11, c0 + 2, 6)
                            act_lo(c0 + 2, 1)
                last_units(2 * f, U + FFN_UNITS - 4, tail)

            def rotate(index, src, n, table, dst, factor=None):
                dve.wait_ge(swapped, index + 1)
                own.step(tt(prod[:, 0:n], src[:, 0:n], table[:, 0, 0:n], ALU.mult))
                own.step(tt(swap[:, 0:n], swap[:, 0:n], table[:, 1, 0:n], ALU.mult))
                own.wait()
                last = tt(dst, prod[:, 0:n], swap[:, 0:n], ALU.add)
                if factor is not None:
                    own.step(last)
                    own.wait()
                    last = tt(dst, dst, factor[:, 0:n], ALU.mult)
                last.then_inc(rotated, 1)
                dve.wait_ge(rotated, index + 1)

            def pair_projections(j, u, r0, h0, p0):
                if j == 1:
                    for c in range(2):
                        rotate(r0 + c, bank[c], TOK, rope_ret, ret_k[:, c, :])
                if j == 3:
                    for c in range(2):
                        rotate(r0 + 2 + c, bank[2 + c], REAL, rope_ret, ret_q[:, c, :])
                if j == 5:
                    dve.wait_ge(unit_used, u + 6)
                    for c in range(2):
                        tt(ret_vT[:, c, :], bank[c][:, 0:TOK], r_pre[:, :], ALU.mult).then_inc(vT_ready, 1)
                if j == 7:
                    dve.wait_ge(unit_used, u + 8)
                    for c in range(2):
                        tt(ret_gate[:, c, :], bank[2 + c][:, 0:REAL], r_pre[:, 0:REAL], ALU.mult).then_inc(rg_scaled, 1)
                if j == 8:
                    dve.wait_ge(unit_used, u + 9)
                    for c in range(2):
                        nc.vector.tensor_copy(mla_q[:, c, :], bank[c][:, 0:REAL]).then_inc(mq_ready, 1)
                    rotate(r0 + 4, bank[2], REAL, rope_mla, mla_qr)

            def values_out(u):
                dve.wait_ge(unit_used, u + PAIR_UNITS)
                nc.vector.tensor_copy(mla_v[:, 0, :], bank[1][:, 0:REAL])
                nc.vector.tensor_copy(mla_v[:, 1, :], bank[2][:, 0:REAL])
                nc.vector.tensor_copy(mla_v[0:META, 2, :], bank[3][0:META, 0:REAL]).then_inc(mv_ready, 1)

            def attention(j, h0, p0):
                if j == 0:
                    dve.wait_ge(decay_in, p0 * 32 + 32)
                    for c in range(2):
                        dve.wait_ge(ret_scores, h0 + c + 1)
                        tt(sc[:, c, 0:3 * P], bank[4 + 2 * c][:, 0:3 * P], decay[:, c, :], ALU.mult)
                        tt(sc[0:META, c, 3 * P:640], bank[5 + 2 * c][0:META, 0:REAL], decay_meta[0:META, c, :], ALU.mult).then_inc(ret_masked, 1)
                    own.step(nc.vector.tensor_copy(small[:, 8:10], gains[:, bass.ds(h0 + G_RET, 2)]))
                if j == 2:
                    softmax(h0)
                if j == 4:
                    group_norm(h0, p0, 0)
                if j == 5:
                    softmax(h0 + 1)
                if j == 6:
                    group_norm(h0, p0, 1)
                    mla_lo(h0, p0, 0)
                if j == 10:
                    mla_lo(h0, p0, 1)

            def softmax(hd):
                softmax_max(hd)
                softmax_scale(hd)

            def softmax_max(hd):
                for t in range(2):
                    b = bank[(5, 7)[t]][:, 0:TOK]
                    dve.wait_ge(mla_scores, hd * 2 + (t + 1))
                    own.step(stt(out=probs[:, t, :], in0=b, scalar=MLA_SCALE, in1=mask[:, t, :], op0=ALU.mult, op1=ALU.add))
                    own.wait()
                    own.step(nc.vector.reduce_max(small[:, 2 + t:3 + t], probs[:, t, :], AX.X))
                    own.wait()
                    ts(small[:, 4 + t:5 + t], small[:, 2 + t:3 + t], -1.0, None, ALU.mult).then_inc(neg_max, 1)

            def softmax_scale(hd):
                for t in range(2):
                    dve.wait_ge(exp_done, hd * 2 + (t + 1))
                    own.step(nc.vector.reciprocal(small[:, 10 + t:11 + t], small[:, 6 + t:7 + t]))
                    own.wait()
                    ts(probs[:, t, :], probs[:, t, :], small[:, 10 + t:11 + t], None, ALU.mult).then_inc(probs_ready, 1)

            def group_norm(h0, p0, c, hi=dn_hi, lo=dn_lo):
                dve.wait_ge(ret_std, h0 + c + 1)
                dve.wait_ge(gate_ready, h0 + c + 1)
                own.step(nc.vector.reciprocal(ret_rs[:, c, :], ret_rs[:, c, :]))
                own.wait()
                own.step(tt(ret_o[:, c, :], ret_o[:, c, :], ret_rs[:, c, :], ALU.mult))
                own.wait()
                stt(out=ret_o[:, c, :], in0=ret_o[:, c, :], scalar=small[:, 8 + c:9 + c], in1=ret_gate[:, c, :],
                    op0=ALU.mult, op1=ALU.mult).then_inc(ret_f, 1)
                dve.wait_ge(mix_hi_done, p0 * 4 + (c + 1))
                tt(lo[:, c, 0:REAL], ret_o[:, c, :], hi[:, c, 0:REAL].bitcast(F32), ALU.subtract).then_inc(mix_ready, 1)

            def mla_lo(h0, p0, c, hi=dn_hi, lo=dn_lo):
                dve.wait_ge(mix_hi_done, p0 * 4 + (c + 3))
                tt(lo[:, 2 + c, 0:REAL], bank[4 + 2 * c][:, 0:REAL], hi[:, 2 + c, 0:REAL].bitcast(F32), ALU.subtract).then_inc(mix_ready, 1)

            dve.wait_ge(gains_tr, 1)
            nc.vector.tensor_copy(gains[:, 0:KC], bank[0][:, 0:KC]).then_inc(gains_ready, 1)
            dve.wait_ge(gains_ready, 1)
            for c in range(KC):
                if c in UNIT_AT_CHUNK:
                    split(UNIT_AT_CHUNK.index(c), UNIT_AT_CHUNK.index(c))
                operand_lo(0, c, TOK)
            split(4, 4)
            dve.wait_ge(gains_tr, 2)
            ts(gains[:, G_POST[0]:G_POST[0] + KC], bank[7][:, G_POST[0]:G_POST[0] + KC], 0.5, None, ALU.mult)
            ts(gains[:, G_POST[2]:G_POST[2] + KC], bank[7][:, G_POST[2]:G_POST[2] + KC], 0.5, None, ALU.mult)
            nc.vector.tensor_copy(gains[:, G_PRE[1]:G_POST[2]], bank[7][:, G_PRE[1]:G_POST[2]])
            nc.vector.tensor_copy(gains[:, G_RET:GAINS], bank[7][:, G_RET:GAINS]).then_inc(gains_ready, 1)

            def tail1(u):
                split(u + 2, u + 2)

            ffn(0, TOK, tail1)
            post_norm(0, TOK, lambda k: split(U_PRE + k, U_PRE + k))

            dve.wait_ge(pad_zero, 2)
            dve.wait_ge(tables_in, 48)

            def latent_read(u, before, tiles, n, banks, f):
                dve.wait_ge(unit_used, u + 1)
                for c in range(tiles):
                    tt(f[:, before + c, 0:n], bank[banks[c]][:, 0:n], r_pre[:, 0:n], ALU.mult).then_inc(lat_read, 1)

            def latent_norm(index, before, tiles, n, f, gain, hi, lo):
                dve.wait_ge(lat_std, index + 1)
                own.step(nc.vector.reciprocal(rstd[:, 0:n], rstd[:, 0:n]))
                own.wait()
                for c in range(tiles):
                    stt(out=f[:, c, 0:n], in0=f[:, c, 0:n], scalar=gains[:, gain + c:gain + c + 1],
                        in1=rstd[:, 0:n], op0=ALU.mult, op1=ALU.mult).then_inc(lat_normed, 1)
                for c in range(tiles):
                    dve.wait_ge(lat_hi_done, before + c + 1)
                    tt(lo[:, c, 0:n], f[:, c, 0:n], hi[:, c, 0:n].bitcast(F32), ALU.subtract).then_inc(lat_ready, 1)

            for j in range(2, PRE_UNITS):
                u = U_PRE + j
                if j == 5:
                    token_factor(2, TOK)
                split(u + 2, u + 2, kind="kr" if u + 2 == U_KR else "full")
                if j == 5:
                    pre_norm(2, TOK)
                    latent_read(U_PRE + 2, 0, CC, TOK, (0, 1), ckv_f)
                    rotate(0, bank[2], TOK, rope_mla, mla_kr, r_pre)
                    latent_read(U_PRE + 3, 0, 2, REAL, CQ_BANKS[0], cq_f)
                    for t in range(2):
                        own.step(tt(rope_ret[:, t, :], rope_ret[:, t, :], r_pre[:, :], ALU.mult))
                if j == 6:
                    latent_read(U_PRE + 6, 2, 2, REAL, CQ_BANKS[1], cq_f)
            own.wait()
            dve.wait_ge(spilled, 16)
            for j in range(PAIR_UNITS):
                u = U_MIX + j
                if 4 <= j < 8:
                    clear_acc(j - 4)
                if j == 10:
                    values_out(U_MIX)
                split(u + 2, u + 2, kind=pair_kind(j + 2))
                if j == 1:
                    latent_norm(0, 0, CC, TOK, ckv_f, G_KV, ckv_hi, ckv_lo)
                if j == 3:
                    latent_norm(1, CC, QC, REAL, cq_f, G_Q, cq_hi, cq_lo)
                pair_projections(j, U_MIX, 1, 0, 0)
            def pair_projection_units(u, u0, h0, h1, r0, p0):
                for j in range(PAIR_UNITS):
                    if j == 10:
                        attention(j, h0, p0)
                        values_out(u)
                    split(u + (j + 2), u0 + j + 2, kind=pair_kind(j + 2))
                    if j != 10:
                        attention(j, h0, p0)
                    pair_projections(j, u, r0, h1, p0 + 1)

            with dve.Fori(0, PAIRS - 2) as i:
                u0 = U_MIX + PAIR_UNITS
                u = dve.snap(i * 15 + u0)
                h0 = dve.snap(i * 2)
                h1 = dve.snap(i * 2 + 2)
                r0 = dve.snap(i * 5 + 6)
                a0 = dve.snap(i * 4 + (A_MIX + 4))
                PER = 27
                own.turn, own.per, start = i, PER, own.n
                pair_projection_units(u, u0, h0, h1, r0, i)
                for q in range(4):
                    j = PAIR_UNITS + q
                    split(u + (j + 2), u0 + j + 2, kind=pair_kind(j + 2))
                    add_group(u + j, q, a0 + (q - 3), REAL)
                assert own.n - start == PER, own.n - start
                own.n, own.turn = start + PER * (PAIRS - 2), None
            v = U_FFN[1] - 8
            a0 = A_MIX + 4 + 4 * (PAIRS - 2)
            pair_projection_units(v - PAIR_UNITS, v - PAIR_UNITS, HEADS - 4, HEADS - 2, 6 + 5 * (PAIRS - 2), PAIRS - 2)
            h0, p0 = HEADS - 2, PAIRS - 1

            def add_tile(k, i):
                if i < 3:
                    dve.wait_ge(tile_done, 3 + 3 * k + i + 1)
                else:
                    dve.wait_ge(unit_used, v + k + 1)
                if i == 0:
                    dve.wait_ge(acc_ready, a0 + k - 3)
                t = acc_t[:, 4 * (k % 4) + i, 0:REAL]
                tt(t, t, bank[i][:, 0:REAL], ALU.add).then_inc(tile_added if i < 3 else acc_ready, 1)

            attention(0, h0, p0)
            split(v + 2, v + 2)
            for i in range(4):
                add_tile(0, i)
            softmax_max(h0)
            split(v + 3, v + 3)
            softmax_scale(h0)
            for i in range(4):
                add_tile(1, i)
            split(v + 4, v + 4)
            group_norm(h0, p0, 0, hn_hi, hn_lo)
            add_tile(2, 0)
            add_tile(2, 1)
            softmax_max(h0 + 1)
            add_tile(2, 2)
            add_tile(2, 3)
            softmax_scale(h0 + 1)
            group_norm(h0, p0, 1, hn_hi, hn_lo)
            mla_lo(h0, p0, 0, hn_hi, hn_lo)
            for i in range(4):
                add_tile(3, i)
            split(v + 5, v + 5)
            split(v + 6, v + 6)
            mla_lo(h0, p0, 1, hn_hi, hn_lo)
            for i in range(4):
                add_tile(4, i)
            last_units(1, U_FFN[1] - 4, lambda u: split(u + 2, u + 2))
            post_norm(1, REAL, lambda k: split(U_FFN[1] + k, U_FFN[1] + k))

            def tail(u):
                if u + 2 < U_ALL:
                    split(u + 2, u + 2)

            ffn(1, REAL, tail)
            post_norm(2, REAL)


_INS = ["x", "meta_tokens", "ffn1_pre_norm", "ffn1_w_gate", "ffn1_w_up", "ffn1_w_down",
        "ffn1_post_norm", "mix_pre_norm", "w_in", "ret_group_norm", "mla_q_norm", "mla_w_uq",
        "mla_kv_norm", "mla_w_uk", "mla_w_uv", "w_out", "mix_post_norm", "ffn2_pre_norm",
        "ffn2_w_gate", "ffn2_w_up", "ffn2_w_down", "ffn2_post_norm"]


def kernel(**inputs):
    import concourse.bacc as bacc
    from concourse.bass_utils import run_bass_kernel_spmd

    nc = bacc.Bacc("TRN2", target_bir_lowering=False, num_devices=1)
    arrays, aps = {}, {}
    for name in _INS:
        x = np.ascontiguousarray(inputs[name])
        if x.ndim == 3:
            x = x.reshape(x.shape[1:])
        arrays[f"in_{name}"] = x
    for name, x in constants().items():
        arrays[f"in_{name}"] = x
    for name, x in arrays.items():
        aps[name[3:]] = nc.dram_tensor(name, x.shape, mybir.dt.from_np(x.dtype), kind="ExternalInput").ap()
    out = nc.dram_tensor("out_dram", (REAL, DM), F32, kind="ExternalOutput").ap()
    build(nc, aps, out)
    r = run_bass_kernel_spmd(nc, [arrays], core_ids=[0])
    return r.results[0]["out_dram"].reshape(1, REAL, DM)
```
